# Optimizing a Trainium2 kernel written in Bass

```python
import math
import jax
import jax.numpy as jnp
from jax import lax
import numpy as np

'''One inference step (one layer) of a hybrid decoder: parallel sliding-window GQA with
sinks (branch A), gated DeltaNet (branch B) and memory cross-attention (branch C) on a
single combined input projection, merged by per-channel sigmoid gates, one output
projection, sandwich RMSNorm, then a sandwich-normed SwiGLU FFN.

Inputs: x_prompt (BATCH, SEQ, D_MODEL), x_sample (DEC_BATCH, DEC_SEQ, D_MODEL),
mem_prompt (BATCH, N_MEM, D_MODEL), state_win_k / state_win_v (DEC_BATCH, WINDOW, A_KV, A_HD),
state_conv (DEC_BATCH, CONV_W-1, B_CONV_CH), state_rec (DEC_BATCH, B_HEADS, B_DK, B_DV),
cache_mem_k / cache_mem_v (DEC_BATCH, N_MEM, C_HEADS, C_HD), then weights.

Returns the tuple:
  y_prompt        (BATCH, SEQ, D_MODEL)
  y_sample        (DEC_BATCH, DEC_SEQ, D_MODEL)
  win_k_prompt    (BATCH, WINDOW, A_KV, A_HD)      rotated keys of the last WINDOW positions
  win_v_prompt    (BATCH, WINDOW, A_KV, A_HD)
  conv_prompt     (BATCH, CONV_W-1, B_CONV_CH)     last pre-conv q/k/v rows of the DeltaNet
  rec_prompt      (BATCH, B_HEADS, B_DK, B_DV)     DeltaNet matrix state after SEQ tokens
  mem_k_prompt    (BATCH, N_MEM, C_HEADS, C_HD)    memory keys
  mem_v_prompt    (BATCH, N_MEM, C_HEADS, C_HD)    memory values
  win_k_sample    (DEC_BATCH, WINDOW, A_KV, A_HD)  updated window buffer
  win_v_sample    (DEC_BATCH, WINDOW, A_KV, A_HD)
  conv_sample     (DEC_BATCH, CONV_W-1, B_CONV_CH)
  rec_sample      (DEC_BATCH, B_HEADS, B_DK, B_DV)
'''

D_MODEL = 1024
BATCH = 1
SEQ = 1024
DEPTH = 1
DEC_BATCH = 8
DEC_SEQ = 4
PAST_LEN = 2048
PAGE_SIZE = 128

EPS = 1e-6
ROPE_THETA = 10000.0
N_MEM = 256
WINDOW = 128
A_HD = 64
A_HEADS = D_MODEL // 128
A_KV = A_HEADS // 4
A_GROUP = A_HEADS // A_KV
A_SCALE = A_HD ** -0.5
B_HEADS = D_MODEL // 256
B_DK = 128
B_DV = 128
CONV_W = 4
GDN_CHUNK = 64
B_CONV_CH = B_HEADS * (2 * B_DK + B_DV)
C_HEADS = 4
C_HD = 128
N_BRANCH = 3
BRANCH_W = A_HEADS * A_HD
D_FF = ((8 * D_MODEL + 3 * 256 - 1) // (3 * 256)) * 256

kernel_name = 'hybrid_swa_sink_gdn_memxattn_step'

def _in_sizes():
    return [A_HEADS * A_HD, A_KV * A_HD, A_KV * A_HD,
            B_CONV_CH,
            B_HEADS, B_HEADS,
            B_HEADS * B_DV,
            C_HEADS * C_HD,
            N_BRANCH * D_MODEL]

def _split_points():
    return np.cumsum(_in_sizes())[:-1].tolist()

def _rms_norm(x, gain):
    xf = x.astype(jnp.float32)
    y = xf * lax.rsqrt(jnp.mean(xf * xf, axis=-1, keepdims=True) + EPS)
    return (y * gain.astype(jnp.float32)).astype(x.dtype)

def _l2norm(x):
    return x * lax.rsqrt(jnp.sum(x * x, axis=-1, keepdims=True) + EPS)

def _rope(x, pos):
    half = x.shape[-1] // 2
    inv = ROPE_THETA ** (-jnp.arange(half, dtype=jnp.float32) / half)
    ang = pos.astype(jnp.float32)[:, None] * inv[None, :]
    cos = jnp.cos(ang)[:, None, :]
    sin = jnp.sin(ang)[:, None, :]
    xf = x.astype(jnp.float32)
    x1, x2 = xf[..., :half], xf[..., half:]
    return jnp.concatenate([x1 * cos - x2 * sin, x2 * cos + x1 * sin], axis=-1).astype(x.dtype)

def _window_mask(qpos, kpos):
    d = qpos - kpos
    return (d >= 0) & (d < WINDOW) & (kpos >= 0)

def _sink_softmax(logits, sink):
    s = jnp.broadcast_to(sink.astype(jnp.float32).reshape(A_KV, A_GROUP, 1, 1), logits.shape[:-1] + (1,))
    p = jax.nn.softmax(jnp.concatenate([logits, s], axis=-1), axis=-1)
    return p[..., :-1]

def _swa_prompt(q, k, v, sink):
    Bsz, L = q.shape[:2]
    nb = L // WINDOW
    qb = q.reshape(Bsz, nb, WINDOW, A_KV, A_GROUP, A_HD)
    kb = k.reshape(Bsz, nb, WINDOW, A_KV, A_HD)
    vb = v.reshape(Bsz, nb, WINDOW, A_KV, A_HD)

    def with_prev(t):
        prev = jnp.concatenate([jnp.zeros_like(t[:, :1]), t[:, :-1]], axis=1)
        return jnp.concatenate([prev, t], axis=2)

    kk, vv = with_prev(kb), with_prev(vb)
    logits = jnp.einsum('bnqkgd,bnskd->bnkgqs', qb, kk, preferred_element_type=jnp.float32) * A_SCALE
    blk = jnp.arange(nb, dtype=jnp.int32)[:, None] * WINDOW
    qpos = blk + jnp.arange(WINDOW, dtype=jnp.int32)[None, :]
    kpos = blk - WINDOW + jnp.arange(2 * WINDOW, dtype=jnp.int32)[None, :]
    mask = _window_mask(qpos[:, :, None], kpos[:, None, :])
    logits = jnp.where(mask[None, :, None, None], logits, -jnp.inf)
    p = _sink_softmax(logits, sink)
    o = jnp.einsum('bnkgqs,bnskd->bnqkgd', p.astype(vv.dtype), vv)
    return o.reshape(Bsz, L, A_HEADS * A_HD)

def _swa_decode(q, k, v, win_k, win_v, sink, pos):
    Bsz, L = q.shape[:2]
    kk = jnp.concatenate([win_k.astype(k.dtype), k], axis=1)
    vv = jnp.concatenate([win_v.astype(v.dtype), v], axis=1)
    qg = q.reshape(Bsz, L, A_KV, A_GROUP, A_HD)
    logits = jnp.einsum('bqkgd,bskd->bkgqs', qg, kk, preferred_element_type=jnp.float32) * A_SCALE
    kpos = jnp.concatenate([pos[0] - WINDOW + jnp.arange(WINDOW, dtype=jnp.int32), pos])
    mask = _window_mask(pos[:, None], kpos[None, :])
    logits = jnp.where(mask, logits, -jnp.inf)
    p = _sink_softmax(logits, sink)
    o = jnp.einsum('bkgqs,bskd->bqkgd', p.astype(vv.dtype), vv)
    return o.reshape(Bsz, L, A_HEADS * A_HD), kk[:, -WINDOW:], vv[:, -WINDOW:]

def _gated_delta_rule(q, k, v, g, beta, state):
    Bsz, L, H, DK = q.shape
    DV = v.shape[-1]
    C = min(GDN_CHUNK, L)
    pad = (-L) % C
    N = (L + pad) // C

    def chunks(t):
        t = jnp.pad(t, [(0, 0), (0, pad)] + [(0, 0)] * (t.ndim - 2))
        t = t.reshape((Bsz, N, C) + t.shape[2:])
        return jnp.moveaxis(jnp.moveaxis(t, 1, 0), 3, 2)

    qc, kc, vc, gc, bc = chunks(q), chunks(k), chunks(v), chunks(g), chunks(beta)
    gcum = jnp.cumsum(gc, axis=-1)
    tri = jnp.tril(jnp.ones((C, C), dtype=bool))
    strict = jnp.tril(jnp.ones((C, C), dtype=bool), -1)
    decay = jnp.exp(jnp.where(tri, gcum[..., :, None] - gcum[..., None, :], -jnp.inf))
    kb = kc * bc[..., None]
    a = jnp.where(strict, jnp.einsum('nbhid,nbhjd->nbhij', kb, kc) * decay, 0.0)
    eye = jnp.eye(C, dtype=jnp.float32)
    rhs = jnp.concatenate([vc * bc[..., None], kb * jnp.exp(gcum)[..., None]], axis=-1)
    sol = lax.linalg.triangular_solve(a + eye, rhs, left_side=True, lower=True, unit_diagonal=True)
    u, w = sol[..., :DV], sol[..., DV:]
    qk = jnp.einsum('nbhid,nbhjd->nbhij', qc, kc) * decay

    def step(S, inp):
        q_i, k_i, u_i, w_i, qk_i, g_i = inp
        v_new = u_i - jnp.einsum('bhck,bhkv->bhcv', w_i, S)
        o_i = (jnp.einsum('bhck,bhkv->bhcv', q_i * jnp.exp(g_i)[..., None], S)
               + jnp.einsum('bhij,bhjv->bhiv', qk_i, v_new))
        g_last = g_i[..., -1]
        S = (S * jnp.exp(g_last)[..., None, None]
             + jnp.einsum('bhck,bhcv->bhkv', k_i * jnp.exp(g_last[..., None] - g_i)[..., None], v_new))
        return S, o_i

    S, o = lax.scan(step, state, (qc, kc, u, w, qk, gcum))
    o = jnp.swapaxes(jnp.moveaxis(o, 0, 1), 2, 3).reshape(Bsz, N * C, H, DV)[:, :L]
    return o, S

def _gdn_branch(qkv_raw, b_raw, a_raw, z, conv_hist, rec_state, conv_w, a_log, dt_bias, norm_w):
    Bsz, L, _ = qkv_raw.shape
    xx = jnp.concatenate([conv_hist.astype(qkv_raw.dtype), qkv_raw], axis=1)
    conv = sum(xx[:, i:i + L] * conv_w[i].astype(qkv_raw.dtype) for i in range(CONV_W))
    qkv = jax.nn.silu(conv).astype(jnp.float32)
    q, k, v = jnp.split(qkv, [B_HEADS * B_DK, 2 * B_HEADS * B_DK], axis=-1)
    q = _l2norm(q.reshape(Bsz, L, B_HEADS, B_DK)) * (B_DK ** -0.5)
    k = _l2norm(k.reshape(Bsz, L, B_HEADS, B_DK))
    v = v.reshape(Bsz, L, B_HEADS, B_DV)
    beta = jax.nn.sigmoid(b_raw.astype(jnp.float32))
    g = -jnp.exp(a_log.astype(jnp.float32)) * jax.nn.softplus(a_raw.astype(jnp.float32) + dt_bias.astype(jnp.float32))
    o, S = _gated_delta_rule(q, k, v, g, beta, rec_state.astype(jnp.float32))
    o = _rms_norm(o, norm_w) * jax.nn.silu(z.astype(jnp.float32).reshape(Bsz, L, B_HEADS, B_DV))
    return o.reshape(Bsz, L, B_HEADS * B_DV).astype(qkv_raw.dtype), xx[:, -(CONV_W - 1):], S

def _mem_kv(mem, ln_mem, w_mem_kv):
    Bsz, M, _ = mem.shape
    k, v = jnp.split(_rms_norm(mem, ln_mem) @ w_mem_kv, 2, axis=-1)
    return k.reshape(Bsz, M, C_HEADS, C_HD), v.reshape(Bsz, M, C_HEADS, C_HD)

def _mem_attend(q, mk, mv):
    logits = jnp.einsum('bqhd,bshd->bhqs', q, mk.astype(q.dtype), preferred_element_type=jnp.float32) * (C_HD ** -0.5)
    p = jax.nn.softmax(logits, axis=-1)
    o = jnp.einsum('bhqs,bshd->bqhd', p.astype(q.dtype), mv.astype(q.dtype))
    return o.reshape(q.shape[0], q.shape[1], C_HEADS * C_HD)

def _layer(x, pos, swa_fn, conv_hist, rec_state, mem_k, mem_v, p):
    Bsz, L, _ = x.shape
    h = _rms_norm(x, p['ln_mix_pre'])
    qa, ka, va, qkvb, bb, ab, zb, qc, gates = jnp.split(h @ p['w_in'], _split_points(), axis=-1)
    qa = _rope(qa.reshape(Bsz, L, A_HEADS, A_HD), pos)
    ka = _rope(ka.reshape(Bsz, L, A_KV, A_HD), pos)
    va = va.reshape(Bsz, L, A_KV, A_HD)
    oa, new_wk, new_wv = swa_fn(qa, ka, va)
    ob, new_conv, new_rec = _gdn_branch(qkvb, bb, ab, zb, conv_hist, rec_state, p['gdn_conv_w'],
                                        p['gdn_a_log'], p['gdn_dt_bias'], p['gdn_norm_w'])
    oc = _mem_attend(qc.reshape(Bsz, L, C_HEADS, C_HD), mem_k, mem_v)
    branches = jnp.stack([oa.astype(x.dtype), ob.astype(x.dtype), oc.astype(x.dtype)], axis=2)
    up = jnp.einsum('blnc,ncd->blnd', branches, p['w_branch'])
    gate = jax.nn.sigmoid(gates.reshape(Bsz, L, N_BRANCH, D_MODEL))
    mix = jnp.sum(gate * up, axis=2) @ p['w_out']
    x = x + _rms_norm(mix, p['ln_mix_post'])
    h = _rms_norm(x, p['ln_ffn_pre'])
    gt, uf = jnp.split(h @ p['w_ffn_in'], 2, axis=-1)
    f = (jax.nn.silu(gt) * uf) @ p['w_ffn_out']
    x = x + _rms_norm(f, p['ln_ffn_post'])
    return x, new_wk, new_wv, new_conv, new_rec

def setup_inputs(seed: int = 0) -> dict:
    key = jax.random.key(seed)
    ks = jax.random.split(key, 26)
    f32 = jnp.float32

    def nrm(k, shape, scale):
        return jax.random.normal(k, shape, f32) * scale

    def gain(k, n):
        return 1.0 + 0.05 * jax.random.normal(k, (n,), f32)

    n_in = int(sum(_in_sizes()))
    dt = jnp.exp(jax.random.uniform(ks[13], (B_HEADS,), f32, math.log(1e-3), math.log(1e-1)))
    return {
        'x_prompt': nrm(ks[0], (BATCH, SEQ, D_MODEL), 1.0),
        'x_sample': nrm(ks[1], (DEC_BATCH, DEC_SEQ, D_MODEL), 1.0),
        'mem_prompt': nrm(ks[2], (BATCH, N_MEM, D_MODEL), 1.0),
        'state_win_k': nrm(ks[3], (DEC_BATCH, WINDOW, A_KV, A_HD), 1.0),
        'state_win_v': nrm(ks[4], (DEC_BATCH, WINDOW, A_KV, A_HD), 1.0),
        'state_conv': nrm(ks[5], (DEC_BATCH, CONV_W - 1, B_CONV_CH), 1.0),
        'state_rec': nrm(ks[6], (DEC_BATCH, B_HEADS, B_DK, B_DV), 0.5),
        'cache_mem_k': nrm(ks[7], (DEC_BATCH, N_MEM, C_HEADS, C_HD), 1.0),
        'cache_mem_v': nrm(ks[8], (DEC_BATCH, N_MEM, C_HEADS, C_HD), 1.0),
        'ln_mix_pre': gain(ks[9], D_MODEL),
        'w_in': nrm(ks[10], (D_MODEL, n_in), D_MODEL ** -0.5),
        'attn_sink': nrm(ks[11], (A_HEADS,), 0.5),
        'gdn_conv_w': nrm(ks[12], (CONV_W, B_CONV_CH), CONV_W ** -0.5),
        'gdn_a_log': jnp.log(jax.random.uniform(ks[14], (B_HEADS,), f32, 1.0, 16.0)),
        'gdn_dt_bias': dt + jnp.log(-jnp.expm1(-dt)),
        'gdn_norm_w': gain(ks[15], B_DV),
        'ln_mem': gain(ks[16], D_MODEL),
        'w_mem_kv': nrm(ks[17], (D_MODEL, 2 * C_HEADS * C_HD), D_MODEL ** -0.5),
        'w_branch': nrm(ks[18], (N_BRANCH, BRANCH_W, D_MODEL), BRANCH_W ** -0.5),
        'w_out': nrm(ks[19], (D_MODEL, D_MODEL), D_MODEL ** -0.5),
        'ln_mix_post': gain(ks[20], D_MODEL),
        'ln_ffn_pre': gain(ks[21], D_MODEL),
        'w_ffn_in': nrm(ks[22], (D_MODEL, 2 * D_FF), D_MODEL ** -0.5),
        'w_ffn_out': nrm(ks[23], (D_FF, D_MODEL), D_FF ** -0.5),
        'ln_ffn_post': gain(ks[24], D_MODEL),
    }

def reference(x_prompt, x_sample, mem_prompt, state_win_k, state_win_v, state_conv, state_rec,
              cache_mem_k, cache_mem_v, ln_mix_pre, w_in, attn_sink, gdn_conv_w, gdn_a_log,
              gdn_dt_bias, gdn_norm_w, ln_mem, w_mem_kv, w_branch, w_out, ln_mix_post,
              ln_ffn_pre, w_ffn_in, w_ffn_out, ln_ffn_post):
    p = {'ln_mix_pre': ln_mix_pre, 'w_in': w_in, 'gdn_conv_w': gdn_conv_w, 'gdn_a_log': gdn_a_log,
         'gdn_dt_bias': gdn_dt_bias, 'gdn_norm_w': gdn_norm_w, 'w_branch': w_branch, 'w_out': w_out,
         'ln_mix_post': ln_mix_post, 'ln_ffn_pre': ln_ffn_pre, 'w_ffn_in': w_ffn_in,
         'w_ffn_out': w_ffn_out, 'ln_ffn_post': ln_ffn_post}

    Bp, Lp, _ = x_prompt.shape
    pos_p = jnp.arange(Lp, dtype=jnp.int32)
    mem_k_p, mem_v_p = _mem_kv(mem_prompt, ln_mem, w_mem_kv)

    def swa_prompt_fn(q, k, v):
        return _swa_prompt(q, k, v, attn_sink), k[:, -WINDOW:], v[:, -WINDOW:]

    conv0 = jnp.zeros((Bp, CONV_W - 1, B_CONV_CH), x_prompt.dtype)
    rec0 = jnp.zeros((Bp, B_HEADS, B_DK, B_DV), jnp.float32)
    y_prompt, wk_p, wv_p, conv_p, rec_p = _layer(x_prompt, pos_p, swa_prompt_fn, conv0, rec0,
                                                 mem_k_p, mem_v_p, p)

    pos_s = PAST_LEN + jnp.arange(x_sample.shape[1], dtype=jnp.int32)

    def swa_sample_fn(q, k, v):
        return _swa_decode(q, k, v, state_win_k, state_win_v, attn_sink, pos_s)

    y_sample, wk_s, wv_s, conv_s, rec_s = _layer(x_sample, pos_s, swa_sample_fn, state_conv, state_rec,
                                                 cache_mem_k, cache_mem_v, p)

    return (y_prompt, y_sample, wk_p, wv_p, conv_p, rec_p, mem_k_p, mem_v_p, wk_s, wv_s, conv_s, rec_s)


_drawn_inputs = setup_inputs


def setup_inputs(seed=0):
    import zlib

    import numpy as np

    out = dict(_drawn_inputs(seed))
    spreads = {}
    factors = {'attn_sink': 7.238}
    for name, (base, spread) in spreads.items():
        noise = np.random.default_rng([zlib.crc32(name.encode()), seed]).standard_normal(out[name].shape)
        drawn = base * np.exp(spread * noise) if base else spread * noise
        out[name] = jnp.asarray(drawn.astype(out[name].dtype))
    for name, factor in factors.items():
        out[name] = (out[name] * factor).astype(out[name].dtype)
    return out
```

```python
from contextlib import ExitStack

import numpy as np
import concourse.bass as bass
from concourse import mybir

F32 = mybir.dt.float32
F32R = mybir.dt.float32r
BF16 = mybir.dt.bfloat16
ALU = mybir.AluOpType
ACT = mybir.ActivationFunctionType
AX = mybir.AxisListType

P = 128
D = 1024
KT = D // P
SEQ, DB, DS = 1024, 8, 4
NS = DB * DS
N = SEQ + NS
CH = N // 3
MEM = 256
WIN = 128
AH, AKV, AHD = 8, 2, 64
BH = 4
CW = 4
FF = 2816
EPS = 1e-6
NT = SEQ // P
C_QKVB, C_BA, C_Z, C_QC, C_GATE = 768, 2304, 2312, 2824, 3336

K_ID, K_ONE, K_GT, K_LE, K_LV = 0, 128, 256, 384, 512
NLV = 7
K_D_LE = K_LV + NLV * P
K_D_GT = K_D_LE + NS
K_D_BLK = K_D_GT + NS
K_COLS = K_D_BLK + NS


def constants():
    k = np.arange(P)[:, None]
    i = np.arange(P)[None, :]
    c = np.zeros((P, K_COLS), np.float32)
    c[:, K_ID:K_ID + P] = k == i
    c[:, K_ONE:K_ONE + P] = 1
    c[:, K_GT:K_GT + P] = k > i
    c[:, K_LE:K_LE + P] = k <= i
    for l in range(NLV):
        s = 2 ** l
        c[:, K_LV + l * P:K_LV + (l + 1) * P] = (k // (2 * s) == i // (2 * s)) & (k % (2 * s) < s) & (i % (2 * s) >= s)
    a, b = k[:NS], i[:, :NS]
    same = a // DS == b // DS
    c[:NS, K_D_LE:K_D_LE + NS] = same & (a <= b)
    c[:NS, K_D_GT:K_D_GT + NS] = same & (a > b)
    c[:NS, K_D_BLK:K_D_BLK + NS] = same
    half = AHD // 2
    inv = np.float32(10000.0) ** (-np.arange(half, dtype=np.float32) / np.float32(half))
    pos = np.concatenate([np.arange(SEQ), np.tile(2048 + np.arange(DS), DB)]).astype(np.float32)
    ang = (inv[:, None].astype(np.float32) * pos[None, :]).astype(np.float32)
    cos, sin = np.cos(ang).astype(np.float32), np.sin(ang).astype(np.float32)
    rope = np.stack([np.concatenate([cos, cos, cos, cos]), np.concatenate([-sin, sin, -sin, sin])])
    q, s = np.arange(WIN)[:, None], np.arange(2 * WIN)[None, :]
    d = q + WIN - s
    swa = np.where((d >= 0) & (d < WIN), 0.0, -1e30).astype(np.float32)
    first = np.where(s < WIN, np.float32(-1e30), swa)
    swa = np.concatenate([first[None], np.repeat(swa[None], NT - 1, 0)]).astype(np.float32)
    step = np.tile(np.arange(DS), 4 * DB)[:, None]
    batch = np.tile(np.repeat(np.arange(DB), DS), 4)[:, None]
    win = np.where(np.arange(WIN)[None, :] > step, 0.0, -1e30)
    new_b, new_s = np.repeat(np.arange(DB), DS)[None, :], np.tile(np.arange(DS), DB)[None, :]
    new = np.where((new_b == batch) & (new_s <= step), 0.0, -1e30)
    dmask = np.concatenate([win, new], 1).astype(np.float32)
    swa = (swa.view(np.uint32) >> 16).astype(np.uint16)
    return c, rope, swa, dmask


def build(nc, io):
    ctx = ExitStack()

    def sb(name, shape, dt=F32, on=None):
        return (on or ctx).enter_context(nc.sbuf_tensor(name, shape, dt))

    def sem(name):
        return ctx.enter_context(nc.semaphore(name))

    def dram(name, shape):
        return nc.dram_tensor(name, shape, F32).ap()

    s_qkv = dram("s_qkv", [12, P, N])
    s_z = dram("s_z", [4, P, N])
    s_qc = dram("s_qc", [4, P, N])
    s_qa = dram("s_qa", [4, P, N])
    s_kv = dram("s_kv", [2, P, WIN + N])
    s_gate = dram("s_gate", [24, P, N])
    s_br = dram("s_br", [12, P, N])

    psum = ctx.enter_context(nc.psum_tensor("psum", [P, 8, 512], F32))
    raw = sb("raw", [P, 2, KT, P])
    wsp = sb("wsp", [P, 2, 2, KT, P], F32R)
    kc = sb("kc", [P, K_COLS])
    ident, ones = kc[:, K_ID:K_ID + P], kc[:, K_ONE:K_ONE + P]
    k_gt, k_le = kc[:, K_GT:K_GT + P], kc[:, K_LE:K_LE + P]
    mkT = sb("mkT", [P, 4, MEM])
    mv = sb("mv", [P, 2, 4 * P])
    ba = sb("ba", [P, NT + 1, 8])
    ssq = sb("ssq", [P, 8, NT + 1])
    tail = sb("tail", [P, 12, 3 + NS])
    st = sb("st", [P, BH, P])
    snk = sb("snk", [P, 2, 8])
    idb = sb("idb", [P, P], BF16)
    hp = sb("hp", [P, 2, BH])
    par = sb("par", [P, 8, NT + 1, BH])
    egl = sb("egl", [P, NT + 1, BH])
    aS = ExitStack()
    actT = sb("actT", [P, 2, KT, N], F32R, on=aS)

    k_in = sem("k_in")
    x_in = [sem("x_in0"), sem("x_in1")]
    x_sq = sem("x_sq")
    x_rs = sem("x_rs")
    x_rt = sem("x_rt")
    x_nm = sem("x_nm")
    x_tr = sem("x_tr")
    x_hi = sem("x_hi")
    x_lo = sem("x_lo")
    w_in = [sem("w_in0"), sem("w_in1")]
    w_hi = sem("w_hi")
    w_lo = sem("w_lo")
    g_mm = sem("g_mm")
    g_ev = sem("g_ev")
    sc_t = sem("sc_t")
    sc_c = sem("sc_c")
    pad0 = sem("pad0")
    cv_in = sem("cv_in")
    cv_st = sem("cv_st")
    y_a = sem("y_a")
    y_d = sem("y_d")
    y_st = [sem("y_st0"), sem("y_st1")]
    sq_ok = sem("sq_ok")
    ss_mm = sem("ss_mm")
    ssq_ok = sem("ssq_ok")
    mt = sem("mt")
    mc = sem("mc")
    o_st = sem("o_st")

    NPB = 35
    B_Z, B_C, B_A, B_K, B_VA, B_BA, B_MEM = 12, 16, 20, 24, 25, 26, 27
    YD = lambda n: n - B_Z + 1 if n < B_C else 4 + 3 * (n - B_A + 1)

    def units(n):
        return 3 * n if not isinstance(n, int) or n <= B_MEM else 3 * B_MEM + n - B_MEM

    b0 = ExitStack()
    memT = sb("memT", [P, 2, KT, MEM], F32R, on=b0)
    scT = sb("scT", [P, 12, 28], on=b0)
    nw = sb("nw", [P, 1], on=b0)
    bA = ExitStack()
    xin = sb("xin", [P, 2, D], on=bA)
    xs = sb("xs", [P, 2, D], on=bA)
    gbc = sb("gbc", [P, 2, D], on=bA)
    rs = sb("rs", [P, 2, 4], on=bA)
    xjunk = sb("xjunk", [P, D], on=bA)
    sc_in = sb("sc_in", [28, 12 * P], on=bA)
    bA.close()
    bB = ExitStack()
    cv = sb("cv", [P, 2, 3 + SEQ + 7 * DB], on=bB)
    y = sb("y", [P, 2, N], on=bB)
    y2 = sb("y2", [P, 2, N], on=bB)
    sqb = sb("sqb", [P, N], on=bB)
    rope = sb("rope", [P, 2, N], on=bB)
    mout = sb("mout", [P, 2, 512], on=bB)
    bB.close()
    b0.close()

    wv = io["w_in"].rearrange("(k p) n -> p k n", p=P)
    wmv = io["w_mem_kv"].rearrange("(k p) n -> p k n", p=P)
    x_view = io["x_prompt"].rearrange("b (t p) d -> (b t) p d", p=P)
    xs_view = io["x_sample"].rearrange("b s d -> (b s) d")
    mem_view = io["mem_prompt"].rearrange("b (t p) d -> (b t) p d", p=P)

    rest_tiles = [(8, NS, xs_view, 0, actT, SEQ), (9, P, mem_view[0], 1, memT, 0), (10, P, mem_view[1], 1, memT, P)]

    def by_step(ap):
        return ap.rearrange("p (b s) -> p b s", b=DB)

    UC = units(NPB)
    cC = ExitStack()
    two = [P, 2]
    gin = sb("gin", [P, 2, 16, P], on=cC)
    ain = sb("ain", [P, 2, 8, P], on=cC)
    awin = sb("awin", [P, 2, 2, 2 * WIN], on=cC)
    mbf = sb("mbf", [P, 2, 2 * WIN], BF16, on=cC)
    Q_BETA, Q_G, Q_BK, Q_BKE, Q_KD, Q_EG, Q_RK, Q_RQ = range(8)
    tmp = sb("tmp", [P, 6, NT + 1, BH], on=cC)
    rr = sb("rr", [P, 2, 8, NT + 1], on=cC)
    vb, kbe, kd = (sb(n, [P, BH, P], on=cC) for n in ("vb", "kbe", "kd"))
    ug, bi, mrk = (sb(n, [P, BH, P], on=cC) for n in ("ug", "bi", "mrk"))
    dec, decm, kqd, at = (sb(n, [P, BH, P], on=cC) for n in ("dec", "decm", "kqd", "at"))
    atl = sb("atl", [P, NLV, BH, P], on=cC)
    xt, xx, yy = (sb(n, [P, BH, P], on=cC) for n in ("xt", "xx", "yy"))
    vn = sb("vn", [P, BH, P], on=cC)
    uu, wt = xx, yy
    o1s, oo = (sb(n, [P, BH, P], on=cC) for n in ("o1s", "oo"))
    obb = sb("obb", [P, BH, P], on=cC)
    osm = sb("osm", [P, 5, BH], on=cC)
    pr = sb("pr", [P, 2, 2 * WIN], on=cC)
    pt = sb("pt", [P, 4, P], on=cC)
    vtok = sb("vtok", [P, 2, P], on=cC)
    oat = sb("oat", [P, 2, 512], on=cC)
    oba = sb("oba", [P, 2, 4, P], on=cC)
    asm = sb("asm", [P, 7, 12], on=cC)
    S_MX, S_NM, S_SK, S_SM, S_ES, S_DEN, S_RD = range(7)
    gst = sb("gst", [P, 3, CH], on=cC)
    cC.close()

    p_in = sem("p_in")
    pp = sem("pp")
    pa = sem("pa")
    pg = sem("pg")
    st0 = sem("st0")
    l_in = {n: [sem(f"l_{n}0"), sem(f"l_{n}1")] for n in ("q", "kv", "z", "qa", "qc", "win")}
    c_sm = sem("c_sm")
    ug_ok, bi_ok, mrk_ok = sem("ug_ok"), sem("bi_ok"), sem("mrk_ok")
    e_tk, e_tv, e_gt, e_br, e_kk, e_kq, e_x0, e_y, e_xx, e_xt, e_u, e_w, e_p1, e_o1, e_sp, e_o2, e_ot = (
        sem("e_" + n) for n in "tk tv gt br kk kq x0 y xx xt u w p1 o1 sp o2 ot".split())
    kd_ok, vb_ok, dec_ok, dm_ok, kq_ok, at_st, al_ok = (sem(n) for n in "kd_ok vb_ok dec_ok dm_ok kq_ok at_st al_ok".split())
    c_x, c_xt, c_y, c_u, c_w, vn_ok, c_o1, c_o, c_s, c_ob = (
        sem(n) for n in "c_x c_xt c_y c_u c_w vn_ok c_o1 c_o c_s c_ob".split())
    o_st1, o_sq, o_rt, on_ok = sem("o_st1"), sem("o_sq"), sem("o_rt"), sem("on_ok")
    ob_st = sem("ob_st")
    a_vt, a_vc = sem("a_vt"), sem("a_vc")
    a_s, a_mx, a_nm, a_sk, a_e, a_t, a_pt, a_v, av_ok = (
        sem(n) for n in "a_s a_mx a_nm a_sk a_e a_t a_pt a_v av_ok".split())
    a_es, a_dn, a_on, a_st = sem("a_es"), sem("a_dn"), sem("a_on"), [sem("a_st0"), sem("a_st1")]
    gs_st = [sem(f"gs_st{c}") for c in range(3)]

    TILE = ("KV", "DEC", "KK", ("S", 0), ("G", 0), "INV", ("T", 0), ("Y", 1), ("G", 1), ("V", 0), ("X", 1),
            ("S", 1), ("Y", 2), ("G", 2), ("T", 1), ("X", 2), ("V", 1), ("Y", 3), ("G", 3), ("S", 2), ("X", 3),
            ("T", 2), ("Y", 4), ("G", 4), ("V", 2), ("X", 4), ("S", 3), ("Y", 5), ("G", 5), ("T", 3), ("X", 5),
            ("V", 3), ("Y", 6), ("G", 6), ("F", 0), ("X", 6), ("S", 4), "UW", ("G", 7), ("T", 4), "PO", ("V", 4),
            ("S", 5), "SO", ("G", 8), ("T", 5), "N1", ("V", 5), "N2", ("F", 1),
            "OT")
    QI = (0, 1, 2, 3, 5, 6)
    A_SC = [AHD ** -0.5] * 4 + [P ** -0.5] * 2

    def bc_h(ap):
        return ap.unsqueeze(1).to_broadcast([P, BH, P])

    def bc_c(ap):
        return ap.rearrange("p a h -> p (a h)").unsqueeze(2).to_broadcast([P, BH, P])

    def per(q, t):
        return par[:, q, bass.ds(t, 1), :]
    aS.close()
    cE = ExitStack()
    ext = sb("ext", [P, 6, NS], on=cE)
    dq = sb("dq", [P, 16, NS], on=cE)
    da = sb("da", [P, 8, NS], on=cE)
    lkv = sb("lkv", [P, 2, P], on=cE)
    wkv = sb("wkv", [P, 2, DB, P], on=cE)
    wkT = sb("wkT", [P, DB, P], on=cE)
    dmk = sb("dmk", [P, WIN + NS], on=cE)
    sd = sb("sd", [P, DB, BH, P], on=cE)
    ck = sb("ck", [P, 2, 2, 4 * P], on=cE)
    cvm = sb("cvm", [P, DB, 2, 4 * P], on=cE)
    ckT = sb("ckT", [P, 2, 4, MEM], on=cE)
    vnm = sb("vnm", [NS, 4, 4, P], on=cE)
    dia = sb("dia", [NS, 4, BH, NS], on=cE)
    dug, dmr, ddc, dat, dat1, dkq, dxt, dxx, dyy = (
        sb(n, [NS, BH, NS], on=cE) for n in "dug dmr ddc dat dat1 dkq dxt dxx dyy".split())
    dkb, dkd, dvb, dvn = (sb(n, [NS, BH, P], on=cE) for n in "dkb dkd dvb dvn".split())
    wq = sb("wq", [P, BH, DB, 2, DS], on=cE)
    duT, dvT, dqe, dsq, dnm = (sb(n, [P, BH, NS], on=cE) for n in "duT dvT dqe dsq dnm".split())
    deg = sb("deg", [P, BH, NS], on=cE)
    del_ = sb("del_", [P, BH, NS], on=cE)
    mS = sb("mS", [P, 2, P], on=cE)
    mR = sb("mR", [P, MEM], on=cE)
    sS = sb("sS", [P, 4, P], on=cE)
    sR = sb("sR", [P, 2, WIN + NS], on=cE)
    dsm = sb("dsm", [P, 20], on=cE)
    sks = sb("sks", [P, 2], on=cE)
    kvo = sb("kvo", [P, 2, 2, P], on=cE)
    tlo = sb("tlo", [3 + NS, 12 * P], on=cE)
    dob = sb("dob", [P, 3, 4, NS], on=cE)
    cE.close()

    F_IN = 16 * (9 + 8 + 2 * DB)
    f_in = sem("f_in")
    f_pe, f_ac, f_dv = sem("f_pe"), sem("f_ac"), sem("f_dv")
    m_in = [sem("m_in0"), sem("m_in1")]
    m_kt, m_ka, m_kd, m_sc = sem("m_kt"), sem("m_ka"), sem("m_kd"), sem("m_sc")
    g_up, g_ad = sem("g_up"), sem("g_ad")
    f_st = sem("f_st")

    PE_E = ("out", "bcast", "win_kt", "mem_rows", "x0", "new_sc", "y", "mem_pt", "xt", "win_rows", "u_w", "mem_o",
            "win_pt", "w_q_s", "win_o", "vn", "o", "sumsq")
    AC_E = ("kv_out", "new_out", "tail_out", "dec", "rq", "wkT", "mem_s", "mem_exp", "x0", "win_s", "y", "mem_p",
            "win_exp", "win_sk", "win_p", "vn", "sq", "root")
    DV_E = ("ug", "d0", "d1", "d2", "d3", "mr", "kb", "kd", "vb", "dcm", "at0", "at", "kq", "x_", "xt0", "at1", "eg",
            "el", "mem_mx", "mem_nm", "mem_rd", "mem_n", "xt", "win_m0", "win_m1", "win_mx", "win_nx", "win_nm",
            "win_sk", "uT", "wT", "mem_o", "win_dn", "win_rd", "win_n", "vT", "qe", "win_c0", "win_c1", "win_o0",
            "win_o1", "vm0", "o_", "s_e", "n0", "n1", "n2", "oq", "oz", "n3", "o_z", "vm1")
    PEn, ACn, DVn = (lambda s: PE_E.index(s) + 1), (lambda s: AC_E.index(s) + 1), (lambda s: DV_E.index(s) + 1)
    NPD = NPB + 24
    NPO = NPD + 12
    NPF = NPO + 8
    NF = FF // P
    UD = UC + 72
    UO = UD + 72
    UF = UO + 24
    ORDER = (2, 0, 1)
    cD = ExitStack()
    actD = sb("actD", [P, 2, KT, N], F32R, on=cD)
    accT = sb("accT", [P, KT, N], on=cD)
    cG = ExitStack()
    brw = sb("brw", [P, 4, N], on=cG)
    gat = sb("gat", [P, 2, 2, N], on=cG)
    prd = sb("prd", [P, 2, CH], on=cG)
    cG.close()
    gn = sb("gn", [P, 3, D], on=cD)
    xr = sb("xr", [P, 2, D], on=cD)
    yr = sb("yr", [P, 2, D], on=cD)
    jk = sb("jk", [P, 2, D], on=cD)
    ns = sb("ns", [P, 2, 2, 4], on=cD)
    fT = sb("fT", [P, 2, 2, N], F32R, on=cD)
    sg = sb("sg", [P, N], on=cD)
    fr = sb("fr", [P, N], on=cD)
    cD.close()
    s_x1 = dram("s_x1", [NT + 1, P, D])

    b_in = sem("b_in")
    b_hi, b_lo = sem("b_hi"), sem("b_lo")
    q_in = [sem("q_in0"), sem("q_in1")]
    q_sg = sem("q_sg")
    q_pr = sem("q_pr")
    q_mx = sem("q_mx")
    r_in = [sem("r_in0"), sem("r_in1")]
    t_tr, t_sq, t_ms, t_rt, t_rd, t_y, t_x1 = (sem("t_" + n) for n in "tr sq ms rt rd y x1".split())
    t_xst = [sem("t_xst0"), sem("t_xst1")]
    u_sq, u_ms, u_rt, u_rd, u_xs, u_tr, u_hi, u_lo = (sem("u_" + n) for n in "sq ms rt rd xs tr hi lo".split())
    f_sg, f_fr, f_hi, f_lo = sem("f_sg"), sem("f_fr"), sem("f_hi"), sem("f_lo")
    o_mm, o_ad = sem("o_mm"), sem("o_ad")
    wbv = io["w_branch"]
    wov = io["w_out"].rearrange("(k p) n -> p k n", p=P)
    wfv = io["w_ffn_in"].rearrange("(k p) n -> p k n", p=P)
    wgv = io["w_ffn_out"].rearrange("(f p) n -> f p n", p=P)
    y_view = io["y_prompt"].rearrange("b (t p) d -> (b t) p d", p=P)
    ys_view = io["y_sample"].rearrange("b s d -> (b s) d")

    def slab(t, slot):
        return t[:, slot].rearrange("p k n -> p (k n)").rearrange("p (k n) -> p k n", k=4)
    block = ctx.enter_context(nc.Block())

    @block.sync
    def _(sp):
        sp.sem_inc(x_nm, 2)
        sp.sem_inc(y_st[0], 16)
        sp.sem_inc(y_st[1], 16)
        sp.dma_start(kc[:], io["k_const"]).then_inc(k_in, 16)
        sp.dma_start(gbc[:, 0, :], io["ln_mix_pre"].partition_broadcast(P)).then_inc(k_in, 16)
        sp.dma_start(gbc[:, 1, :], io["ln_mem"].partition_broadcast(P)).then_inc(k_in, 16)
        sp.dma_start(hp[:, 0, :], io["gdn_a_log"].partition_broadcast(P)).then_inc(p_in, 16)
        sp.dma_start(hp[:, 1, :], io["gdn_dt_bias"].partition_broadcast(P)).then_inc(p_in, 16)
        sp.dma_start(snk[:, 0, :], io["attn_sink"].partition_broadcast(P)).then_inc(p_in, 16)
        sp.wait_ge(pad0, 3)
        sp.dma_start(s_kv.rearrange("a p n -> p a n")[:, :, 0:WIN], st[:, 0:2, :]).then_inc(p_in, 16)
        sp.dma_start(nw[:], io["gdn_norm_w"].rearrange("(p a) -> p a", a=1)).then_inc(k_in, 16)
        sp.dma_start(sc_in[0:24, :], io["state_conv"].rearrange("b c n -> (b c) n")).then_inc(k_in, 16)
        sp.dma_start(sc_in[24:28, :], io["gdn_conv_w"]).then_inc(k_in, 16)

        def load_x(n, slot, rows, src):
            sp.wait_ge(x_nm, n + 1)
            sp.dma_start(xin[0:rows, slot, :], src).then_inc(x_in[slot], 16)

        with sp.Fori(0, NT // 2) as i:
            for b in range(2):
                load_x(2 * i + b, b, P, x_view[bass.ds(2 * i + b, 1)].rearrange("a p d -> (a p) d"))
        for n, rows, src, *_ in rest_tiles:
            load_x(n, n % 2, rows, src)

        def load_w(n, halves):
            sp.wait_ge(w_lo, n + 1)
            for dst, src in halves:
                sp.dma_start(dst, src).then_inc(w_in[n % 2], 16)

        def k_halves(n, view, col, width=P):
            return [(raw[:, n % 2, 4 * h:4 * h + 4, 0:width], view[:, 4 * h:4 * h + 4, col:col + width])
                    for h in range(2)]

        def load_b(n):
            if n < B_Z:
                load_w(n, k_halves(n, wv, C_QKVB + P * n))
            elif n < B_C:
                load_w(n, k_halves(n, wv, C_Z + P * (n - B_Z)))
            elif n < B_A:
                load_w(n, k_halves(n, wv, C_QC + P * (n - B_C)))
            elif n < B_K:
                g = n - B_A
                load_w(n, [(raw[:, n % 2, :, 64 * h:64 * h + 64], wv[:, :, 256 * h + 64 * g:256 * h + 64 * g + 64])
                           for h in range(2)])
            elif n < B_MEM:
                load_w(n, k_halves(n, wv, {B_K: 512, B_VA: 640, B_BA: C_BA}[n], 8 if n == B_BA else P))
            else:
                load_w(n, k_halves(n, wmv, P * (n - B_MEM)))

        load_b(0)
        load_b(1)
        sp.wait_ge(x_lo, 2 + 11)
        sp.dma_start(rope[:], io["k_rope"].rearrange("a p n -> p a n")).then_inc(k_in, 16)
        rows = [s_qkv[n] for n in range(12)] + [s_z[n] for n in range(4)] + [s_qc[n] for n in range(4)]
        rows += [s_qa[n] for n in range(4)] + [s_kv[n][:, WIN:] for n in range(2)]
        for n in range(B_BA):
            load_b(n + 2)
            if n < B_Z:
                sp.wait_ge(y_a, 2 + n + 1)
            elif n < B_C or B_A <= n < B_VA:
                sp.wait_ge(y_d, YD(n))
            else:
                sp.wait_ge(g_ev, 3 + 3 * n + 3)
            sp.dma_start(rows[n], y2[:, n % 2, :]).then_inc(y_st[n % 2], 16)
        for n in range(B_BA + 2, NPB):
            load_b(n)
        for s in range(2):
            sp.wait_ge(mc, NT + 1 + 2 * s + 1)
            sp.dma_start(io["mem_k_prompt"][0, P * s:P * s + P].rearrange("t h d -> t (h d)"), mout[:, s, :]).then_inc(o_st, 16)
            sp.wait_ge(mc, NT + 1 + 2 * s + 2)
            sp.dma_start(io["mem_v_prompt"][0, P * s:P * s + P].rearrange("t h d -> t (h d)"), mv[:, s, :]).then_inc(o_st, 16)
        def load_tile(t, b):
            def cols(src, w=P):
                return src.rearrange("n p t -> p n t")[:, :, bass.ds(P * t, w)]

            if not isinstance(t, int):
                sp.wait_ge(c_ob, t)
            sp.dma_start(gin[:, b, 4:12, :], cols(s_qkv[4:12])).then_inc(l_in["kv"][b], 16)
            sp.dma_start(awin[:, b], cols(s_kv, 2 * WIN)).then_inc(l_in["win"][b], 16)
            sp.dma_start(mbf[:, b], io["k_swa"][bass.ds(t, 1)].rearrange("a q s -> (a q) s").bitcast(BF16)).then_inc(l_in["win"][b], 16)
            sp.dma_start(ain[:, b, 0:4, :], cols(s_qa)).then_inc(l_in["qa"][b], 16)
            sp.dma_start(gin[:, b, 0:4, :], cols(s_qkv[0:4])).then_inc(l_in["q"][b], 16)
            sp.dma_start(ain[:, b, 4:8, :], cols(s_qc)).then_inc(l_in["qc"][b], 16)
            sp.dma_start(gin[:, b, 12:16, :], cols(s_z)).then_inc(l_in["z"][b], 16)

        def load_gate(m, slot):
            sp.wait_ge(w_lo, NPB + m + 1)
            for h in range(2):
                sp.dma_start(raw[:, slot, 4 * h:4 * h + 4, :], wv[:, 4 * h:4 * h + 4, bass.ds(C_GATE + P * m, P)]).then_inc(w_in[slot], 16)

        def serve_tile(t, b, last=False):
            for j in range(3):
                if not (last and j > 0):
                    load_gate(3 * t + 2 + j, (NPB + 3 * b + 2 + j) % 2)
                for c in range(3):
                    sp.wait_ge(g_ev, 3 + UC + 9 * t + 3 * j + c + 1)
                    sp.dma_start(s_gate[bass.ds(3 * t + j, 1)].rearrange("a p n -> (a p) n")[:, CH * c:CH * c + CH],
                                 gst[:, c]).then_inc(gs_st[c], 16)
                if j == 1 and not last:
                    load_tile(t + 1, 1 - b)
            sp.wait_ge(c_ob, 2 + t)
            sp.dma_start(s_br[4:8].rearrange("n p t -> p n t")[:, :, bass.ds(P * t, P)], obb[:]).then_inc(ob_st, 16)

        sp.wait_ge(y_st[0], 16 + 16 * 13)
        sp.wait_ge(y_st[1], 16 + 16 * 13)
        sp.wait_ge(p_in, 64)
        sp.wait_ge(mc, NT + 1 + 4)
        sp.wait_ge(o_st, 64)
        sp.sem_inc(c_ob, 1)
        for s in range(2):
            load_gate(s, (NPB + s) % 2)
        load_tile(0, 0)
        with sp.Fori(0, 3) as i:
            for b in range(2):
                serve_tile(2 * i + b, b)
        serve_tile(6, 0)
        serve_tile(7, 1, last=True)
        sp.wait_ge(c_ob, 2 + NT - 1)
        sp.wait_ge(ob_st, 16 + 16 * NT)
        for s in range(2):
            sp.wait_ge(a_st[s], 16 + 16 * NT)
        for c in range(3):
            sp.wait_ge(gs_st[c], 16 + 16 * 24)
        sp.wait_ge(c_s, 1 + NT)
        sp.dma_start(io["rec_prompt"][0].rearrange("h k v -> k h v"), st[:]).then_inc(f_st, 16)
        cols = lambda src, n: src.rearrange("n p t -> p n t")[:, :, n:]
        sp.dma_start(lkv[:], s_kv.rearrange("n p t -> p n t")[:, :, SEQ:SEQ + WIN]).then_inc(f_in, 16)
        sp.dma_start(ext[:, 0:2, :], cols(s_kv, WIN + SEQ)).then_inc(f_in, 16)
        sp.dma_start(dq[:, 0:12, :], cols(s_qkv, SEQ)).then_inc(f_in, 16)
        sp.dma_start(dq[:, 12:16, :], cols(s_z, SEQ)).then_inc(f_in, 16)
        sp.dma_start(da[:, 0:4, :], cols(s_qa, SEQ)).then_inc(f_in, 16)
        sp.dma_start(da[:, 4:8, :], cols(s_qc, SEQ)).then_inc(f_in, 16)
        sp.dma_start(wkv[:, 0], io["state_win_k"].rearrange("b s v d -> s b (v d)")).then_inc(f_in, 16)
        sp.dma_start(wkv[:, 1], io["state_win_v"].rearrange("b s v d -> s b (v d)")).then_inc(f_in, 16)
        sp.dma_start(dmk[:], io["k_dmask"]).then_inc(f_in, 16)
        for v in range(2):
            for g in range(4):
                sp.dma_start(sks[32 * g:32 * g + 32, v:v + 1], io["attn_sink"][4 * v + g:4 * v + g + 1].partition_broadcast(32)).then_inc(f_in, 16)

        def load_ck(b, slot):
            sp.wait_ge(m_kt, b + 1)
            sp.dma_start(ck[:, slot], io["cache_mem_k"][bass.ds(b, 1)].rearrange("b (t s) h d -> s (b t) (h d)", s=P)).then_inc(m_in[slot], 16)

        for b in range(DB):
            sp.dma_start(cvm[:, b], io["cache_mem_v"][b].rearrange("(t s) h d -> s t (h d)", s=P)).then_inc(f_in, 16)
        for b in range(DB):
            sp.dma_start(sd[:, b], io["state_rec"][b].rearrange("h k v -> k h v")).then_inc(f_in, 16)
        with sp.Fori(0, DB // 2) as i:
            for b in range(2):
                load_ck(2 * i + b, b)
        for v, (src, dst, pdst) in enumerate((("state_win_k", "win_k_sample", "win_k_prompt"), ("state_win_v", "win_v_sample", "win_v_prompt"))):
            sp.dma_start(io[dst][:, 0:WIN - DS].rearrange("b s v d -> b (s v d)"),
                         io[src][:, DS:WIN].rearrange("b s v d -> b (s v d)")).then_inc(f_st, 16)
            sp.wait_ge(f_ac, ACn("new_out"))
            sp.dma_start(io[pdst][0].rearrange("s v d -> s (v d)"), kvo[:, 0, v, :]).then_inc(f_st, 16)
            for b in range(DB):
                sp.dma_start(io[dst][b, WIN - DS:WIN].rearrange("s v d -> s (v d)"), kvo[DS * b:DS * b + DS, 1, v, :]).then_inc(f_st, 16)
        sp.wait_ge(f_ac, ACn("tail_out"))
        sp.dma_start(io["conv_prompt"][0], tlo[0:3, :]).then_inc(f_st, 16)
        for b in range(DB):
            sp.dma_start(io["conv_sample"][b], tlo[4 + DS * b:7 + DS * b, :]).then_inc(f_st, 16)
        for f, name in ((2, "mem_o"), (0, "win_o1"), (1, "o_z")):
            sp.wait_ge(f_dv, DVn(name))
            sp.dma_start(cols(s_br[4 * f:4 * f + 4], SEQ), dob[:, f]).then_inc(f_st, 16)
        sp.wait_ge(g_ad, 8)
        for b in range(DB):
            sp.dma_start(io["rec_sample"][b].rearrange("h k v -> k h v"), sd[:, b]).then_inc(f_st, 16)
        F_ST = 16 * (1 + 2 * (2 + DB) + 1 + DB + 3 + DB)
        sp.wait_ge(f_st, F_ST)
        def load_wb(j):
            n = NPD + j
            sp.wait_ge(w_lo, n + 1)
            src = wbv[ORDER[j // 4]][:, 256 * (j % 4):256 * (j % 4) + 256]
            dst = slab(raw, n % 2)
            for h in range(2):
                if ORDER[j // 4] == 0:
                    sp.dma_start(dst[64 * h:64 * h + 64], src.rearrange("(v g d) n -> v d g n", v=2, g=4)[h]).then_inc(w_in[n % 2], 16)
                else:
                    sp.dma_start(dst[:, 2 * h:2 * h + 2], src.rearrange("(k p) n -> p k n", p=P)[:, 2 * h:2 * h + 2]).then_inc(w_in[n % 2], 16)

        def load_br(r):
            sp.wait_ge(b_lo, r + 1)
            sp.dma_start(brw[:], s_br[4 * ORDER[r]:4 * ORDER[r] + 4].rearrange("n p t -> p n t")).then_inc(b_in, 16)

        def load_q(j):
            sp.wait_ge(q_mx, 6 * j + 6)
            m = 8 * ORDER[j // 4] + 2 * (j % 4)
            sp.dma_start(gat[:, j % 2], s_gate[m:m + 2].rearrange("n p t -> p n t")).then_inc(q_in[j % 2], 16)

        load_wb(0)
        load_wb(1)
        sp.sem_inc(b_lo, 1)
        load_br(0)
        load_q(0)
        load_q(1)
        for j in range(12):
            if j + 2 < 12:
                load_wb(j + 2)
                load_q(j + 2)
            if j in (0, 4):
                load_br(j // 4 + 1)
        for m in range(8):
            n = NPO + m
            load_w(n, [(raw[:, n % 2, 4 * h:4 * h + 4, :], wov[:, 4 * h:4 * h + 4, P * m:P * m + P]) for h in range(2)])
        sp.wait_ge(q_mx, 12 + 72)
        sp.wait_ge(b_hi, 11)
        for j, name in enumerate(("ln_mix_post", "ln_ffn_pre", "ln_ffn_post")):
            sp.dma_start(gn[:, j, :], io[name].partition_broadcast(P)).then_inc(b_in, 16)

        def load_f(n, slot, view, col):
            sp.wait_ge(w_lo, n + 1)
            for h in range(2):
                sp.dma_start(raw[:, slot, 4 * h:4 * h + 4, :], view[:, 4 * h:4 * h + 4, bass.ds(col, P)]).then_inc(w_in[slot], 16)

        def load_fo(n, slot, f):
            sp.wait_ge(w_lo, n + 1)
            for h in range(2):
                sp.dma_start(raw[:, slot, 4 * h:4 * h + 4, :], wgv[bass.ds(f, 1)].rearrange("a p (k n) -> p (a k) n", n=P)[:, 4 * h:4 * h + 4]).then_inc(w_in[slot], 16)

        def norm_io(t, slot, rows, src, before):
            sp.wait_ge(t_xst[slot], before)
            sp.dma_start(xr[0:rows, slot, :], src).then_inc(r_in[slot], 16)

        def store_x1(t, slot, rows, dst):
            sp.wait_ge(u_xs, 2 + t + 1)
            sp.dma_start(dst, xr[0:rows, slot, :]).then_inc(t_xst[slot], 16)

        def store_y(t, slot, rows, dst):
            sp.wait_ge(t_x1, t + 1)
            sp.dma_start(dst, xr[0:rows, slot, :]).then_inc(t_xst[slot], 16)

        load_f(NPF, NPF % 2, wfv, 0)
        load_f(NPF + 1, (NPF + 1) % 2, wfv, FF)
        sp.sem_inc(t_xst[0], 16)
        sp.sem_inc(t_xst[1], 16)
        one = lambda v, t: v[bass.ds(t, 1)].rearrange("a p d -> (a p) d")
        with sp.Fori(0, NT // 2) as i:
            for b in range(2):
                norm_io(2 * i + b, b, P, one(x_view, 2 * i + b), 16 * i + 16)
            for b in range(2):
                store_x1(2 * i + b, b, P, one(s_x1, 2 * i + b))
        norm_io(NT, 0, NS, xs_view, 16 * 5)
        store_x1(NT, 0, NS, s_x1[NT][0:NS])

        def load_step(i, b):
            n = NPF + 3 * i - 1
            s = (NPF + 3 * b - 1) % 2
            load_f(n, s, wfv, P * i)
            load_f(n + 1, 1 - s, wfv, P * i + FF)
            load_fo(n + 2, s, i - 1)

        with sp.Fori(0, (NF - 2) // 2) as i:
            for b in (1, 2):
                load_step(2 * i + b, b)
        load_step(NF - 1, 1)
        load_fo(NPF + 3 * NF - 1, (NPF + 3 * NF - 1) % 2, NF - 1)

        def final_in(t, slot, rows, src, before):
            sp.wait_ge(t_xst[slot], before)
            sp.dma_start(xr[0:rows, slot, :], src).then_inc(r_in[slot], 16)

        final_in(0, 0, P, s_x1[0], 16 * 6)
        final_in(1, 1, P, s_x1[1], 16 * 5)
        with sp.Fori(0, NT // 2 - 1) as i:
            for b in range(2):
                store_y(9 + 2 * i + b, b, P, one(y_view, 2 * i + b))
            for b in range(2):
                final_in(2 * i + 2 + b, b, P, one(s_x1, 2 * i + 2 + b), 16 * i + 16 * (7 - b))
        for b in range(2):
            store_y(9 + 6 + b, b, P, y_view[6 + b])
        final_in(NT, 0, NS, s_x1[NT][0:NS], 16 * 10)
        store_y(9 + NT, 0, NS, ys_view)
        sp.wait_ge(t_xst[0], 16 * 11)
        sp.wait_ge(t_xst[1], 16 * 9)
        for s in range(2):
            sp.wait_ge(y_st[s], 16 + 16 * B_BA // 2)
            sp.wait_ge(a_st[s], 16 + 16 * NT)
        sp.wait_ge(o_st, 64)
        sp.wait_ge(ob_st, 16 + 16 * NT)
        for c in range(3):
            sp.wait_ge(gs_st[c], 16 + 16 * 24)

    @block.gpsimd
    def _(pool):
        pool.sem_inc(w_lo, 2)
        pool.memset(ssq[:], 1.0).then_inc(pad0, 1)
        pool.memset(ba[:], 0.0).then_inc(pad0, 1)
        pool.memset(st[:], 0.0).then_inc(pad0, 1)

        def split_at(n, slot, landed, done):
            pool.wait_ge(w_in[slot], landed)
            pool.wait_ge(g_mm, done)
            pool.tensor_tensor(wsp[:, slot, 0], raw[:, slot], ones.unsqueeze(1).to_broadcast([P, KT, P]),
                               ALU.mult).then_inc(w_hi, 1)
            pool.wait_ge(w_hi, n + 1)
            pool.tensor_tensor(wsp[:, slot, 1], raw[:, slot], wsp[:, slot, 0].bitcast(F32),
                               ALU.subtract).then_inc(w_lo, 1)

        def split(n, slot, landed):
            split_at(n, slot, landed, 6 + units(n - 1))

        pool.wait_ge(k_in, 16 * 6)
        split(0, 0, 32)
        split(1, 1, 32)
        pool.wait_ge(x_lo, 2 + 11)
        pool.memset(cv[:, 0, 0:3], 0.0).then_inc(pad0, 1)
        pool.memset(cv[:, 1, 0:3], 0.0).then_inc(pad0, 1)
        with pool.Fori(1, 13) as i:
            for b in range(2):
                split(2 * i + b, b, 32 * i + 32)
        for n in range(26, NPB):
            split(n, n % 2, 32 * (n // 2) + 32)
        pool.sem_inc(dm_ok, 1)
        pool.wait_ge(pp, 17)
        pool.wait_ge(g_mm, 6 + UC)

        with pool.Fori(0, 4) as i:
            for b in range(2):
                t = 2 * i + b
                pool.wait_ge(dm_ok, t + 1)
                pool.tensor_tensor(ug[:], bc_h(k_le), bc_c(per(Q_G, t)), ALU.mult).then_inc(ug_ok, 1)
                pool.tensor_tensor(mrk[:], bc_h(k_le), bc_c(per(Q_RK, t)), ALU.mult).then_inc(mrk_ok, 1)
                pool.wait_ge(kq_ok, t + 1)
                pool.tensor_tensor(bi[:], bc_h(ident), bc_c(per(Q_BK, t)), ALU.mult).then_inc(bi_ok, 1)
                for j in range(3):
                    s = NPB + 3 * b + j
                    split_at(NPB + 3 * t + j, s % 2, 32 * (3 * i + s // 2) + 32, 6 + UC + 9 * t + 3 * j - 3)
        for j in range(12):
            n = NPD + j
            split_at(n, n % 2, 32 * (n // 2) + 32, 6 + UD + (6 * (j - 1) if j > 0 else -3))
        for m in range(8):
            n = NPO + m
            split_at(n, n % 2, 32 * (n // 2) + 32, 6 + UO + (3 * (m - 1) if m > 0 else -6))
        split_at(NPF, NPF % 2, 32 * (NPF // 2) + 32, 6 + UF - 3)
        split_at(NPF + 1, (NPF + 1) % 2, 32 * ((NPF + 1) // 2) + 32, 6 + UF)

        def split_step(i, b, landed):
            for j in range(3):
                if isinstance(i, int):
                    done = (3, 6, 9)[j]
                else:
                    done = 6 * i + (0, 0, 3)[j]
                    if j == 1:
                        pool.wait_ge(o_mm, 24 * i + 24)
                split_at(NPF + 3 * i - 1 + j, (NPF + 3 * b - 1 + j) % 2, landed(j), 6 + UF + done)

        base = lambda b, j: 32 * ((NPF + 3 * b - 1 + j) // 2) + 32
        split_step(1, 1, lambda j: base(1, j))
        with pool.Fori(0, (NF - 2) // 2) as i:
            for b in (2, 3):
                split_step(2 * i + b, b, lambda j, b=b: 96 * i + base(b, j))
        n = NPF + 3 * NF - 1
        split_at(n, n % 2, 32 * (n // 2) + 32, 6 + UF + 6 * NF)

    @block.tensor
    def _(pe):
        pe.sem_inc(g_mm, 6)
        pe.sem_inc(ss_mm, 1)
        pe.wait_ge(k_in, 16 * 6)
        for j in range(12):
            mm = pe.transpose(psum[:, 5, 28 * j:28 * j + 28], sc_in[:, P * j:P * j + P], ident[0:28, 0:28])
        mm.then_inc(sc_t, 1)

        def turn_x(n, slot, rows):
            pe.wait_ge(x_nm, 2 + n + 1)
            pe.wait_ge(x_lo, n + 1)
            for k in range(KT):
                mm = pe.transpose(psum[:, 2 * slot + k // 4, P * (k % 4):P * (k % 4) + rows],
                                  xs[0:rows, slot, P * k:P * k + P], ident[0:rows, 0:rows])
            mm.then_inc(x_tr, 1)

        with pe.Fori(0, NT // 2) as i:
            for b in range(2):
                turn_x(2 * i + b, b, P)
        for n, rows, *_ in rest_tiles:
            turn_x(n, n % 2, rows)

        def gemm(n, slot, m=P):
            pe.wait_ge(w_lo, n + 3)
            for c in range(3):
                pe.wait_ge(g_ev, units(n) + c + 1)
                for k in range(KT):
                    for q, (a, h) in enumerate(((0, 0), (0, 1), (1, 0))):
                        mm = pe.matmul(psum[0:m, c, 0:CH], wsp[:, slot, a, k, 0:m],
                                       actT[:, h, k, CH * c:CH * c + CH],
                                       start=(k == 0 and q == 0), stop=(k == KT - 1 and q == 2))
                mm.then_inc(g_mm, 1)

        def head_squares(n):
            pe.wait_ge(sq_ok, n + 1)
            for t in range(NT + 1):
                r = P if t < NT else NS
                mm = pe.matmul(psum[0:r, 4, bass.ds(n * (NT + 1) + t, 1)], sqb[:, P * t:P * t + r], ones[:, 0:1],
                               start=True, stop=True)
            mm.then_inc(ss_mm, 1)

        pe.wait_ge(x_lo, 2 + 11)
        gemm(0, 0)
        gemm(1, 1)
        with pe.Fori(0, 4) as i:
            for b in range(2):
                gemm(2 * i + 2 + b, b)
                head_squares(2 * i + b)
        with pe.Fori(5, 13) as i:
            for b in range(2):
                gemm(2 * i + b, b)
        gemm(B_BA, 0, m=8)
        for j in range(8):
            n = B_MEM + j
            pe.wait_ge(w_lo, n + 3)
            pe.wait_ge(g_ev, units(n) + 1)
            for k in range(KT):
                for q, (a, h) in enumerate(((0, 0), (0, 1), (1, 0))):
                    mm = pe.matmul(psum[:, j % 3, 0:MEM], wsp[:, n % 2, a, k], memT[:, h, k, :],
                                   start=(k == 0 and q == 0), stop=(k == KT - 1 and q == 2))
            mm.then_inc(g_mm, 1)
        for t in range(NT + 1):
            r = P if t < NT else NS
            if t >= 2:
                pe.wait_ge(mc, t - 1)
            pe.transpose(psum[0:r, 5 + t % 2, 0:8], y2[0:8, 0, P * t:P * t + r], ident[0:8, 0:8]).then_inc(mt, 1)
        pe.wait_ge(g_ev, 3 + units(NPB))
        for s in range(2):
            for v in range(2):
                j = 2 * s + v
                pe.wait_ge(mc, NT + 1 + max(j - 1, 0))
                for h in range(4):
                    src = mkT[:, h, P * s:P * s + P] if v == 0 else y[:, h // 2, MEM * (h % 2) + P * s:MEM * (h % 2) + P * s + P]
                    mm = pe.transpose(psum[:, 5 + j % 2, P * h:P * h + P], src, ident)
                mm.then_inc(mt, 1)
        pe.wait_ge(pp, 10)
        pe.wait_ge(mc, NT + 1 + 4)
        for j, (full, dcd) in enumerate(((K_LE, K_D_LE), (K_GT, K_D_GT), (K_ONE, K_D_BLK))):
            pe.matmul(psum[:, 5, 36 * j:36 * j + 32], kc[:, full:full + P], par[:, Q_G, 0:NT, :],
                      start=True, stop=True)
            mm = pe.matmul(psum[0:NS, 5, 36 * j + 32:36 * j + 36], kc[0:NS, dcd:dcd + NS], par[0:NS, Q_G, NT, :],
                           start=True, stop=True)
        mm.then_inc(pg, 1)
        pe.wait_ge(pa, 10)
        pe.wait_ge(st0, 3)

        def mm4(bank, lhs, rhs, done, w=P):
            for h in range(BH):
                mm = pe.matmul(psum[:, bank, w * h:w * h + w], lhs(h), rhs(h), start=True, stop=True)
            mm.then_inc(done, 1)

        def pe_tile(i, b):
            t = 2 * i + b
            k, v, q = (lambda h: gin[:, b, 4 + h, :]), (lambda h: gin[:, b, 8 + h, :]), (lambda h: gin[:, b, h, :])

            def turn4(bank, src, done):
                for h in range(BH):
                    mm = pe.transpose(psum[:, bank, P * h:P * h + P], src(h), ident)
                mm.then_inc(done, 1)

            for step in TILE:
                if step == "KV":
                    pe.wait_ge(l_in["kv"][b], 16 * i + 16)
                    pe.wait_ge(c_ob, t + 1)
                    turn4(5, k, e_tk)
                    pe.wait_ge(c_o, t + 1)
                    turn4(6, v, e_tv)
                elif step == "DEC":
                    pe.wait_ge(ug_ok, t + 1)
                    pe.wait_ge(c_s, t + 1)
                    pe.matmul(psum[:, 7, :], k_gt, ug[:], start=True, stop=True).then_inc(e_gt, 1)
                    pe.wait_ge(bi_ok, t + 1)
                    pe.wait_ge(kd_ok, t + 1)
                    pe.matmul(psum[:, 5, :], ones, bi[:], start=True, stop=True).then_inc(e_br, 1)
                elif step == "KK":
                    pe.wait_ge(vb_ok, t + 1)
                    mm4(6, k, k, e_kk)
                    pe.wait_ge(dec_ok, t + 1)
                    pe.wait_ge(l_in["q"][b], 16 * i + 16)
                    mm4(7, k, q, e_kq)
                elif step == "INV":
                    pe.wait_ge(at_st, 4 * t + 4)
                    turn4(5, lambda h: xt[:, h, :], e_x0)
                elif step == "UW":
                    pe.wait_ge(c_xt, 6 * t + 6)
                    mm4(6, lambda h: xt[:, h, :], lambda h: vb[:, h, :], e_u)
                    mm4(5, lambda h: kbe[:, h, :], lambda h: xt[:, h, :], e_w)
                elif step == "PO":
                    pe.wait_ge(c_w, t + 1)
                    mm4(7, lambda h: wt[:, h, :], lambda h: st[:, h, :], e_p1)
                    mm4(5, q, lambda h: st[:, h, :], e_o1)
                elif step == "SO":
                    pe.wait_ge(vn_ok, t + 1)
                    mm4(7, lambda h: kd[:, h, :], lambda h: vn[:, h, :], e_sp)
                    pe.wait_ge(c_u, t + 1)
                    mm4(6, lambda h: kqd[:, h, :], lambda h: vn[:, h, :], e_o2)
                elif step == "OT":
                    pe.wait_ge(on_ok, t + 1)
                    pe.wait_ge(c_o1, t + 1)
                    turn4(5, lambda h: oo[:, h, :], e_ot)
                elif step[0] == "Y":
                    l = step[1]
                    pe.wait_ge(al_ok, 6 * t + l + 1)
                    pe.wait_ge(c_x, 6 * t + l)
                    mm4(6, lambda h: atl[:, l, h, :], lambda h: xx[:, h, :], e_y)
                elif step[0] == "X":
                    l = step[1]
                    pe.wait_ge(c_y, 6 * t + l)
                    if l == 1:
                        pe.wait_ge(kq_ok, t + 2)
                    else:
                        pe.wait_ge(c_xt, 6 * t + l - 1)
                    if l < 6:
                        mm4(5, lambda h: xt[:, h, :], lambda h: yy[:, h, :], e_xx)
                    mm4(7, lambda h: yy[:, h, :], lambda h: xt[:, h, :], e_xt)
                elif step[0] == "G":
                    j, c = divmod(step[1], 3)
                    if c == 0:
                        pe.wait_ge(w_lo, NPB + 3 * t + j + 3)
                    gate_chunk((NPB + 3 * b + j) % 2, c, UC + 9 * t + step[1])
                elif step[0] == "S":
                    j = step[1]
                    if j == 0:
                        pe.wait_ge(l_in["win"][b], 32 * i + 32)
                        pe.wait_ge(l_in["qa"][b], 16 * i + 16)
                        pe.wait_ge(a_pt, 8 * t + 1)
                        for w in range(2):
                            mm = pe.transpose(psum[:, 4, P * w:P * w + P], awin[:, b, 1, P * w:P * w + P], ident)
                        mm.then_inc(a_vt, 1)
                    if j == 4:
                        pe.wait_ge(l_in["qc"][b], 16 * i + 16)
                    pe.wait_ge(av_ok, 6 * t + j + 1)
                    if j < 4:
                        kv, g = j // 2, 2 * (j % 2)
                        for a in range(2):
                            pe.matmul(psum[:, 3, 256 * a:256 * a + 256], idb[:], mbf[:, b, :], start=True, stop=False)
                            mm = pe.matmul(psum[:, 3, 256 * a:256 * a + 256], ain[64 * kv:64 * kv + 64, b, g + a, :],
                                           awin[64 * kv:64 * kv + 64, b, 0, :], start=False, stop=True)
                    else:
                        for a in range(2):
                            h = 2 * (j - 4) + a
                            mm = pe.matmul(psum[:, 3, 256 * a:256 * a + 256], ain[:, b, 4 + h, :], mkT[:, h, :],
                                           start=True, stop=True)
                    mm.then_inc(a_s, 1)
                elif step[0] == "T":
                    j = step[1]
                    pe.wait_ge(a_e, 6 * t + j + 1)
                    pe.wait_ge(a_pt, 8 * t + QI[j] + 1)
                    if j == 0:
                        pe.wait_ge(a_vc, t + 1)
                    for a in range(2):
                        for w in range(2):
                            mm = pe.transpose(psum[:, 4, P * (2 * a + w):P * (2 * a + w) + P],
                                              pr[:, a, P * w:P * w + P], ident)
                    mm.then_inc(a_t, 1)
                elif step[0] == "V":
                    j = step[1]
                    pe.wait_ge(a_pt, 8 * t + QI[j] + 2)
                    for a in range(2):
                        w = AHD if j < 4 else P
                        for s in range(2):
                            rhs = vtok[:, s, 64 * (j // 2):64 * (j // 2) + 64] if j < 4 else \
                                mv[:, s, P * (2 * (j - 4) + a):P * (2 * (j - 4) + a) + P]
                            mm = pe.matmul(psum[:, 3, w * a:w * a + w], pt[:, 2 * a + s, :], rhs,
                                           start=(s == 0), stop=(s == 1))
                    mm.then_inc(a_v, 1)
                elif step[0] == "F":
                    f = step[1]
                    pe.wait_ge(a_on, 2 * t + f + 1)
                    pe.wait_ge(a_pt, 8 * t + (5, 8)[f])
                    for g in range(4):
                        mm = pe.transpose(psum[:, 4, P * g:P * g + P], oat[:, f, P * g:P * g + P], ident)
                    mm.then_inc(a_t, 1)

        def gate_chunk(slot, c, u):
            pe.wait_ge(g_ev, u + 1)
            for k in range(KT):
                for q, (a, h) in enumerate(((0, 0), (0, 1), (1, 0))):
                    mm = pe.matmul(psum[:, c, 0:CH], wsp[:, slot, a, k, :], actT[:, h, k, CH * c:CH * c + CH],
                                   start=(k == 0 and q == 0), stop=(k == KT - 1 and q == 2))
            mm.then_inc(g_mm, 1)

        with pe.Fori(0, 4) as i:
            for b in range(2):
                pe_tile(i, b)
        Dn = NS
        pe.wait_ge(gs_st[2], 16 + 16 * 24)
        pe.wait_ge(c_ob, 2 + NT - 1)
        pe.wait_ge(c_s, 1 + NT)
        pe.wait_ge(a_st[1], 16 + 16 * NT)
        pe.sem_inc(m_kt, 2)
        pe.sem_inc(m_sc, 2)

        def done(mm, name):
            mm.then_inc(f_pe, 1)

        pe.wait_ge(f_in, F_IN)
        for v in range(2):
            pe.transpose(psum[:, 5, P * v:P * v + P], lkv[:, v, :], ident)
            pe.transpose(psum[0:Dn, 5, 256 + P * v:256 + P * v + P], ext[:, v, :], ident)
        for n in range(12):
            mm = pe.transpose(psum[0:3 + NS, n // 4, P * (n % 4):P * (n % 4) + P], tail[:, n, :], ident)
        done(mm, "out")
        pe.wait_ge(f_ac, ACn("tail_out"))
        pe.wait_ge(f_dv, DVn("d3"))
        for h in range(BH):
            pe.transpose(psum[0:Dn, 0, P * h:P * h + P], dq[:, 4 + h, :], ident)
            pe.transpose(psum[0:Dn, 1, P * h:P * h + P], dq[:, 8 + h, :], ident)
        pe.matmul(psum[0:Dn, 2, 0:P], kc[0:Dn, K_D_GT:K_D_GT + NS], dug[:], start=True, stop=True)
        pe.matmul(psum[0:Dn, 2, P:2 * P], ones[0:Dn, 0:Dn], dia[:, 0], start=True, stop=True)
        pe.matmul(psum[:, 2, 2 * P:3 * P], ones[0:Dn, :], dia[:, 1], start=True, stop=True)
        pe.matmul(psum[:, 2, 3 * P:4 * P], ones[0:Dn, :], dia[:, 2], start=True, stop=True)
        pe.matmul(psum[:, 3, 0:P], ones[0:Dn, :], dia[:, 3], start=True, stop=True)
        for h in range(BH):
            pe.matmul(psum[0:Dn, 3, P + NS * h:P + NS * h + NS], dq[:, 4 + h, :], dq[:, 4 + h, :], start=True, stop=True)
            mm = pe.matmul(psum[0:Dn, 3, 2 * P + NS * h:2 * P + NS * h + NS], dq[:, 4 + h, :], dq[:, h, :], start=True, stop=True)
        done(mm, "bcast")
        for b in range(DB):
            mm = pe.transpose(psum[:, 6 + b // 4, P * (b % 4):P * (b % 4) + P], wkv[:, 0, b, :], ident)
        done(mm, "win_kt")
        pe.wait_ge(f_dv, DVn("el"))
        pe.wait_ge(f_ac, ACn("rq"))

        def mem_keys(b, slot, landed):
            pe.wait_ge(m_in[slot], landed)
            pe.wait_ge(m_ka, b + 1)
            pe.wait_ge(m_kd, b + 1)
            for h in range(4):
                for t in range(2):
                    mm = pe.transpose(psum[:, 2 * slot + h // 2, 256 * (h % 2) + P * t:256 * (h % 2) + P * t + P],
                                      ck[:, slot, t, P * h:P * h + P], ident)
            mm.then_inc(m_kt, 1)

        def mem_scores(b, slot):
            pe.wait_ge(m_ka, b + 3)
            pe.wait_ge(m_kd, b + 3)
            for h in range(4):
                for t in range(2):
                    mm = pe.matmul(psum[:, 4, bass.ds(P * t + DS * h + 16 * b, DS)], ckT[:, slot, h, P * t:P * t + P],
                                   da[:, 4 + h, bass.ds(DS * b, DS)], start=True, stop=True)
            mm.then_inc(m_sc, 1)

        mem_keys(0, 0, 16)
        with pe.Fori(0, DB // 2 - 1) as i:
            mem_keys(2 * i + 1, 1, 16 * i + 16)
            mem_scores(2 * i, 0)
            mem_keys(2 * i + 2, 0, 16 * i + 32)
            mem_scores(2 * i + 1, 1)
        mem_keys(DB - 1, 1, 64)
        mem_scores(DB - 2, 0)
        mem_scores(DB - 1, 1)
        pe.wait_ge(f_ac, ACn("mem_s"))
        for t in range(2):
            mm = pe.transpose(psum[:, 5, P * t:P * t + P], mS[:, t, :], ident)
        done(mm, "mem_rows")
        pe.wait_ge(f_dv, DVn("xt0"))
        for h in range(BH):
            mm = pe.transpose(psum[0:Dn, 0, NS * h:NS * h + NS], dxt[:, h, :], ident[0:Dn, 0:Dn])
        done(mm, "x0")
        pe.wait_ge(f_ac, ACn("wkT"))
        for v in range(2):
            rows = slice(64 * v, 64 * v + 64)
            for b in range(DB):
                pe.matmul(psum[:, 6 + v, 0:P].rearrange("p (g b s) -> p g b s", g=4, b=DB)[:, :, b, :], wkT[rows, b, :],
                          da[rows, 0:4, DS * b:DS * b + DS], start=True, stop=True)
            mm = pe.matmul(psum[0:Dn, 6 + v, 256:256 + P], ext[rows, 0, :], da[rows, 0:4, :], start=True, stop=True)
        done(mm, "new_sc")
        pe.wait_ge(f_dv, DVn("at1"))
        pe.wait_ge(f_ac, ACn("x0"))
        for h in range(BH):
            mm = pe.matmul(psum[0:Dn, 0, P + NS * h:P + NS * h + NS], dat1[:, h, :], dxx[:, h, :], start=True, stop=True)
        done(mm, "y")
        pe.wait_ge(f_dv, DVn("mem_n"))
        for t in range(2):
            mm = pe.transpose(psum[:, 5, P * t:P * t + P], mR[:, P * t:P * t + P], ident)
        done(mm, "mem_pt")
        pe.wait_ge(f_ac, ACn("y"))
        for h in range(BH):
            mm = pe.matmul(psum[0:Dn, 0, 2 * P + NS * h:2 * P + NS * h + NS], dyy[:, h, :], dxt[:, h, :], start=True, stop=True)
        done(mm, "xt")
        pe.wait_ge(f_ac, ACn("win_s"))
        for v in range(2):
            pe.transpose(psum[:, 7, 160 * v:160 * v + P], sS[:, v, :], ident)
            mm = pe.transpose(psum[:, 7, 160 * v + P:160 * v + 160], sS[0:Dn, 2 + v, :], ident[0:Dn, 0:Dn])
        done(mm, "win_rows")
        pe.wait_ge(f_dv, DVn("xt"))
        for h in range(BH):
            pe.matmul(psum[:, 1, NS * h:NS * h + NS], dvb[:, h, :], dxt[:, h, :], start=True, stop=True)
            mm = pe.matmul(psum[:, 1, P + NS * h:P + NS * h + NS], dkb[:, h, :], dxt[:, h, :], start=True, stop=True)
        done(mm, "u_w")
        pe.wait_ge(f_ac, ACn("mem_p"))
        for b in range(DB):
            for h in range(4):
                for t in range(2):
                    val = cvm[:, b, t, P * h:P * h + P]
                    mm = pe.matmul(psum[:, 5, 2 * P + NS * h + DS * b:2 * P + NS * h + DS * b + DS], val,
                                   mS[:, t, 16 * b + DS * h:16 * b + DS * h + DS], start=(t == 0), stop=(t == 1))
        done(mm, "mem_o")
        pe.wait_ge(f_dv, DVn("win_n"))
        for v in range(2):
            pe.transpose(psum[:, 6, P * v:P * v + P], sR[:, v, 0:P], ident)
            mm = pe.transpose(psum[0:Dn, 6, 256 + P * v:256 + P * v + P], sR[:, v, P:P + NS], ident)
        done(mm, "win_pt")
        pe.wait_ge(f_dv, DVn("wT"))
        for b in range(DB):
            for h in range(BH):
                mm = pe.matmul(psum[:, 4, 64 * h + 8 * b:64 * h + 8 * b + 8], sd[:, b, h, :],
                               wq[:, h, b].rearrange("p a s -> p (a s)"), start=True, stop=True)
        done(mm, "w_q_s")
        pe.wait_ge(f_ac, ACn("win_p"))
        for b in range(DB):
            pe.matmul(psum[:, 7, 0:256].rearrange("p (a b s) -> p a b s", a=8, b=DB)[:, :, b, :], wkv[:, 1, b, :],
                      sS[:, 0:2, :].rearrange("p v (g b s) -> p (v g) b s", g=4, b=DB)[:, :, b, :], start=True, stop=True)
        mm = pe.matmul(psum[:, 7, 256:512], kvo[0:Dn, 1, 1, :], sS[0:Dn, 2:4, :], start=True, stop=True)
        done(mm, "win_o")
        pe.wait_ge(f_dv, DVn("vT"))
        for h in range(BH):
            mm = pe.transpose(psum[0:Dn, 0, P * h:P * h + P], dvT[:, h, :], ident)
        done(mm, "vn")
        pe.wait_ge(f_ac, ACn("vn"))
        for h in range(BH):
            mm = pe.matmul(psum[:, 1, 2 * P + NS * h:2 * P + NS * h + NS], dvn[:, h, :], dkq[:, h, :], start=True, stop=True)
        done(mm, "o")
        pe.wait_ge(f_ac, ACn("sq"))
        mm = pe.matmul(psum[:, 1, 3 * P:4 * P], ones, dsq[:], start=True, stop=True)
        done(mm, "sumsq")
        for j in range(8):
            half, h = divmod(j, 4)
            pe.wait_ge(f_dv, DVn(f"vm{half}"))
            if j >= 3:
                pe.wait_ge(g_ad, j - 2)
            pe.matmul(psum[:, (0, 3, 4)[j % 3], :], dkd[:, h, :], vnm[:, h], start=True, stop=True).then_inc(g_up, 1)
        pe.sem_inc(o_mm, 48)
        passes = ((0, 0), (0, 1), (1, 0))
        for j in range(12):
            n, a4 = NPD + j, 4 * ((j // 4) % 2)
            pe.wait_ge(w_lo, n + 3)
            pe.wait_ge(b_lo, j // 4 + 2)
            for half in range(2):
                for c in range(3):
                    pe.wait_ge(g_ev, UD + 6 * j + 3 * half + c + 1)
                    for k in range(4):
                        for q, (a, h) in enumerate(passes):
                            mm = pe.matmul(psum[:, c, 0:CH], slab(wsp[:, :, a], n % 2)[:, k, P * half:P * half + P],
                                           actD[:, h, a4 + k, CH * c:CH * c + CH], start=(k == 0 and q == 0), stop=(k == 3 and q == 2))
                    mm.then_inc(g_mm, 1)

        def full_chunk(slot, c):
            for k in range(KT):
                for q, (a, h) in enumerate(passes):
                    mm = pe.matmul(psum[:, c, 0:CH], wsp[:, slot, a, k, :], actD[:, h, k, CH * c:CH * c + CH],
                                   start=(k == 0 and q == 0), stop=(k == KT - 1 and q == 2))
            mm.then_inc(g_mm, 1)

        def mix_chunk(slot, c, first):
            for m in range(KT):
                if first:
                    pe.wait_ge(b_lo, 4 + m + 1)
                for q, (a, h) in enumerate(passes):
                    mm = pe.matmul(psum[:, c, 0:CH], wsp[:, slot, a, m, :], actD[:, h, (m + 4) % 8, CH * c:CH * c + CH],
                                   start=(m == 0 and q == 0), stop=(m == KT - 1 and q == 2))
            mm.then_inc(g_mm, 1)

        for m in range(8):
            n = NPO + m
            pe.wait_ge(w_lo, n + 3)
            for c in range(3):
                pe.wait_ge(g_ev, UO + 3 * m + c + 1)
                mix_chunk(n % 2, c, m == 0 and c == 0)

        def turn_rows(t, slot, rows, col, ahead):
            pe.wait_ge(t_y, ahead)
            for k in range(KT):
                mm = pe.transpose(psum[0:rows, 2 * slot + k // 4, P * (k % 4):P * (k % 4) + P], accT[:, k, col:col + rows], ident)
            mm.then_inc(t_tr, 1)

        def turn_back(t, slot, rows):
            pe.wait_ge(u_xs, 2 + t + 1)
            pe.wait_ge(u_lo, t + 1)
            for k in range(KT):
                mm = pe.transpose(psum[:, 4 + 2 * slot + k // 4, P * (k % 4):P * (k % 4) + rows],
                                  yr[0:rows, slot, P * k:P * k + P], ident[0:rows, 0:rows])
            mm.then_inc(u_tr, 1)

        pe.wait_ge(g_ev, 3 + UF)
        turn_rows(0, 0, P, 0, 1)
        turn_rows(1, 1, P, P, 2)
        for i in range(NT // 2 - 1):
            for b in range(2):
                turn_rows(2 * i + 2 + b, b, P, 2 * P * i + 2 * P + P * b, 2 * i + 3 + b)
            for b in range(2):
                turn_back(2 * i + b, b, P)
        turn_rows(NT, 0, NS, SEQ, NT + 1)
        turn_back(6, 0, P)
        turn_back(7, 1, P)
        turn_back(8, 0, NS)

        def in_panel(n, slot, read, before):
            pe.wait_ge(w_lo, n + 3)
            for c in range(3):
                pe.wait_ge(read, before + c + 1)
                full_chunk(slot, c)

        def out_panel(n, slot, i, fs):
            pe.wait_ge(w_lo, n + 3)
            pe.wait_ge(f_lo, 3 + 3 * i + 3)
            for m in range(KT):
                for c in range(3):
                    x = 3 * m + c
                    pe.wait_ge(o_ad, 24 * i + x + 1)
                    for q, (a, h) in enumerate(passes):
                        mm = pe.matmul(psum[:, 3 + x % 4, 0:CH], wsp[:, slot, a, m, :], fT[:, fs, h, CH * c:CH * c + CH],
                                       start=(q == 0), stop=(q == 2))
                    mm.then_inc(o_mm, 1)

        pe.wait_ge(u_lo, 2 + 9)
        pe.wait_ge(t_y, 2 + 9)
        in_panel(NPF, NPF % 2, f_fr, 0)
        in_panel(NPF + 1, (NPF + 1) % 2, g_ev, 3 + UF)

        def ffn_step(i, b):
            n, s = NPF + 3 * i - 1, (NPF + 3 * b - 1) % 2
            in_panel(n, s, f_fr, 3 * i)
            in_panel(n + 1, 1 - s, g_ev, 3 + UF + 3 * i)
            out_panel(n + 2, s, i - 1, (b - 1) % 2)

        with pe.Fori(0, (NF - 2) // 2) as i:
            for b in (1, 2):
                ffn_step(2 * i + b, b)
        ffn_step(NF - 1, 1)
        n = NPF + 3 * NF - 1
        out_panel(n, n % 2, NF - 1, 1)

        pe.wait_ge(o_ad, 4 + 24 * NF)
        for i in range(NT // 2):
            for b in range(2):
                turn_rows(9 + 2 * i + b, b, P, 2 * P * i + P * b, 2 * i + 10 + b)
        turn_rows(9 + NT, 0, NS, SEQ, 9 + NT + 1)

    @block.scalar
    def _(act):
        act.sem_inc(g_ev, 3)
        act.sem_inc(y_a, 2)

        def squares(n, slot, rows, landed):
            act.wait_ge(x_in[slot], landed)
            act.activation(xjunk[0:rows, :], xin[0:rows, slot, :], ACT.Square,
                           accum_out=rs[0:rows, slot, 0:1]).then_inc(x_sq, 1)

        def root(n, slot, rows):
            act.wait_ge(x_rs, 2 * n + 1)
            act.activation(rs[0:rows, slot, 2:3], rs[0:rows, slot, 1:2], ACT.Sqrt).then_inc(x_rt, 1)

        def hi_x(n, slot, rows, dst, col):
            act.wait_ge(x_tr, n + 1)
            act.activation(dst[:, 0, :, bass.ds(col, rows)],
                           psum[:, 2 * slot:2 * slot + 2, :].rearrange("p b (k t) -> p (b k) t", t=P)[:, :, 0:rows],
                           ACT.Copy).then_inc(x_hi, 1)

        act.wait_ge(sc_t, 1)
        act.activation(scT[:].rearrange("p n c -> p (n c)"), psum[:, 5, 0:336], ACT.Copy).then_inc(sc_c, 1)
        with act.Fori(0, NT // 2) as i:
            for b in range(2):
                squares(2 * i + b, b, P, 16 * i + 16)
                root(2 * i + b, b, P)
            for b in range(2):
                hi_x(2 * i + b, b, P, actT, 2 * P * i + P * b)
        for n, rows, _, _, dst, col in rest_tiles:
            squares(n, n % 2, rows, 16 * (n // 2) + 16)
            root(n, n % 2, rows)
            hi_x(n, n % 2, rows, dst, col)

        def evac_conv(n, slot):
            act.wait_ge(cv_st, 8 * n + 8)
            act.activation(by_step(cv[:, slot, 3 + SEQ:])[:, :, 0:3],
                           scT[:, bass.ds(n, 1), 0:24].rearrange("p a (b s) -> p (a b) s", b=DB), ACT.Copy)
            for c in range(3):
                act.wait_ge(g_mm, 6 + 3 * n + c + 1)
                w = CH if c < 2 else SEQ - 2 * CH
                if c == 2:
                    act.activation(by_step(cv[:, slot, 3 + SEQ:])[:, :, 3:7], by_step(psum[:, 2, w:CH]), ACT.Copy)
                    act.activation(cv[:, slot, 3 + CH * c:3 + CH * c + w], psum[:, c, 0:w], ACT.Copy).then_inc(cv_in, 1)
                    act.activation(tail[:, bass.ds(n, 1), :].rearrange("p a t -> p (a t)"),
                                   psum[:, 2, w - 3:CH], ACT.Copy).then_inc(g_ev, 1)
                else:
                    act.activation(cv[:, slot, 3 + CH * c:3 + CH * c + w], psum[:, c, 0:w], ACT.Copy).then_inc(g_ev, 1)

        def silu(n, slot, stored):
            act.wait_ge(cv_st, 16 + 8 * n + 8)
            act.wait_ge(y_st[slot], stored)
            act.activation(y2[:, slot, :], y[:, slot, :], ACT.Silu).then_inc(y_a, 1)

        def squares_of(n, slot):
            act.wait_ge(y_a, 2 + n + 1)
            act.wait_ge(ss_mm, n + 1)
            act.activation(sqb[:], y2[:, slot, :], ACT.Square).then_inc(sq_ok, 1)

        act.wait_ge(pad0, 5)
        act.wait_ge(sc_c, 1)
        evac_conv(0, 0)
        evac_conv(1, 1)
        with act.Fori(0, 4) as i:
            for b in range(2):
                evac_conv(2 * i + 2 + b, b)
                silu(2 * i + b, b, 16 * i + 16)
                squares_of(2 * i + b, b)
        for n in (10, 11):
            evac_conv(n, n % 2)
            silu(n - 2, n % 2, 16 * ((n - 2) // 2) + 16)

        def copy_row(n, dst_of, func, before=None):
            for c in range(3):
                act.wait_ge(g_mm, 6 + 3 * n + c + 1)
                if before is not None and c == 0:
                    act.wait_ge(*before)
                act.activation(dst_of(c), psum[:, c, 0:CH], func).then_inc(g_ev, 1)

        for n in range(B_Z, B_C):
            if n < B_Z + 2:
                silu(n - 2, n % 2, 16 * ((n - 2) // 2) + 16)
            copy_row(n, lambda c, n=n: y[:, n % 2, CH * c:CH * c + CH], ACT.Silu, (y_d, n - B_Z - 1) if n >= B_Z + 2 else (y_a, n + 1))
        for n in range(B_C, B_A):
            copy_row(n, lambda c, n=n: y2[:, n % 2, CH * c:CH * c + CH], ACT.Copy, (y_st[n % 2], 16 * (n // 2) + 16))
        act.wait_ge(ss_mm, 9)
        ssps = psum[:, 4, 0:8 * (NT + 1)].rearrange("p (n t) -> p n t", n=8)
        act.activation(ssq[:, :, 0:NT], ssps[:, :, 0:NT], ACT.Copy)
        act.activation(ssq[0:NS, :, NT:NT + 1], ssps[0:NS, :, NT:NT + 1], ACT.Copy).then_inc(ssq_ok, 1)
        for n in range(B_A, B_VA):
            act.wait_ge(y_d, (3, 4)[n - B_A] if n < B_A + 2 else YD(n - 2))
            for c in range(3):
                act.wait_ge(g_mm, 6 + 3 * n + c + 1)
                act.activation(y[:, n % 2, CH * c:CH * c + CH], psum[:, c, 0:CH], ACT.Copy)
                for quad in range(4):
                    mm = act.activation(cv[32 * quad:32 * quad + 32, n % 2, CH * c:CH * c + CH],
                                        psum[32 * (quad ^ 1):32 * (quad ^ 1) + 32, c, 0:CH], ACT.Copy)
                mm.then_inc(g_ev, 1)
        n = B_VA
        copy_row(n, lambda c: y2[:, 1, CH * c:CH * c + CH], ACT.Copy, (y_st[1], 16 * (n // 2) + 16))
        n = B_BA
        act.wait_ge(y_st[0], 16 * (n // 2) + 16)
        for c in range(3):
            act.wait_ge(g_mm, 6 + 3 * n + c + 1)
            act.activation(y2[0:8, 0, CH * c:CH * c + CH], psum[0:8, c, 0:CH], ACT.Copy).then_inc(g_ev, 1)
        act.wait_ge(y_d, YD(B_K))
        for j in range(8):
            act.wait_ge(g_mm, 6 + units(B_MEM + j) + 1)
            dst = mkT[:, j, :] if j < 4 else y[:, (j - 4) // 2, MEM * (j % 2):MEM * (j % 2) + MEM]
            act.activation(dst, psum[:, j % 3, 0:MEM], ACT.Copy).then_inc(g_ev, 1)
        for t in range(NT + 1):
            r = P if t < NT else NS
            act.wait_ge(mt, t + 1)
            act.activation(ba[0:r, t, :], psum[0:r, 5 + t % 2, 0:8], ACT.Copy).then_inc(mc, 1)
        for s in range(2):
            for v in range(2):
                j = 2 * s + v
                act.wait_ge(mt, NT + 1 + j + 1)
                act.activation(mout[:, s, :] if v == 0 else mv[:, s, :], psum[:, 5 + j % 2, :], ACT.Copy).then_inc(mc, 1)
        for c in range(3):
            act.sem_inc(gs_st[c], 16)
        act.sem_inc(a_st[0], 16)
        act.sem_inc(a_st[1], 16)
        act.sem_inc(a_pt, 1)
        act.wait_ge(mc, NT + 1 + 4)
        act.wait_ge(o_st, 64)
        act.wait_ge(p_in, 64)
        act.activation(par[:, Q_BETA], ba[:, :, 0:4], ACT.Sigmoid).then_inc(pa, 1)
        act.wait_ge(pp, 2)
        act.activation(tmp[:, 2], tmp[:, 1], ACT.Exp, scale=-1.0).then_inc(pa, 1)
        act.wait_ge(pp, 3)
        act.activation(tmp[:, 4], tmp[:, 3], ACT.Ln).then_inc(pa, 1)
        act.activation(hp[:, 0, :], hp[:, 0, :], ACT.Exp).then_inc(pa, 1)
        act.wait_ge(pg, 1)
        act.wait_ge(st0, 1)
        for j, dst in enumerate((par[:, Q_EG], tmp[:, 2], egl[:])):
            if j == 1:
                act.wait_ge(pp, 6)
            act.activation(dst[:, 0:NT, :], psum[:, 5, 36 * j:36 * j + 32].rearrange("p (t h) -> p t h", h=BH), ACT.Exp).then_inc(pa, 1)
            act.activation(dst[0:NS, NT, :], psum[0:NS, 5, 36 * j + 32:36 * j + 36], ACT.Exp).then_inc(pa, 1)
        act.wait_ge(pp, 11)
        act.activation(rr[:, 1], rr[:, 0], ACT.Sqrt).then_inc(pa, 1)
        act.wait_ge(k_in, 16)
        act.activation(idb[:], ident, ACT.Copy).then_inc(st0, 1)
        act.activation(snk[:, 1, :], snk[:, 0, :], ACT.Copy, scale=-1.0).then_inc(st0, 1)

        def act_tile(i, b):
            t = 2 * i + b

            def copy(waits, dst, src, done):
                act.wait_ge(*waits)
                act.activation(dst, src, ACT.Copy).then_inc(done, 1)

            for step in TILE:
                if step == "DEC":
                    act.wait_ge(e_gt, t + 1)
                    act.wait_ge(dm_ok, t + 1)
                    act.activation(dec[:].rearrange("p h i -> p (h i)"), psum[:, 7, :], ACT.Exp).then_inc(dec_ok, 1)
                elif step == "INV":
                    copy((e_x0, t + 1), xx[:].rearrange("p h i -> p (h i)"), psum[:, 5, :], c_x)
                elif step == "UW":
                    copy((e_u, t + 1), uu[:].rearrange("p h i -> p (h i)"), psum[:, 6, :], c_u)
                    copy((e_w, t + 1), wt[:].rearrange("p h i -> p (h i)"), psum[:, 5, :], c_w)
                elif step == "SO":
                    act.wait_ge(c_o, t + 2)
                    for h in range(BH):
                        mm = act.activation(dec[:, h, :], oo[:, h, :], ACT.Square, accum_out=osm[:, 0, h:h + 1])
                    mm.then_inc(o_sq, 1)
                elif step == "N1":
                    act.wait_ge(o_st1, 5 * t + 3)
                    act.activation(osm[:, 2, :], osm[:, 1, :], ACT.Sqrt).then_inc(o_rt, 1)
                elif step[0] == "Y":
                    copy((e_y, 6 * t + step[1]), yy[:].rearrange("p h i -> p (h i)"), psum[:, 6, :], c_y)
                elif step[0] == "G":
                    j, c = divmod(step[1], 3)
                    act.wait_ge(gs_st[c], 16 * (3 * t + j) + 16)
                    copy((g_mm, 6 + UC + 9 * t + step[1] + 1), gst[:, c], psum[:, c, 0:CH], g_ev)
                elif step[0] == "S":
                    j = step[1]
                    if j == 0:
                        copy((a_vt, t + 1), vtok[:].rearrange("p a d -> p (a d)"), psum[:, 4, 0:2 * P], a_vc)
                    act.wait_ge(a_nm, 6 * t + j + 1)
                    for a in range(2):
                        mm = act.activation(pr[:, a, :], psum[:, 3, 256 * a:256 * a + 256], ACT.Exp, scale=A_SC[j],
                                            bias=asm[:, S_NM, 2 * j + a:2 * j + a + 1],
                                            accum_out=asm[:, S_SM, 2 * j + a:2 * j + a + 1])
                    mm.then_inc(a_e, 1)
                elif step[0] == "T":
                    copy((a_t, 8 * t + QI[step[1]] + 1), pt[:].rearrange("p a d -> p (a d)"), psum[:, 4, :], a_pt)
                elif step[0] == "F":
                    f = step[1]
                    if f == 0:
                        act.wait_ge(a_sk, 4 * t + 4)
                        act.activation(asm[:, S_ES, 0:8], asm[:, S_SK, 0:8], ACT.Exp).then_inc(a_es, 1)
                    act.wait_ge(a_st[f], 16 * t + 16)
                    copy((a_t, 8 * t + (5, 8)[f]), oba[:, f].rearrange("p a d -> p (a d)"), psum[:, 4, :], a_pt)
                    act.wait_ge(a_pt, 8 * t + (5, 8)[f] + 1)
                    act.dma_start(s_br[8 * f:8 * f + 4].rearrange("n p t -> p n t")[:, :, bass.ds(P * t, P)],
                                  oba[:, f]).then_inc(a_st[f], 16)

        with act.Fori(0, 4) as i:
            for b in range(2):
                act_tile(i, b)
        Dn = NS
        act.sem_inc(m_ka, 2)

        def fdone(op, name):
            op.then_inc(f_ac, 1)

        def copy_e(name, dst, src, after):
            act.wait_ge(f_pe, PEn(after))
            fdone(act.activation(dst, src, ACT.Copy), name)

        flat = lambda ap: ap.rearrange("p h i -> p (h i)")
        copy_e("kv_out", kvo[:, 0].rearrange("p v d -> p (v d)"), psum[:, 5, 0:256], "out")
        copy_e("new_out", kvo[0:Dn, 1].rearrange("p v d -> p (v d)"), psum[0:Dn, 5, 256:512], "out")
        copy_e("tail_out", tlo[:], psum[0:3 + NS, 0:3, :].rearrange("p b n -> p (b n)"), "out")
        act.wait_ge(f_pe, PEn("bcast"))
        fdone(act.activation(flat(ddc[:]), psum[0:Dn, 2, 0:P], ACT.Exp), "dec")
        fdone(act.activation(flat(dnm[:]), psum[:, 2, 3 * P:4 * P], ACT.Copy), "rq")
        act.wait_ge(f_pe, PEn("win_kt"))
        fdone(act.activation(wkT[:].rearrange("p b s -> p (b s)"), psum[:, 6:8, :].rearrange("p b n -> p (b n)"), ACT.Copy), "wkT")
        with act.Fori(0, DB // 2) as i:
            for s in range(2):
                act.wait_ge(m_kt, 2 * i + s + 3)
                act.wait_ge(m_sc, 2 * i + s + 1)
                act.activation(ckT[:, s, 0:2, :].rearrange("p h k -> p (h k)"), psum[:, 2 * s, :], ACT.Copy).then_inc(m_ka, 1)
        act.wait_ge(m_sc, 2 + DB)
        fdone(act.activation(flat(mS[:]), psum[:, 4, 0:256], ACT.Copy), "mem_s")
        act.wait_ge(f_dv, DVn("mem_nm"))
        fdone(act.activation(mR[:], psum[:, 5, 0:256], ACT.Exp, scale=P ** -0.5, bias=dsm[:, 1:2], accum_out=dsm[:, 2:3]), "mem_exp")
        copy_e("x0", flat(dxx[:]), psum[0:Dn, 0, 0:P], "x0")
        act.wait_ge(f_pe, PEn("new_sc"))
        act.activation(sS[:, 0:2, :], psum[:, 6:8, 0:P], ACT.Copy)
        fdone(act.activation(sS[0:Dn, 2:4, :], psum[0:Dn, 6:8, 256:256 + P], ACT.Copy), "win_s")
        copy_e("y", flat(dyy[:]), psum[0:Dn, 0, P:2 * P], "y")
        copy_e("mem_p", flat(mS[:]), psum[:, 5, 0:256], "mem_pt")
        act.wait_ge(f_dv, DVn("win_nm"))
        for v in range(2):
            mm = act.activation(sR[:, v, :], sR[:, v, :], ACT.Exp, scale=AHD ** -0.5, bias=dsm[:, 6 + v:7 + v], accum_out=dsm[:, 8 + v:9 + v])
        fdone(mm, "win_exp")
        act.wait_ge(f_dv, DVn("win_sk"))
        fdone(act.activation(dsm[:, 12:14], dsm[:, 10:12], ACT.Exp), "win_sk")
        act.wait_ge(f_pe, PEn("win_pt"))
        act.activation(flat(sS[:, 0:2, :]), psum[:, 6, 0:256], ACT.Copy)
        fdone(act.activation(flat(sS[0:Dn, 2:4, :]), psum[0:Dn, 6, 256:512], ACT.Copy), "win_p")
        copy_e("vn", flat(dvn[:]), psum[0:Dn, 0, :], "vn")
        act.wait_ge(f_dv, DVn("o_"))
        fdone(act.activation(dsq[:], dqe[:], ACT.Square), "sq")
        act.wait_ge(f_dv, DVn("n2"))
        fdone(act.activation(dsq[:], duT[:], ACT.Sqrt), "root")
        for j in range(12):
            if j in (0, 2, 5):
                r = (0, 2, 5).index(j)
                act.wait_ge(b_in, 16 * r + 16)
                if r == 2:
                    act.wait_ge(g_mm, 6 + UD + 24)
                act.activation(actD[:, 0, 4 * (r % 2):4 * (r % 2) + 4, :], brw[:], ACT.Copy).then_inc(b_hi, 1)
            act.wait_ge(q_in[j % 2], 16 * (j // 2) + 16)
            act.activation(gat[:, j % 2], gat[:, j % 2], ACT.Sigmoid).then_inc(q_sg, 1)
        for m in range(8):
            act.wait_ge(q_mx, 12 + 48 + 3 * m + 3)
            if m == 4:
                act.wait_ge(g_mm, 6 + UO)
            act.activation(actD[:, 0, (m + 4) % 8, :], accT[:, m, :], ACT.Copy).then_inc(b_hi, 1)
        for m in range(8):
            if m == 0:
                act.wait_ge(b_lo, 12)
            for c in range(3):
                act.wait_ge(g_mm, 6 + UO + 3 * m + c + 1)
                act.activation(accT[:, m, CH * c:CH * c + CH], psum[:, c, 0:CH], ACT.Copy).then_inc(g_ev, 1)

        def rows_psum(slot, rows):
            return psum[0:rows, 2 * slot:2 * slot + 2, :].rearrange("p b n -> p (b n)")

        def norm1(t, slot, rows):
            act.wait_ge(t_tr, t + 1)
            act.activation(jk[0:rows, slot, :], rows_psum(slot, rows), ACT.Square, accum_out=ns[0:rows, slot, 0, 0:1]).then_inc(t_sq, 1)

        def root1(t, slot, rows):
            act.wait_ge(t_ms, t + 1)
            act.activation(ns[0:rows, slot, 0, 2:3], ns[0:rows, slot, 0, 1:2], ACT.Sqrt).then_inc(t_rt, 1)

        def norm2(t, slot, rows):
            act.wait_ge(t_x1, t + 1)
            act.activation(jk[0:rows, slot, :], xr[0:rows, slot, :], ACT.Square, accum_out=ns[0:rows, slot, 1, 0:1]).then_inc(u_sq, 1)

        def root2(t, slot, rows):
            act.wait_ge(u_ms, t + 1)
            act.activation(ns[0:rows, slot, 1, 2:3], ns[0:rows, slot, 1, 1:2], ACT.Sqrt).then_inc(u_rt, 1)

        def hi_back(t, slot, rows, col):
            act.wait_ge(u_tr, t + 1)
            act.activation(actD[:, 0, :, bass.ds(col, rows)],
                           psum[:, 4 + 2 * slot:6 + 2 * slot, :].rearrange("p b (k t) -> p (b k) t", t=P)[:, :, 0:rows], ACT.Copy).then_inc(u_hi, 1)

        def pair_norms(t, tiles):
            for f in (norm1, root1, norm2, root2):
                for o, slot, rows, _ in tiles:
                    f(t + o, slot, rows)
            for o, slot, rows, col in tiles:
                hi_back(t + o, slot, rows, col)

        act.wait_ge(b_in, 96)
        with act.Fori(0, NT // 2) as i:
            pair_norms(2 * i, [(b, b, P, 2 * P * i + P * b) for b in range(2)])
        pair_norms(NT, [(0, 0, NS, SEQ)])

        def gt_panel(u, i):
            for c in range(3):
                act.wait_ge(g_mm, 6 + UF + u + c + 1)
                if c == 0:
                    act.wait_ge(f_fr, 3 * i + 3)
                act.activation(sg[:, CH * c:CH * c + CH], psum[:, c, 0:CH], ACT.Silu).then_inc(g_ev, 1)

        act.sem_inc(f_hi, 3)

        def hi_f(i, fs):
            act.wait_ge(o_mm, 24 * i + 24)
            for c in range(3):
                act.wait_ge(f_fr, 3 + 3 * i + c + 1)
                act.activation(fT[:, fs, 0, CH * c:CH * c + CH], fr[:, CH * c:CH * c + CH], ACT.Copy).then_inc(f_hi, 1)

        with act.Fori(0, NF // 2) as i:
            for b in range(2):
                gt_panel(12 * i + 6 * b, 2 * i + b)
                hi_f(2 * i + b, b)
        with act.Fori(0, NT // 2) as i:
            for f in (norm1, root1):
                for b in range(2):
                    f(9 + 2 * i + b, b, P)
        norm1(9 + NT, 0, NS)
        root1(9 + NT, 0, NS)

    @block.vector
    def _(dve):
        dve.sem_inc(x_lo, 2)
        dve.sem_inc(cv_st, 16)
        dve.wait_ge(k_in, 16 * 6)

        def norm(n, slot, rows, gain):
            dve.wait_ge(x_sq, n + 1)
            dve.tensor_scalar(rs[0:rows, slot, 1:2], rs[0:rows, slot, 0:1], 1.0 / D, EPS, ALU.mult, ALU.add).then_inc(x_rs, 1)
            dve.wait_ge(x_rt, n + 1)
            dve.reciprocal(rs[0:rows, slot, 3:4], rs[0:rows, slot, 2:3]).then_inc(x_rs, 1)
            dve.wait_ge(x_rs, 2 * n + 2)
            dve.scalar_tensor_tensor(out=xs[0:rows, slot, :], in0=xin[0:rows, slot, :], scalar=rs[0:rows, slot, 3:4],
                                     in1=gbc[0:rows, gain, :], op0=ALU.mult, op1=ALU.mult).then_inc(x_nm, 1)

        def lo_x(n, slot, rows, dst, col):
            dve.wait_ge(x_hi, n + 1)
            src = psum[:, 2 * slot:2 * slot + 2, :].rearrange("p b (k t) -> p (b k) t", t=P)[:, :, 0:rows]
            dve.tensor_tensor(dst[:, 1, :, bass.ds(col, rows)], src, dst[:, 0, :, bass.ds(col, rows)].bitcast(F32),
                              ALU.subtract).then_inc(x_lo, 1)

        with dve.Fori(0, NT // 2) as i:
            for b in range(2):
                norm(2 * i + b, b, P, 0)
            for b in range(2):
                lo_x(2 * i + b, b, P, actT, 2 * P * i + P * b)
        for n, rows, _, gain, dst, col in rest_tiles:
            norm(n, n % 2, rows, gain)
            lo_x(n, n % 2, rows, dst, col)

        def conv(n, slot):
            dve.wait_ge(cv_in, n + 1)
            dve.wait_ge(y_a, n + 1)
            dst = (y[:, slot, 0:SEQ], by_step(y[:, slot, SEQ:N]))
            for tap in range(CW):
                src = (cv[:, slot, tap:tap + SEQ], by_step(cv[:, slot, 3 + SEQ:])[:, :, tap:tap + DS])
                w = scT[:, bass.ds(n, 1), 24 + tap]
                for part in range(2):
                    if tap == 0:
                        op = dve.tensor_scalar(dst[part], src[part], w, None, ALU.mult)
                    else:
                        dve.wait_ge(cv_st, 16 + 8 * n + 2 * tap + part - 1)
                        op = dve.scalar_tensor_tensor(out=dst[part], in0=src[part], scalar=w, in1=dst[part],
                                                      op0=ALU.mult, op1=ALU.add)
                    op.then_inc(cv_st, 1)

        with dve.Fori(0, 6) as i:
            for b in range(2):
                conv(2 * i + b, b)
        for n in range(B_Z, B_C):
            dve.wait_ge(g_ev, 3 + 3 * n + 3)
            dve.wait_ge(y_st[n % 2], 16 * (n // 2) + 16)
            dve.tensor_scalar(y2[:, n % 2, :], y[:, n % 2, :], nw[:, 0:1], None, ALU.mult).then_inc(y_d, 1)
        dve.wait_ge(k_in, 16 * 7)
        for n in range(B_A, B_VA):
            dve.wait_ge(g_ev, 3 + 3 * n + 3)
            dve.wait_ge(y_st[n % 2], 16 * (n // 2) + 16)
            dve.tensor_tensor(y2[:, n % 2, :], y[:, n % 2, :], rope[:, 0, :], ALU.mult).then_inc(y_d, 1)
            dve.tensor_tensor(cv[:, n % 2, 0:N], cv[:, n % 2, 0:N], rope[:, 1, :], ALU.mult).then_inc(y_d, 1)
            dve.wait_ge(y_d, YD(n) - 1)
            dve.tensor_tensor(y2[:, n % 2, :], y2[:, n % 2, :], cv[:, n % 2, 0:N], ALU.add).then_inc(y_d, 1)
        dve.sem_inc(kq_ok, 1)
        dve.sem_inc(al_ok, 1)
        dve.sem_inc(c_o, 1)
        dve.sem_inc(c_s, 1)
        dve.sem_inc(av_ok, 1)
        dve.sem_inc(ob_st, 16)

        class Chain:
            n = 0

        def pstep(op):
            Chain.n += 1
            op.then_inc(pp, 1)
            dve.wait_ge(pp, Chain.n)

        allp = [P, NT + 1, BH]
        dve.wait_ge(mc, NT + 1 + 4)
        dve.wait_ge(o_st, 64)
        dve.wait_ge(p_in, 64)
        dve.memset(par[:, Q_EG], 0.0).then_inc(st0, 1)
        pstep(dve.tensor_tensor(tmp[:, 0], ba[:, :, 4:8], hp[:, 1, :].unsqueeze(1).to_broadcast(allp), ALU.add))
        pstep(dve.scalar_tensor_tensor(out=tmp[:, 1], in0=tmp[:, 0], scalar=-1.0, in1=tmp[:, 0], op0=ALU.mult, op1=ALU.max))
        dve.wait_ge(pa, 2)
        pstep(dve.tensor_scalar(tmp[:, 3], tmp[:, 2], 1.0, None, ALU.add))
        pstep(dve.reciprocal(tmp[:, 5], tmp[:, 3]))
        pstep(dve.tensor_scalar(tmp[:, 1], tmp[:, 3], 1.0, None, ALU.subtract))
        pstep(dve.tensor_tensor(tmp[:, 1], tmp[:, 2], tmp[:, 1], ALU.subtract))
        pstep(dve.tensor_tensor(tmp[:, 1], tmp[:, 1], tmp[:, 5], ALU.mult))
        dve.wait_ge(pa, 4)
        pstep(dve.tensor_tensor(tmp[:, 1], tmp[:, 1], tmp[:, 4], ALU.add))
        pstep(dve.scalar_tensor_tensor(out=tmp[:, 0], in0=tmp[:, 0], scalar=0.0, in1=tmp[:, 1], op0=ALU.max, op1=ALU.add))
        pstep(dve.scalar_tensor_tensor(out=par[:, Q_G], in0=tmp[:, 0], scalar=-1.0,
                                       in1=hp[:, 0, :].unsqueeze(1).to_broadcast(allp), op0=ALU.mult, op1=ALU.mult))
        dve.wait_ge(ssq_ok, 1)
        pstep(dve.tensor_scalar(rr[:, 0], ssq[:], EPS, None, ALU.add))
        dve.wait_ge(pa, 11)
        pstep(dve.reciprocal(rr[:, 0], rr[:, 1]))
        pstep(dve.tensor_copy(par[:, Q_RK], rr[:, 0, 4:8, :].rearrange("p h t -> p t h")))
        pstep(dve.tensor_scalar(par[:, Q_RQ], rr[:, 0, 0:4, :].rearrange("p h t -> p t h"), P ** -0.5, None, ALU.mult))
        pstep(dve.tensor_tensor(par[:, Q_BK], par[:, Q_BETA], par[:, Q_RK], ALU.mult))
        pstep(dve.tensor_tensor(par[:, Q_BKE], par[:, Q_BK], par[:, Q_EG], ALU.mult))
        pstep(dve.tensor_tensor(par[:, Q_KD], tmp[:, 2], par[:, Q_RK], ALU.mult))
        dve.wait_ge(st0, 3)

        def head4(bank):
            return psum[:, bank, :].rearrange("p (h i) -> p h i", h=BH)

        def dve_tile(i, b):
            t = 2 * i + b
            for step in TILE:
                if step == "KV":
                    dve.wait_ge(e_tk, t + 1)
                    dve.tensor_tensor(kbe[:], head4(5), bc_c(per(Q_BKE, t)), ALU.mult)
                    dve.tensor_tensor(kd[:], head4(5), bc_c(per(Q_KD, t)), ALU.mult).then_inc(kd_ok, 1)
                    dve.wait_ge(e_tv, t + 1)
                    dve.tensor_tensor(vb[:], head4(6), bc_c(per(Q_BETA, t)), ALU.mult).then_inc(vb_ok, 1)
                elif step == "DEC":
                    dve.wait_ge(dec_ok, t + 1)
                    dve.wait_ge(mrk_ok, t + 1)
                    dve.wait_ge(kq_ok, t + 1)
                    dve.tensor_tensor(decm[:], dec[:], mrk[:], ALU.mult).then_inc(dm_ok, 1)
                elif step == "KK":
                    dve.wait_ge(dm_ok, t + 2)
                    dve.wait_ge(al_ok, 6 * t + 1)
                    dve.wait_ge(e_kk, t + 1)
                    dve.tensor_tensor(at[:], head4(6), decm[:], ALU.mult).then_inc(at_st, 1)
                    dve.wait_ge(e_br, t + 1)
                    dve.wait_ge(at_st, 4 * t + 1)
                    dve.tensor_tensor(at[:], at[:], head4(5), ALU.mult).then_inc(at_st, 1)
                    dve.wait_ge(e_kq, t + 1)
                    dve.tensor_tensor(kqd[:], head4(7), decm[:], ALU.mult).then_inc(kq_ok, 1)
                    dve.wait_ge(at_st, 4 * t + 2)
                    for l in range(NLV):
                        m = bc_h(kc[:, K_LV + P * l:K_LV + P * l + P])
                        if l == 0:
                            dve.tensor_tensor(xt[:], at[:], m, ALU.mult).then_inc(at_st, 1)
                            dve.wait_ge(at_st, 4 * t + 3)
                            dve.tensor_tensor(xt[:], bc_h(ident), xt[:], ALU.subtract).then_inc(at_st, 1)
                        else:
                            dve.tensor_tensor(atl[:, l], at[:], m, ALU.mult).then_inc(al_ok, 1)
                elif step == "PO":
                    dve.wait_ge(c_u, t + 1)
                    dve.wait_ge(e_p1, t + 1)
                    dve.tensor_tensor(vn[:], uu[:], head4(7), ALU.subtract).then_inc(vn_ok, 1)
                    dve.wait_ge(e_o1, t + 1)
                    dve.wait_ge(c_o, t + 1)
                    dve.tensor_tensor(o1s[:], head4(5), bc_c(per(Q_EG, t)), ALU.mult).then_inc(c_o1, 1)
                    dve.wait_ge(c_s, t + 1)
                    dve.tensor_tensor(st[:], st[:], bc_c(egl[:, bass.ds(t, 1), :]), ALU.mult).then_inc(c_sm, 1)
                elif step == "SO":
                    dve.wait_ge(e_sp, t + 1)
                    dve.wait_ge(c_sm, t + 1)
                    dve.tensor_tensor(st[:], st[:], head4(7), ALU.add).then_inc(c_s, 1)
                    dve.wait_ge(e_o2, t + 1)
                    dve.wait_ge(c_o1, t + 1)
                    dve.tensor_tensor(oo[:], o1s[:], head4(6), ALU.add).then_inc(c_o, 1)
                elif step == "N1":
                    dve.wait_ge(o_sq, t + 1)
                    rq = per(Q_RQ, t).rearrange("p a h -> p (a h)")
                    dve.tensor_tensor(osm[:, 1, :], osm[:, 0, :], rq, ALU.mult).then_inc(o_st1, 1)
                    dve.wait_ge(o_st1, 5 * t + 1)
                    dve.tensor_tensor(osm[:, 1, :], osm[:, 1, :], rq, ALU.mult).then_inc(o_st1, 1)
                    dve.wait_ge(o_st1, 5 * t + 2)
                    dve.tensor_scalar(osm[:, 1, :], osm[:, 1, :], 1.0 / P, EPS, ALU.mult, ALU.add).then_inc(o_st1, 1)
                elif step == "N2":
                    dve.wait_ge(o_rt, t + 1)
                    rq = per(Q_RQ, t).rearrange("p a h -> p (a h)")
                    dve.reciprocal(osm[:, 3, :], osm[:, 2, :]).then_inc(o_st1, 1)
                    dve.wait_ge(o_st1, 5 * t + 4)
                    dve.tensor_tensor(osm[:, 4, :], osm[:, 3, :], rq, ALU.mult).then_inc(o_st1, 1)
                    dve.wait_ge(o_st1, 5 * t + 5)
                    dve.tensor_tensor(oo[:], oo[:], osm[:, 4, :].unsqueeze(2).to_broadcast([P, BH, P]), ALU.mult).then_inc(on_ok, 1)
                elif step == "OT":
                    dve.wait_ge(e_ot, t + 1)
                    dve.wait_ge(l_in["z"][b], 16 * i + 16)
                    dve.wait_ge(ob_st, 16 * t + 16)
                    dve.tensor_tensor(obb[:], head4(5), gin[:, b, 12:16, :], ALU.mult).then_inc(c_ob, 1)
                elif step[0] == "X":
                    l = step[1]
                    if l < 6:
                        dve.wait_ge(e_xx, 5 * t + l)
                        dve.tensor_tensor(xx[:], xx[:], head4(5), ALU.subtract).then_inc(c_x, 1)
                    dve.wait_ge(e_xt, 6 * t + l)
                    dve.tensor_tensor(xt[:], xt[:], head4(7), ALU.subtract).then_inc(c_xt, 1)
                elif step[0] == "S":
                    j = step[1]
                    cols = slice(2 * j, 2 * j + 2)
                    dve.wait_ge(a_s, 6 * t + j + 1)
                    dve.tensor_reduce(asm[:, S_MX, cols], psum[:, 3, :].rearrange("p (a k) -> p a k", a=2), AX.X, ALU.max).then_inc(a_mx, 1)
                    dve.wait_ge(a_mx, 6 * t + j + 1)
                    if j < 4:
                        dve.scalar_tensor_tensor(out=asm[:, S_NM, cols], in0=asm[:, S_MX, cols], scalar=-A_SC[j],
                                                 in1=snk[:, 1, cols], op0=ALU.mult, op1=ALU.min).then_inc(a_nm, 1)
                        dve.wait_ge(a_nm, 6 * t + j + 1)
                        dve.tensor_tensor(asm[:, S_SK, cols], asm[:, S_NM, cols], snk[:, 0, cols], ALU.add).then_inc(a_sk, 1)
                    else:
                        dve.tensor_scalar(asm[:, S_NM, cols], asm[:, S_MX, cols], -A_SC[j], None, ALU.mult).then_inc(a_nm, 1)
                elif step[0] == "V":
                    j = step[1]
                    dve.wait_ge(a_v, 6 * t + j + 1)
                    if j < 4:
                        dst = oat[:, 0, :].rearrange("p (g v d) -> p g v d", g=4, v=2)[:, 2 * (j % 2):2 * (j % 2) + 2, j // 2]
                        src = psum[:, 3, 0:P].rearrange("p (g d) -> p g d", g=2)
                    else:
                        dst, src = oat[:, 1, 256 * (j - 4):256 * (j - 4) + 256], psum[:, 3, 0:2 * P]
                    dve.tensor_copy(dst, src).then_inc(av_ok, 1)
                elif step[0] == "F":
                    f = step[1]
                    cols, heads, w = ((slice(0, 8), 8, AHD), (slice(8, 12), 4, P))[f]
                    if f == 0:
                        dve.wait_ge(a_es, t + 1)
                        dve.tensor_tensor(asm[:, S_DEN, cols], asm[:, S_SM, cols], asm[:, S_ES, cols], ALU.add).then_inc(a_dn, 1)
                    else:
                        dve.tensor_copy(asm[:, S_DEN, cols], asm[:, S_SM, cols]).then_inc(a_dn, 1)
                    dve.wait_ge(a_dn, 4 * t + 2 * f + 1)
                    dve.reciprocal(asm[:, S_RD, cols], asm[:, S_DEN, cols]).then_inc(a_dn, 1)
                    dve.wait_ge(a_dn, 4 * t + 2 * f + 2)
                    dve.wait_ge(av_ok, 6 * t + (5, 7)[f])
                    if f == 0:
                        o = oat[:, 0, :].rearrange("p (g v d) -> p g v d", g=4, v=2)
                        rd = asm[:, S_RD, cols].rearrange("p (v g) -> p g v", v=2).unsqueeze(3).to_broadcast([P, 4, 2, w])
                    else:
                        o = oat[:, 1, :].rearrange("p (h d) -> p h d", d=w)
                        rd = asm[:, S_RD, cols].unsqueeze(2).to_broadcast([P, heads, w])
                    dve.tensor_tensor(o, o, rd, ALU.mult).then_inc(a_on, 1)

        with dve.Fori(0, 4) as i:
            for b in range(2):
                dve_tile(i, b)
        Dn = NS
        dve.sem_inc(m_kd, 2)
        dve.wait_ge(f_in, F_IN)

        def f(name, op):
            op.then_inc(f_dv, 1)

        own = lambda name: dve.wait_ge(f_dv, DVn(name))
        dP = lambda q: par[0:Dn, q, NT, :].unsqueeze(2).to_broadcast([Dn, BH, NS])
        dW = lambda q: par[0:Dn, q, NT, :].unsqueeze(2).to_broadcast([Dn, BH, P])
        bD = lambda ap: ap.unsqueeze(1).to_broadcast([Dn, BH, NS])
        q4 = lambda bank, j, rows=Dn: psum[0:rows, bank, P * j:P * j + P].rearrange("p (h i) -> p h i", h=BH)
        le, idd = bD(kc[0:Dn, K_D_LE:K_D_LE + NS]), bD(ident[0:Dn, 0:Dn])
        f("ug", dve.tensor_tensor(dug[:], le, dP(Q_G), ALU.mult))
        f("d0", dve.tensor_tensor(dia[:, 0], idd, dP(Q_BK), ALU.mult))
        f("d1", dve.tensor_tensor(dia[:, 1], idd, dP(Q_EG), ALU.mult))
        f("d2", dve.tensor_tensor(dia[:, 2], idd, dP(Q_RQ), ALU.mult))
        f("d3", dve.tensor_tensor(dia[:, 3], idd, egl[0:Dn, NT, :].unsqueeze(2).to_broadcast([Dn, BH, NS]), ALU.mult))
        f("mr", dve.tensor_tensor(dmr[:], le, dP(Q_RK), ALU.mult))
        dve.wait_ge(f_pe, PEn("bcast"))
        f("kb", dve.tensor_tensor(dkb[:], psum[0:Dn, 0, :].rearrange("p (h i) -> p h i", h=BH), dW(Q_BKE), ALU.mult))
        f("kd", dve.tensor_tensor(dkd[:], psum[0:Dn, 0, :].rearrange("p (h i) -> p h i", h=BH), dW(Q_KD), ALU.mult))
        f("vb", dve.tensor_tensor(dvb[:], psum[0:Dn, 1, :].rearrange("p (h i) -> p h i", h=BH), dW(Q_BETA), ALU.mult))
        dve.wait_ge(f_ac, ACn("rq"))
        own("mr")
        f("dcm", dve.tensor_tensor(ddc[:], ddc[:], dmr[:], ALU.mult))
        own("dcm")
        f("at0", dve.tensor_tensor(dat[:], q4(3, 1), ddc[:], ALU.mult))
        own("at0")
        f("at", dve.tensor_tensor(dat[:], dat[:], q4(2, 1), ALU.mult))
        f("kq", dve.tensor_tensor(dkq[:], q4(3, 2), ddc[:], ALU.mult))
        own("at")
        f("x_", dve.tensor_tensor(dxt[:], dat[:], bD(kc[0:Dn, K_LV:K_LV + NS]), ALU.mult))
        own("x_")
        f("xt0", dve.tensor_tensor(dxt[:], idd, dxt[:], ALU.subtract))
        f("at1", dve.tensor_tensor(dat1[:], dat[:], bD(kc[0:Dn, K_LV + P:K_LV + P + NS]), ALU.mult))
        f("eg", dve.tensor_copy(deg[:], q4(2, 2, P)))
        f("el", dve.tensor_copy(del_[:], q4(3, 0, P)))
        with dve.Fori(0, DB // 2) as i:
            for s in range(2):
                dve.wait_ge(m_kt, 2 * i + s + 3)
                dve.wait_ge(m_sc, 2 * i + s + 1)
                dve.tensor_copy(ckT[:, s, 2:4, :].rearrange("p h k -> p (h k)"), psum[:, 2 * s + 1, :]).then_inc(m_kd, 1)
        dve.wait_ge(f_pe, PEn("mem_rows"))
        f("mem_mx", dve.tensor_reduce(dsm[:, 0:1], psum[:, 5, 0:256], AX.X, ALU.max))
        own("mem_mx")
        f("mem_nm", dve.tensor_scalar(dsm[:, 1:2], dsm[:, 0:1], -P ** -0.5, None, ALU.mult))
        dve.wait_ge(f_ac, ACn("mem_exp"))
        f("mem_rd", dve.reciprocal(dsm[:, 3:4], dsm[:, 2:3]))
        own("mem_rd")
        f("mem_n", dve.tensor_scalar(mR[:], mR[:], dsm[:, 3:4], None, ALU.mult))
        dve.wait_ge(f_pe, PEn("xt"))
        f("xt", dve.tensor_tensor(dxt[:], dxt[:], q4(0, 2), ALU.subtract))
        dve.wait_ge(f_pe, PEn("win_rows"))
        for v in range(2):
            f(f"win_m{v}", dve.tensor_tensor(sR[:, v, :], psum[:, 7, 160 * v:160 * v + 160], dmk[:], ALU.add))
        own("win_m1")
        f("win_mx", dve.tensor_reduce(dsm[:, 4:6], sR[:], AX.X, ALU.max))
        own("win_mx")
        f("win_nx", dve.scalar_tensor_tensor(out=dsm[:, 4:6], in0=dsm[:, 4:6], scalar=AHD ** -0.5, in1=sks[:], op0=ALU.mult, op1=ALU.max))
        own("win_nx")
        f("win_nm", dve.tensor_scalar(dsm[:, 6:8], dsm[:, 4:6], -1.0, None, ALU.mult))
        own("win_nm")
        f("win_sk", dve.tensor_tensor(dsm[:, 10:12], sks[:], dsm[:, 6:8], ALU.add))
        dve.wait_ge(f_pe, PEn("u_w"))
        f("uT", dve.tensor_copy(duT[:], q4(1, 0, P)))
        for h in range(BH):
            dve.tensor_copy(wq[:, h, :, 1, :], by_step(dq[:, h, :]))
        for h in range(BH):
            op = dve.tensor_copy(wq[:, h, :, 0, :], by_step(psum[:, 1, P + NS * h:P + NS * h + NS]))
        f("wT", op)
        dve.wait_ge(f_pe, PEn("mem_o"))
        f("mem_o", dve.tensor_copy(dob[:, 2], q4(5, 2, P)))
        dve.wait_ge(f_ac, ACn("win_sk"))
        f("win_dn", dve.tensor_tensor(dsm[:, 14:16], dsm[:, 8:10], dsm[:, 12:14], ALU.add))
        own("win_dn")
        f("win_rd", dve.reciprocal(dsm[:, 16:18], dsm[:, 14:16]))
        own("win_rd")
        f("win_n", dve.tensor_tensor(sR[:], sR[:], dsm[:, 16:18].unsqueeze(2).to_broadcast([P, 2, WIN + NS]), ALU.mult))
        dve.wait_ge(f_pe, PEn("w_q_s"))
        for h in range(BH):
            src = psum[:, 4, 64 * h:64 * h + 64].rearrange("p (b a s) -> p b a s", b=DB, a=2)
            op = dve.tensor_tensor(by_step(dvT[:, h, :]), by_step(duT[:, h, :]), src[:, :, 0, :], ALU.subtract)
        f("vT", op)
        for h in range(BH):
            src = psum[:, 4, 64 * h:64 * h + 64].rearrange("p (b a s) -> p b a s", b=DB, a=2)
            op = dve.tensor_tensor(by_step(dqe[:, h, :]), by_step(deg[:, h, :]), src[:, :, 1, :], ALU.mult)
        f("qe", op)
        dve.wait_ge(f_pe, PEn("win_o"))
        for v in range(2):
            rows = slice(64 * v, 64 * v + 64)
            f(f"win_c{v}", dve.tensor_copy(dob[rows, 0], psum[rows, 7, P * v:P * v + P].rearrange("p (g t) -> p g t", g=4)))
        own("win_c1")
        for v in range(2):
            rows = slice(64 * v, 64 * v + 64)
            f(f"win_o{v}", dve.tensor_tensor(dob[rows, 0], dob[rows, 0], psum[rows, 7, 256 + P * v:256 + P * v + P].rearrange("p (g t) -> p g t", g=4), ALU.add))
        dve.wait_ge(f_ac, ACn("vn"))
        blk = kc[0:Dn, K_D_BLK:K_D_BLK + NS].rearrange("p (b s) -> p b s", s=DS)[:, :, 0]

        def keep(half):
            return dve.tensor_tensor(vnm[:], dvn[:].unsqueeze(2).to_broadcast([Dn, 4, 4, P]),
                                     blk[:, 4 * half:4 * half + 4].unsqueeze(1).unsqueeze(3).to_broadcast([Dn, 4, 4, P]), ALU.mult)

        f("vm0", keep(0))
        dve.wait_ge(f_pe, PEn("o"))
        f("o_", dve.tensor_tensor(dqe[:], dqe[:], q4(1, 2, P), ALU.add))
        el4 = del_[:].rearrange("p h (b s) -> p b h s", s=DS)[:, :, :, 0].unsqueeze(3)
        f("s_e", dve.tensor_tensor(sd[:], sd[:], el4.to_broadcast([P, DB, BH, P]), ALU.mult))
        dve.wait_ge(f_pe, PEn("sumsq"))
        f("n0", dve.tensor_tensor(duT[:], q4(1, 3, P), dnm[:], ALU.mult))
        own("n0")
        f("n1", dve.tensor_tensor(duT[:], duT[:], dnm[:], ALU.mult))
        own("n1")
        f("n2", dve.tensor_scalar(duT[:], duT[:], 1.0 / P, EPS, ALU.mult, ALU.add))
        f("oq", dve.tensor_tensor(dqe[:], dqe[:], dnm[:], ALU.mult))
        own("oq")
        f("oz", dve.tensor_tensor(dqe[:], dqe[:], dq[:, 12:16, :], ALU.mult))
        dve.wait_ge(f_ac, ACn("root"))
        f("n3", dve.reciprocal(dvT[:], dsq[:]))
        own("n3")
        f("o_z", dve.tensor_tensor(dob[:, 1], dqe[:], dvT[:], ALU.mult))
        for j in range(8):
            half, h = divmod(j, 4)
            dve.wait_ge(g_up, j + 1)
            own("s_e")
            dve.tensor_tensor(sd[:, 4 * half:4 * half + 4, h, :], sd[:, 4 * half:4 * half + 4, h, :],
                              psum[:, (0, 3, 4)[j % 3], :].rearrange("p (b d) -> p b d", b=4), ALU.add).then_inc(g_ad, 1)
            if j == 3:
                f("vm1", keep(1))
        dve.sem_inc(q_mx, 12)
        dve.sem_inc(t_y, 2)
        dve.sem_inc(u_xs, 2)
        dve.sem_inc(u_lo, 2)
        dve.sem_inc(f_fr, 3)
        dve.sem_inc(f_lo, 3)
        dve.sem_inc(o_ad, 3)

        def lo_br(r):
            dve.wait_ge(b_hi, r + 1)
            dve.tensor_tensor(actD[:, 1, 4 * (r % 2):4 * (r % 2) + 4, :], brw[:],
                              actD[:, 0, 4 * (r % 2):4 * (r % 2) + 4, :].bitcast(F32), ALU.subtract).then_inc(b_lo, 1)

        lo_br(0)
        for j in range(12):
            r = j // 4
            if j in (2, 5):
                lo_br((1, 2)[j == 5])
            dve.wait_ge(q_sg, j + 1)
            for half in range(2):
                for c in range(3):
                    x = 6 * j + 3 * half + c
                    m = 2 * (j % 4) + half
                    cols = slice(CH * c, CH * c + CH)
                    dve.wait_ge(g_mm, 6 + UD + x + 1)
                    if r == 0:
                        dve.tensor_tensor(accT[:, m, cols], psum[:, c, 0:CH], gat[:, j % 2, half, cols], ALU.mult).then_inc(q_mx, 1)
                        dve.wait_ge(q_mx, 12 + x + 1)
                        dve.sem_inc(g_ev, 1)
                    else:
                        dve.wait_ge(q_mx, 12 + x - 1)
                        dve.tensor_tensor(prd[:, x % 2], psum[:, c, 0:CH], gat[:, j % 2, half, cols], ALU.mult).then_inc(g_ev, 1)
                        dve.wait_ge(g_ev, 3 + UD + x + 1)
                        dve.tensor_tensor(accT[:, m, cols], accT[:, m, cols], prd[:, x % 2], ALU.add).then_inc(q_mx, 1)
        for m in range(8):
            dve.wait_ge(b_hi, 3 + m + 1)
            dve.tensor_tensor(actD[:, 1, (m + 4) % 8, :], accT[:, m, :], actD[:, 0, (m + 4) % 8, :].bitcast(F32), ALU.subtract).then_inc(b_lo, 1)

        def mean1(t, slot, rows):
            dve.wait_ge(t_sq, t + 1)
            dve.tensor_scalar(ns[0:rows, slot, 0, 1:2], ns[0:rows, slot, 0, 0:1], 1.0 / D, EPS, ALU.mult, ALU.add).then_inc(t_ms, 1)

        def apply1(t, slot, rows, gain, landed):
            dve.wait_ge(t_rt, t + 1)
            dve.reciprocal(ns[0:rows, slot, 0, 3:4], ns[0:rows, slot, 0, 2:3]).then_inc(t_rd, 1)
            dve.wait_ge(t_rd, t + 1)
            dve.scalar_tensor_tensor(out=yr[0:rows, slot, :], in0=rows_v(slot, rows), scalar=ns[0:rows, slot, 0, 3:4],
                                     in1=gn[0:rows, gain, :], op0=ALU.mult, op1=ALU.mult).then_inc(t_y, 1)
            dve.wait_ge(t_y, 2 + t + 1)
            dve.wait_ge(r_in[slot], landed)
            dve.tensor_tensor(xr[0:rows, slot, :], xr[0:rows, slot, :], yr[0:rows, slot, :], ALU.add).then_inc(t_x1, 1)

        def rows_v(slot, rows):
            return psum[0:rows, 2 * slot:2 * slot + 2, :].rearrange("p b n -> p (b n)")

        def mean2(t, slot, rows):
            dve.wait_ge(u_sq, t + 1)
            dve.tensor_scalar(ns[0:rows, slot, 1, 1:2], ns[0:rows, slot, 1, 0:1], 1.0 / D, EPS, ALU.mult, ALU.add).then_inc(u_ms, 1)

        def apply2(t, slot, rows):
            dve.wait_ge(u_rt, t + 1)
            dve.reciprocal(ns[0:rows, slot, 1, 3:4], ns[0:rows, slot, 1, 2:3]).then_inc(u_rd, 1)
            dve.wait_ge(u_rd, t + 1)
            dve.scalar_tensor_tensor(out=yr[0:rows, slot, :], in0=xr[0:rows, slot, :], scalar=ns[0:rows, slot, 1, 3:4],
                                     in1=gn[0:rows, 1, :], op0=ALU.mult, op1=ALU.mult).then_inc(u_xs, 1)

        def lo_back(t, slot, rows, col):
            dve.wait_ge(u_hi, t + 1)
            src = psum[:, 4 + 2 * slot:6 + 2 * slot, :].rearrange("p b (k t) -> p (b k) t", t=P)[:, :, 0:rows]
            dve.tensor_tensor(actD[:, 1, :, bass.ds(col, rows)], src, actD[:, 0, :, bass.ds(col, rows)].bitcast(F32), ALU.subtract).then_inc(u_lo, 1)

        def pair_rows(t, tiles, landed):
            for o, slot, rows, _ in tiles:
                mean1(t + o, slot, rows)
            for o, slot, rows, _ in tiles:
                apply1(t + o, slot, rows, 0, landed)
            for o, slot, rows, _ in tiles:
                mean2(t + o, slot, rows)
            for o, slot, rows, _ in tiles:
                apply2(t + o, slot, rows)
            for o, slot, rows, col in tiles:
                lo_back(t + o, slot, rows, col)

        dve.wait_ge(b_in, 96)
        with dve.Fori(0, NT // 2) as i:
            pair_rows(2 * i, [(b, b, P, 2 * P * i + P * b) for b in range(2)], 16 * i + 16)
        pair_rows(NT, [(0, 0, NS, SEQ)], 16 * 5)
        dve.memset(accT[:], 0.0).then_inc(o_ad, 1)

        def uf_panel(i, fs):
            for c in range(3):
                cols = slice(CH * c, CH * c + CH)
                dve.wait_ge(g_ev, 3 + UF + 3 * i + c + 1)
                dve.wait_ge(g_mm, 6 + UF + 6 * i + 3 + c + 1)
                dve.wait_ge(f_hi, 3 * i + c + 1)
                dve.wait_ge(f_lo, 3 * i + c + 1)
                dve.tensor_tensor(fr[:, cols], psum[:, c, 0:CH], sg[:, cols], ALU.mult).then_inc(f_fr, 1)
            for c in range(3):
                cols = slice(CH * c, CH * c + CH)
                dve.wait_ge(f_hi, 3 + 3 * i + c + 1)
                dve.tensor_tensor(fT[:, fs, 1, cols], fr[:, cols], fT[:, fs, 0, cols].bitcast(F32), ALU.subtract).then_inc(f_lo, 1)

        def add_out(i):
            dve.wait_ge(o_ad, 24 * i + 4)
            for m in range(KT):
                for c in range(3):
                    x = 3 * m + c
                    cols = slice(CH * c, CH * c + CH)
                    dve.wait_ge(o_mm, 48 + 24 * i + x + 1)
                    dve.tensor_tensor(accT[:, m, cols], accT[:, m, cols], psum[:, 3 + x % 4, 0:CH], ALU.add).then_inc(o_ad, 1)

        uf_panel(0, 0)
        with dve.Fori(0, (NF - 2) // 2) as i:
            for b in (1, 2):
                uf_panel(2 * i + b, b % 2)
                add_out(2 * i + b - 1)
        uf_panel(NF - 1, 1)
        add_out(NF - 2)
        add_out(NF - 1)

        def last_rows(t, tiles, landed):
            for o, slot, rows in tiles:
                mean1(t + o, slot, rows)
            for o, slot, rows in tiles:
                dve.wait_ge(t_x1, t + o - 1)
                apply1(t + o, slot, rows, 2, landed - 16 * slot)

        with dve.Fori(0, NT // 2) as i:
            last_rows(9 + 2 * i, [(b, b, P) for b in range(2)], 16 * i + 16 * 6)
        last_rows(9 + NT, [(0, 0, NS)], 16 * 10)

    ctx.close()


INS = ["x_prompt", "x_sample", "mem_prompt", "state_win_k", "state_win_v", "state_conv", "state_rec", "cache_mem_k",
       "cache_mem_v", "ln_mix_pre", "w_in", "attn_sink", "gdn_conv_w", "gdn_a_log", "gdn_dt_bias", "gdn_norm_w",
       "ln_mem", "w_mem_kv", "w_branch", "w_out", "ln_mix_post", "ln_ffn_pre", "w_ffn_in", "w_ffn_out", "ln_ffn_post"]
OUTS = [("y_prompt", (1, SEQ, D)), ("y_sample", (DB, DS, D)),
        ("win_k_prompt", (1, WIN, AKV, AHD)), ("win_v_prompt", (1, WIN, AKV, AHD)),
        ("conv_prompt", (1, CW - 1, 12 * P)), ("rec_prompt", (1, BH, P, P)),
        ("mem_k_prompt", (1, MEM, 4, P)), ("mem_v_prompt", (1, MEM, 4, P)),
        ("win_k_sample", (DB, WIN, AKV, AHD)), ("win_v_sample", (DB, WIN, AKV, AHD)),
        ("conv_sample", (DB, CW - 1, 12 * P)), ("rec_sample", (DB, BH, P, P))]


def kernel(**inputs):
    import concourse.bacc as bacc
    from concourse.bass_utils import run_bass_kernel_spmd

    nc = bacc.Bacc("TRN2", target_bir_lowering=False, num_devices=1)
    arrays, io = {}, {}
    tables = dict(zip(("k_const", "k_rope", "k_swa", "k_dmask"), constants()))
    for name in INS + list(tables):
        a = np.ascontiguousarray(inputs[name] if name in inputs else tables[name])
        arrays["in_" + name] = a
        io[name] = nc.dram_tensor("in_" + name, a.shape, mybir.dt.from_np(a.dtype), kind="ExternalInput").ap()
    for name, shape in OUTS:
        io[name] = nc.dram_tensor("out_" + name, shape, F32, kind="ExternalOutput").ap()
    build(nc, io)
    r = run_bass_kernel_spmd(nc, [arrays], core_ids=[0])
    return tuple(r.results[0]["out_" + name] for name, _ in OUTS)
```

```python
from contextlib import ExitStack

import numpy as np
import concourse.bass as bass
from concourse import mybir

F32 = mybir.dt.float32
F32R = mybir.dt.float32r
BF16 = mybir.dt.bfloat16
ALU = mybir.AluOpType
ACT = mybir.ActivationFunctionType
AX = mybir.AxisListType

P = 128
D = 1024
KT = D // P
SEQ, DB, DS = 1024, 8, 4
NS = DB * DS
N = SEQ + NS
CH = N // 3
MEM = 256
WIN = 128
AH, AKV, AHD = 8, 2, 64
BH = 4
CW = 4
FF = 2816
EPS = 1e-6
NT = SEQ // P
C_QKVB, C_BA, C_Z, C_QC, C_GATE = 768, 2304, 2312, 2824, 3336

K_ID, K_ONE, K_GT, K_LE, K_LV = 0, 128, 256, 384, 512
NLV = 7
K_D_LE = K_LV + NLV * P
K_D_GT = K_D_LE + NS
K_D_BLK = K_D_GT + NS
K_COLS = K_D_BLK + NS


def constants():
    k = np.arange(P)[:, None]
    i = np.arange(P)[None, :]
    c = np.zeros((P, K_COLS), np.float32)
    c[:, K_ID:K_ID + P] = k == i
    c[:, K_ONE:K_ONE + P] = 1
    c[:, K_GT:K_GT + P] = k > i
    c[:, K_LE:K_LE + P] = k <= i
    for l in range(NLV):
        s = 2 ** l
        c[:, K_LV + l * P:K_LV + (l + 1) * P] = (k // (2 * s) == i // (2 * s)) & (k % (2 * s) < s) & (i % (2 * s) >= s)
    a, b = k[:NS], i[:, :NS]
    same = a // DS == b // DS
    c[:NS, K_D_LE:K_D_LE + NS] = same & (a <= b)
    c[:NS, K_D_GT:K_D_GT + NS] = same & (a > b)
    c[:NS, K_D_BLK:K_D_BLK + NS] = same
    half = AHD // 2
    inv = np.float32(10000.0) ** (-np.arange(half, dtype=np.float32) / np.float32(half))
    pos = np.concatenate([np.arange(SEQ), np.tile(2048 + np.arange(DS), DB)]).astype(np.float32)
    ang = (inv[:, None].astype(np.float32) * pos[None, :]).astype(np.float32)
    cos, sin = np.cos(ang).astype(np.float32), np.sin(ang).astype(np.float32)
    rope = np.stack([np.concatenate([cos, cos, cos, cos]), np.concatenate([-sin, sin, -sin, sin])])
    q, s = np.arange(WIN)[:, None], np.arange(2 * WIN)[None, :]
    d = q + WIN - s
    swa = np.where((d >= 0) & (d < WIN), 0.0, -1e30).astype(np.float32)
    first = np.where(s < WIN, np.float32(-1e30), swa)
    swa = np.concatenate([first[None], np.repeat(swa[None], NT - 1, 0)]).astype(np.float32)
    step = np.tile(np.arange(DS), 4 * DB)[:, None]
    batch = np.tile(np.repeat(np.arange(DB), DS), 4)[:, None]
    win = np.where(np.arange(WIN)[None, :] > step, 0.0, -1e30)
    new_b, new_s = np.repeat(np.arange(DB), DS)[None, :], np.tile(np.arange(DS), DB)[None, :]
    new = np.where((new_b == batch) & (new_s <= step), 0.0, -1e30)
    dmask = np.concatenate([win, new], 1).astype(np.float32)
    swa = (swa.view(np.uint32) >> 16).astype(np.uint16)
    return c, rope, swa, dmask


def build(nc, io):
    ctx = ExitStack()

    def sb(name, shape, dt=F32, on=None):
        return (on or ctx).enter_context(nc.sbuf_tensor(name, shape, dt))

    def sem(name):
        return ctx.enter_context(nc.semaphore(name))

    def dram(name, shape):
        return nc.dram_tensor(name, shape, F32).ap()

    s_qkv = dram("s_qkv", [12, P, N])
    s_z = dram("s_z", [4, P, N])
    s_qc = dram("s_qc", [4, P, N])
    s_qa = dram("s_qa", [4, P, N])
    s_kv = dram("s_kv", [2, P, WIN + N])
    s_gate = dram("s_gate", [24, P, N])
    s_br = dram("s_br", [12, P, N])

    psum = ctx.enter_context(nc.psum_tensor("psum", [P, 8, 512], F32))
    raw = sb("raw", [P, 2, KT, P])
    wsp = sb("wsp", [P, 2, 2, KT, P], F32R)
    kc = sb("kc", [P, K_COLS])
    ident, ones = kc[:, K_ID:K_ID + P], kc[:, K_ONE:K_ONE + P]
    k_gt, k_le = kc[:, K_GT:K_GT + P], kc[:, K_LE:K_LE + P]
    mkT = sb("mkT", [P, 4, MEM])
    mv = sb("mv", [P, 2, 4 * P])
    ba = sb("ba", [P, NT + 1, 8])
    ssq = sb("ssq", [P, 8, NT + 1])
    tail = sb("tail", [P, 12, 3 + NS])
    st = sb("st", [P, BH, P])
    snk = sb("snk", [P, 2, 8])
    idb = sb("idb", [P, P], BF16)
    hp = sb("hp", [P, 2, BH])
    par = sb("par", [P, 8, NT + 1, BH])
    egl = sb("egl", [P, NT + 1, BH])
    tmp = sb("tmp", [P, 6, NT + 1, BH])
    rr = sb("rr", [P, 2, 8, NT + 1])
    gst = sb("gst", [P, 3, CH])
    aS = ExitStack()
    actT = sb("actT", [P, 2, KT, N], F32R, on=aS)

    k_in = sem("k_in")
    x_in = [sem("x_in0"), sem("x_in1")]
    x_sq = sem("x_sq")
    x_rs = sem("x_rs")
    x_rt = sem("x_rt")
    x_nm = sem("x_nm")
    x_tr = sem("x_tr")
    x_hi = sem("x_hi")
    x_lo = sem("x_lo")
    w_in = [sem("w_in0"), sem("w_in1")]
    w_hi = sem("w_hi")
    w_lo = sem("w_lo")
    g_mm = sem("g_mm")
    g_ev = sem("g_ev")
    sc_t = sem("sc_t")
    sc_c = sem("sc_c")
    pad0 = sem("pad0")
    cv_in = sem("cv_in")
    cv_st = sem("cv_st")
    y_a = sem("y_a")
    y_d = sem("y_d")
    y_st = [sem("y_st0"), sem("y_st1")]
    sq_ok = sem("sq_ok")
    ss_mm = sem("ss_mm")
    ssq_ok = sem("ssq_ok")
    mt = sem("mt")
    mc = sem("mc")
    o_st = sem("o_st")

    NPB = 35
    B_Z, B_C, B_A, B_K, B_VA, B_BA, B_MEM = 12, 16, 20, 24, 25, 26, 27
    YD = lambda n: n - B_Z + 1 if n < B_C else 4 + 3 * (n - B_A + 1)

    def units(n):
        return 3 * n if not isinstance(n, int) or n <= B_MEM else 3 * B_MEM + n - B_MEM

    b0 = ExitStack()
    memT = sb("memT", [P, 2, KT, MEM], F32R, on=b0)
    scT = sb("scT", [P, 12, 28], on=b0)
    nw = sb("nw", [P, 1], on=b0)
    bA = ExitStack()
    xin = sb("xin", [P, 2, D], on=bA)
    xs = sb("xs", [P, 2, D], on=bA)
    gbc = sb("gbc", [P, 2, D], on=bA)
    rs = sb("rs", [P, 2, 4], on=bA)
    xjunk = sb("xjunk", [P, D], on=bA)
    sc_in = sb("sc_in", [28, 12 * P], on=bA)
    bA.close()
    bB = ExitStack()
    cv = sb("cv", [P, 2, 3 + SEQ + 7 * DB], on=bB)
    y = sb("y", [P, 2, N], on=bB)
    y2 = sb("y2", [P, 2, N], on=bB)
    sqb = sb("sqb", [P, N], on=bB)
    rope = sb("rope", [P, 2, N], on=bB)
    mout = sb("mout", [P, 2, 512], on=bB)
    bB.close()
    b0.close()

    wv = io["w_in"].rearrange("(k p) n -> p k n", p=P)
    wmv = io["w_mem_kv"].rearrange("(k p) n -> p k n", p=P)
    x_view = io["x_prompt"].rearrange("b (t p) d -> (b t) p d", p=P)
    xs_view = io["x_sample"].rearrange("b s d -> (b s) d")
    mem_view = io["mem_prompt"].rearrange("b (t p) d -> (b t) p d", p=P)

    rest_tiles = [(8, NS, xs_view, 0, actT, SEQ), (9, P, mem_view[0], 1, memT, 0), (10, P, mem_view[1], 1, memT, P)]

    def by_step(ap):
        return ap.rearrange("p (b s) -> p b s", b=DB)

    UC = units(NPB)
    cC = ExitStack()
    two = [P, 2]
    gin = sb("gin", [P, 2, 16, P], on=cC)
    ain = sb("ain", [P, 2, 8, P], on=cC)
    awin = sb("awin", [P, 2, 2, 2 * WIN], on=cC)
    mbf = sb("mbf", [P, 2, 2 * WIN], BF16, on=cC)
    Q_BETA, Q_G, Q_BK, Q_BKE, Q_KD, Q_EG, Q_RK, Q_RQ = range(8)
    vb, kbe, kd = (sb(n, [P, BH, P], on=cC) for n in ("vb", "kbe", "kd"))
    ug, bi, mrk = (sb(n, [P, BH, P], on=cC) for n in ("ug", "bi", "mrk"))
    dec, decm, kqd, at = (sb(n, [P, BH, P], on=cC) for n in ("dec", "decm", "kqd", "at"))
    atl = sb("atl", [P, NLV, BH, P], on=cC)
    xt, xx, yy = (sb(n, [P, BH, P], on=cC) for n in ("xt", "xx", "yy"))
    vn = sb("vn", [P, BH, P], on=cC)
    uu, wt = xx, yy
    o1s, oo = (sb(n, [P, BH, P], on=cC) for n in ("o1s", "oo"))
    obb = sb("obb", [P, BH, P], on=cC)
    osm = sb("osm", [P, 5, BH], on=cC)
    pr = sb("pr", [P, 2, 2 * WIN], on=cC)
    pt = sb("pt", [P, 4, P], on=cC)
    vtok = sb("vtok", [P, 2, P], on=cC)
    oat = sb("oat", [P, 2, 512], on=cC)
    oba = sb("oba", [P, 2, 4, P], on=cC)
    asm = sb("asm", [P, 7, 12], on=cC)
    S_MX, S_NM, S_SK, S_SM, S_ES, S_DEN, S_RD = range(7)
    cC.close()

    p_in = sem("p_in")
    pp = sem("pp")
    pa = sem("pa")
    pg = sem("pg")
    st0 = sem("st0")
    l_in = {n: [sem(f"l_{n}0"), sem(f"l_{n}1")] for n in ("q", "kv", "z", "qa", "qc", "win")}
    c_sm = sem("c_sm")
    ug_ok, bi_ok, mrk_ok = sem("ug_ok"), sem("bi_ok"), sem("mrk_ok")
    e_tk, e_tv, e_gt, e_br, e_kk, e_kq, e_x0, e_y, e_xx, e_xt, e_u, e_w, e_p1, e_o1, e_sp, e_o2, e_ot = (
        sem("e_" + n) for n in "tk tv gt br kk kq x0 y xx xt u w p1 o1 sp o2 ot".split())
    kd_ok, vb_ok, dec_ok, dm_ok, kq_ok, at_st, al_ok = (sem(n) for n in "kd_ok vb_ok dec_ok dm_ok kq_ok at_st al_ok".split())
    c_x, c_xt, c_y, c_u, c_w, vn_ok, c_o1, c_o, c_s, c_ob = (
        sem(n) for n in "c_x c_xt c_y c_u c_w vn_ok c_o1 c_o c_s c_ob".split())
    o_st1, o_sq, o_rt, on_ok = sem("o_st1"), sem("o_sq"), sem("o_rt"), sem("on_ok")
    ob_st = sem("ob_st")
    a_vt, a_vc = sem("a_vt"), sem("a_vc")
    a_s, a_mx, a_nm, a_sk, a_e, a_t, a_pt, a_v, av_ok = (
        sem(n) for n in "a_s a_mx a_nm a_sk a_e a_t a_pt a_v av_ok".split())
    a_es, a_dn, a_on, a_st = sem("a_es"), sem("a_dn"), sem("a_on"), [sem("a_st0"), sem("a_st1")]
    gs_st = [sem(f"gs_st{c}") for c in range(3)]

    TILE = ("KV", ("S", 0), "DEC", "KK", ("T", 0), ("G", 0), "INV", ("V", 0), ("Y", 1), ("S", 1), ("X", 1),
            ("T", 1), ("Y", 2), ("G", 1), ("X", 2), ("V", 1), ("Y", 3), ("S", 2), ("X", 3), ("T", 2), ("Y", 4), ("G", 2), ("X", 4),
            ("V", 2), ("Y", 5), ("S", 3), ("X", 5), ("T", 3), ("Y", 6), ("G", 3), ("X", 6), ("V", 3), "UW", ("D", 0),
            ("S", 4), "PO", ("G", 4), ("F", 0), ("T", 4), "SO", ("V", 4), "N1", ("S", 5), ("G", 5), ("T", 5), "N2",
            ("V", 5), ("D", 1), "OT", ("F", 1))
    QI = (0, 1, 2, 3, 5, 6)
    A_SC = [AHD ** -0.5] * 4 + [P ** -0.5] * 2

    def bc_h(ap):
        return ap.unsqueeze(1).to_broadcast([P, BH, P])

    def bc_c(ap):
        return ap.rearrange("p a h -> p (a h)").unsqueeze(2).to_broadcast([P, BH, P])

    def per(q, t):
        return par[:, q, bass.ds(t, 1), :]
    cE = ExitStack()
    tlo = sb("tlo", [3 + NS, 12 * P], on=cE)
    wkT = sb("wkT", [P, DB, P], on=cE)
    ckT = sb("ckT", [P, 4, MEM], on=cE)
    dkb = sb("dkb", [NS, BH, P], on=cE)
    lkv = sb("lkv", [P, 2, P], on=cE)
    ext = sb("ext", [P, 6, NS], on=cE)
    dq = sb("dq", [P, 16, NS], on=cE)
    da = sb("da", [P, 8, NS], on=cE)
    wkv = sb("wkv", [P, 2, DB, P], on=cE)
    dmk = sb("dmk", [P, WIN + NS], on=cE)
    sd = sb("sd", [P, DB, BH, P], on=cE)
    ck = sb("ck", [P, 2, 2, 4 * P], on=cE)
    vnm = sb("vnm", [NS, 4, 4, P], on=cE)
    dia = sb("dia", [NS, 4, BH, NS], on=cE)
    dug, dmr, ddc, dat, dat1, dkq, dxt, dxx, dyy = (
        sb(n, [NS, BH, NS], on=cE) for n in "dug dmr ddc dat dat1 dkq dxt dxx dyy".split())
    dkd, dvb, dvn = (sb(n, [NS, BH, P], on=cE) for n in "dkd dvb dvn".split())
    wq = sb("wq", [P, BH, DB, 2, DS], on=cE)
    duT, dvT, dqe, dsq, dnm = (sb(n, [P, BH, NS], on=cE) for n in "duT dvT dqe dsq dnm".split())
    deg = sb("deg", [P, BH, NS], on=cE)
    del_ = sb("del_", [P, BH, NS], on=cE)
    mS = sb("mS", [P, 2, P], on=cE)
    mR = sb("mR", [P, MEM], on=cE)
    sS = sb("sS", [P, 4, P], on=cE)
    sR = sb("sR", [P, 2, WIN + NS], on=cE)
    dsm = sb("dsm", [P, 20], on=cE)
    sks = sb("sks", [P, 2], on=cE)
    kvo = sb("kvo", [P, 2, 2, P], on=cE)
    dob = sb("dob", [P, 3, 4, NS], on=cE)
    cE.close()

    F_IN = 16 * (9 + 8)
    f_in = sem("f_in")
    f_pe, f_ac, f_dv = sem("f_pe"), sem("f_ac"), sem("f_dv")
    m_in = [sem("m_in0"), sem("m_in1")]
    m_kt, m_ka, m_kd, m_sc = sem("m_kt"), sem("m_ka"), sem("m_kd"), sem("m_sc")
    g_up, g_ad = sem("g_up"), sem("g_ad")
    f_st = sem("f_st")
    s_in = pad0
    LOAD_G = {0: 18, 3: 19, 5: 20, 8: 21, 10: 22, 12: 23}

    PE_E = ("out", "win_kt0", "bcast", "win_kt1", "x0", "new_sc", "mem_rows", "y", "win_rows", "xt", "mem_pt", "u_w",
            "win_pt", "w_q_s", "vn", "win_o", "o", "sumsq", "mem_o")
    AC_E = ("kv_out", "new_out", "tail_out", "wkT0", "dec", "rq", "wkT1", "mem_s", "x0", "win_s", "y", "mem_exp",
            "win_exp", "win_sk", "mem_p", "win_p", "vn", "sq", "root")
    DV_E = ("ug", "d0", "d1", "d2", "d3", "mr", "kb", "kd", "vb", "dcm", "at0", "at", "kq", "x_", "xt0", "at1", "eg",
            "el", "mem_mx", "mem_nm", "win_m0", "win_m1", "win_mx", "win_nx", "win_nm", "win_sk", "mem_rd", "mem_n",
            "xt", "win_dn", "win_rd", "win_n", "uT", "wT", "vT", "qe", "vm0", "win_c0", "win_c1", "win_o0", "win_o1",
            "o_", "s_e", "n0", "n1", "n2", "oq", "oz", "n3", "o_z", "vm1", "mem_o")
    PEn, ACn, DVn = (lambda s: PE_E.index(s) + 1), (lambda s: AC_E.index(s) + 1), (lambda s: DV_E.index(s) + 1)
    NPD = NPB + 24
    NPO = NPD + 12
    NPF = NPO + 8
    NF = FF // P
    UD = UC + 72
    UO = UD + 72
    UF = UO + 24
    ORDER = (0, 1, 2)
    aS.close()
    cD = ExitStack()
    actD = sb("actD", [P, 2, KT, N], F32R, on=cD)
    cB = ExitStack()
    brw = sb("brw", [P, 4, N], on=cB)
    cB.close()
    fT = sb("fT", [P, 2, 2, N], F32R, on=cD)
    accT = sb("accT", [P, KT, N], on=cD)
    cG = ExitStack()
    gat = sb("gat", [P, 2, 2, N], on=cG)
    prd = sb("prd", [P, 2, CH], on=cG)
    cG.close()
    gn = sb("gn", [P, 3, D], on=cD)
    xr = sb("xr", [P, 2, D], on=cD)
    yr = sb("yr", [P, 2, D], on=cD)
    jk = sb("jk", [P, 2, D], BF16, on=cD)
    ns = sb("ns", [P, 2, 2, 4], on=cD)
    cX = ExitStack()
    xs2 = sb("xs2", [P, 2, D], on=cX)
    cX.close()
    sg = sb("sg", [P, N], on=cD)
    fr = sb("fr", [P, N], on=cD)
    cD.close()
    s_x1 = dram("s_x1", [NT + 1, P, D])

    b_in = sem("b_in")
    b_hi, b_lo = sem("b_hi"), sem("b_lo")
    q_in = [sem("q_in0"), sem("q_in1")]
    q_sg = sem("q_sg")
    q_pr = sem("q_pr")
    q_mx = sem("q_mx")
    r_in = [sem("r_in0"), sem("r_in1")]
    t_tr, t_sq, t_ms, t_rt, t_rd, t_y, t_x1 = (sem("t_" + n) for n in "tr sq ms rt rd y x1".split())
    t_xst = [sem("t_xst0"), sem("t_xst1")]
    u_sq, u_ms, u_rt, u_rd, u_xs, u_tr, u_hi, u_lo = (sem("u_" + n) for n in "sq ms rt rd xs tr hi lo".split())
    f_sg, f_fr, f_hi, f_lo = sem("f_sg"), sem("f_fr"), sem("f_hi"), sem("f_lo")
    o_mm, o_ad = sem("o_mm"), sem("o_ad")
    wbv = io["w_branch"]
    wov = io["w_out"].rearrange("(k p) n -> p k n", p=P)
    wfv = io["w_ffn_in"].rearrange("(k p) n -> p k n", p=P)
    wgv = io["w_ffn_out"].rearrange("(f p) n -> f p n", p=P)
    y_view = io["y_prompt"].rearrange("b (t p) d -> (b t) p d", p=P)
    ys_view = io["y_sample"].rearrange("b s d -> (b s) d")

    BR_AT = {(j + k // 2, k % 2): (r, k) for r, j in ((1, 2), (2, 6)) for k in range(4)}

    def slab(t, slot):
        return t[:, slot].rearrange("p k n -> p (k n)").rearrange("p (k n) -> p k n", k=4)

    def add_row(eng, t, slot, rows, landed):
        eng.wait_ge(t_y, 2 + t + 1)
        eng.wait_ge(r_in[slot], landed)
        eng.tensor_tensor(xr[0:rows, slot, :], xr[0:rows, slot, :], yr[0:rows, slot, :], ALU.add).then_inc(t_x1, 1)
    block = ctx.enter_context(nc.Block())

    @block.sync
    def _(sp):
        sp.sem_inc(x_nm, 2)
        sp.sem_inc(y_st[0], 16)
        sp.sem_inc(y_st[1], 16)
        sp.dma_start(kc[:], io["k_const"]).then_inc(k_in, 16)
        sp.dma_start(gbc[:, 0, :], io["ln_mix_pre"].partition_broadcast(P)).then_inc(k_in, 16)
        sp.dma_start(gbc[:, 1, :], io["ln_mem"].partition_broadcast(P)).then_inc(k_in, 16)
        sp.dma_start(hp[:, 0, :], io["gdn_a_log"].partition_broadcast(P)).then_inc(p_in, 16)
        sp.dma_start(hp[:, 1, :], io["gdn_dt_bias"].partition_broadcast(P)).then_inc(p_in, 16)
        sp.dma_start(snk[:, 0, :], io["attn_sink"].partition_broadcast(P)).then_inc(p_in, 16)
        sp.wait_ge(pad0, 3)
        sp.dma_start(s_kv.rearrange("a p n -> p a n")[:, :, 0:WIN], st[:, 0:2, :]).then_inc(p_in, 16)
        sp.dma_start(nw[:], io["gdn_norm_w"].rearrange("(p a) -> p a", a=1)).then_inc(k_in, 16)
        sp.dma_start(sc_in[0:24, :], io["state_conv"].rearrange("b c n -> (b c) n")).then_inc(k_in, 16)
        sp.dma_start(sc_in[24:28, :], io["gdn_conv_w"]).then_inc(k_in, 16)

        def load_x(n, slot, rows, src):
            sp.wait_ge(x_nm, n + 1)
            sp.dma_start(xin[0:rows, slot, :], src).then_inc(x_in[slot], 16)

        with sp.Fori(0, NT // 2) as i:
            for b in range(2):
                load_x(2 * i + b, b, P, x_view[bass.ds(2 * i + b, 1)].rearrange("a p d -> (a p) d"))
        for n, rows, src, *_ in rest_tiles:
            load_x(n, n % 2, rows, src)

        def load_w(n, halves):
            sp.wait_ge(w_lo, n + 1)
            for dst, src in halves:
                sp.dma_start(dst, src).then_inc(w_in[n % 2], 16)

        def k_halves(n, view, col, width=P):
            return [(raw[:, n % 2, 4 * h:4 * h + 4, 0:width], view[:, 4 * h:4 * h + 4, col:col + width])
                    for h in range(2)]

        def load_b(n):
            if n < B_Z:
                load_w(n, k_halves(n, wv, C_QKVB + P * n))
            elif n < B_C:
                load_w(n, k_halves(n, wv, C_Z + P * (n - B_Z)))
            elif n < B_A:
                load_w(n, k_halves(n, wv, C_QC + P * (n - B_C)))
            elif n < B_K:
                g = n - B_A
                load_w(n, [(raw[:, n % 2, :, 64 * h:64 * h + 64], wv[:, :, 256 * h + 64 * g:256 * h + 64 * g + 64])
                           for h in range(2)])
            elif n < B_MEM:
                load_w(n, k_halves(n, wv, {B_K: 512, B_VA: 640, B_BA: C_BA}[n], 8 if n == B_BA else P))
            else:
                load_w(n, k_halves(n, wmv, P * (n - B_MEM)))

        load_b(0)
        load_b(1)
        sp.wait_ge(x_lo, 2 + 11)
        sp.dma_start(rope[:], io["k_rope"].rearrange("a p n -> p a n")).then_inc(k_in, 16)
        rows = [s_qkv[n] for n in range(12)] + [s_z[n] for n in range(4)] + [s_qc[n] for n in range(4)]
        rows += [s_qa[n] for n in range(4)] + [s_kv[n][:, WIN:] for n in range(2)]
        for n in range(2, 4):
            load_b(n)
        for n in range(B_BA):
            load_b(n + 4)
            if n < B_Z:
                sp.wait_ge(y_a, 2 + n + 1)
            elif n < B_C or B_A <= n < B_VA:
                sp.wait_ge(y_d, YD(n))
            else:
                sp.wait_ge(g_ev, 3 + 3 * n + 3)
            sp.dma_start(rows[n], y2[:, n % 2, :]).then_inc(y_st[n % 2], 16)
        for n in range(B_BA + 4, NPB):
            load_b(n)
        for s in range(2):
            sp.wait_ge(mc, 1 + 2 * s + 1)
            sp.dma_start(io["mem_k_prompt"][0, P * s:P * s + P].rearrange("t h d -> t (h d)"), mout[:, s, :]).then_inc(o_st, 16)
            sp.wait_ge(mc, 1 + 2 * s + 2)
            sp.dma_start(io["mem_v_prompt"][0, P * s:P * s + P].rearrange("t h d -> t (h d)"), mv[:, s, :]).then_inc(o_st, 16)
        def load_tile(t, b):
            def cols(src, w=P):
                return src.rearrange("n p t -> p n t")[:, :, bass.ds(P * t, w)]

            if not isinstance(t, int):
                sp.wait_ge(c_ob, t)
            sp.dma_start(gin[:, b, 4:12, :], cols(s_qkv[4:12])).then_inc(l_in["kv"][b], 16)
            sp.dma_start(awin[:, b], cols(s_kv, 2 * WIN)).then_inc(l_in["win"][b], 16)
            sp.dma_start(mbf[:, b], io["k_swa"][bass.ds(t, 1)].rearrange("a q s -> (a q) s").bitcast(BF16)).then_inc(l_in["win"][b], 16)
            sp.dma_start(ain[:, b, 0:4, :], cols(s_qa)).then_inc(l_in["qa"][b], 16)
            sp.dma_start(gin[:, b, 0:4, :], cols(s_qkv[0:4])).then_inc(l_in["q"][b], 16)
            sp.dma_start(ain[:, b, 4:8, :], cols(s_qc)).then_inc(l_in["qc"][b], 16)
            sp.dma_start(gin[:, b, 12:16, :], cols(s_z)).then_inc(l_in["z"][b], 16)

        def load_gate(m, slot):
            sp.wait_ge(w_lo, NPB + m + 1)
            for h in range(2):
                sp.dma_start(raw[:, slot, 4 * h:4 * h + 4, :], wv[:, 4 * h:4 * h + 4, bass.ds(C_GATE + P * m, P)]).then_inc(w_in[slot], 16)

        def serve_tile(t, b, last=False):
            for j in range(2):
                load_gate(2 * t + 2 + j, (NPB + j) % 2)
                for c in range(3):
                    sp.wait_ge(g_ev, 3 + UC + 6 * t + 3 * j + c + 1)
                    sp.dma_start(s_gate[bass.ds(2 * t + j, 1)].rearrange("a p n -> (a p) n")[:, CH * c:CH * c + CH],
                                 gst[:, c]).then_inc(gs_st[c], 16)
                if j == 0 and not last:
                    load_tile(t + 1, 1 - b)
            sp.wait_ge(c_ob, 2 + t)
            sp.dma_start(s_br[4:8].rearrange("n p t -> p n t")[:, :, bass.ds(P * t, P)], obb[:]).then_inc(ob_st, 16)

        sp.wait_ge(y_st[0], 16 + 16 * 13)
        sp.wait_ge(y_st[1], 16 + 16 * 13)
        sp.wait_ge(p_in, 64)
        sp.wait_ge(mc, 1 + 4)
        sp.wait_ge(o_st, 64)
        sp.sem_inc(c_ob, 1)
        for s in range(2):
            load_gate(s, (NPB + s) % 2)
        load_tile(0, 0)
        with sp.Fori(0, 3) as i:
            for b in range(2):
                serve_tile(2 * i + b, b)
        serve_tile(6, 0)
        serve_tile(7, 1, last=True)
        def load_wb(j):
            n = NPD + j
            sp.wait_ge(w_lo, n + 1)
            src = wbv[ORDER[j // 4]][:, 256 * (j % 4):256 * (j % 4) + 256]
            dst = slab(raw, n % 2)
            for h in range(2):
                if ORDER[j // 4] == 0:
                    sp.dma_start(dst[64 * h:64 * h + 64], src.rearrange("(v g d) n -> v d g n", v=2, g=4)[h]).then_inc(w_in[n % 2], 16)
                else:
                    sp.dma_start(dst[:, 2 * h:2 * h + 2], src.rearrange("(k p) n -> p k n", p=P)[:, 2 * h:2 * h + 2]).then_inc(w_in[n % 2], 16)

        def load_br(r):
            sp.wait_ge(b_lo, 4 * r + 1)
            sp.dma_start(brw[:], s_br[4 * ORDER[r]:4 * ORDER[r] + 4].rearrange("n p t -> p n t")).then_inc(b_in, 16)

        def load_q(j):
            sp.wait_ge(q_mx, 6 * j + 6)
            m = 8 * ORDER[j // 4] + 2 * (j % 4)
            sp.dma_start(gat[:, j % 2], s_gate[m:m + 2].rearrange("n p t -> p n t")).then_inc(q_in[j % 2], 16)

        sp.wait_ge(c_ob, 2 + NT - 1)
        sp.wait_ge(ob_st, 16 + 16 * NT)
        for s in range(2):
            sp.wait_ge(a_st[s], 16 + 16 * NT)
        for c in range(3):
            sp.wait_ge(gs_st[c], 16 + 16 * 16)
        sp.wait_ge(c_s, 1 + NT)
        sp.dma_start(io["rec_prompt"][0].rearrange("h k v -> k h v"), st[:]).then_inc(f_st, 16)
        cols = lambda src, n: src.rearrange("n p t -> p n t")[:, :, n:]
        sp.dma_start(lkv[:], s_kv.rearrange("n p t -> p n t")[:, :, SEQ:SEQ + WIN]).then_inc(f_in, 16)
        sp.dma_start(ext[:, 0:2, :], cols(s_kv, WIN + SEQ)).then_inc(f_in, 16)
        sp.dma_start(dq[:, 0:12, :], cols(s_qkv, SEQ)).then_inc(f_in, 16)
        sp.dma_start(dq[:, 12:16, :], cols(s_z, SEQ)).then_inc(f_in, 16)
        sp.dma_start(da[:, 0:4, :], cols(s_qa, SEQ)).then_inc(f_in, 16)
        sp.dma_start(da[:, 4:8, :], cols(s_qc, SEQ)).then_inc(f_in, 16)
        sp.dma_start(wkv[:, 0], io["state_win_k"].rearrange("b s v d -> s b (v d)")).then_inc(f_in, 16)
        sp.dma_start(wkv[:, 1], io["state_win_v"].rearrange("b s v d -> s b (v d)")).then_inc(f_in, 16)
        sp.dma_start(dmk[:], io["k_dmask"]).then_inc(f_in, 16)
        for v in range(2):
            for g in range(4):
                sp.dma_start(sks[32 * g:32 * g + 32, v:v + 1], io["attn_sink"][4 * v + g:4 * v + g + 1].partition_broadcast(32)).then_inc(f_in, 16)

        for x in range(2 * DB):
            b, name = x % DB, "cache_mem_k" if x < DB else "cache_mem_v"
            sp.wait_ge(m_kt, 2 * x + 2)
            sp.dma_start(ck[:, x % 2], io[name][b].rearrange("(t s) h d -> s t (h d)", s=P)).then_inc(m_in[x % 2], 16)
            if x in LOAD_G:
                m = LOAD_G[x]
                load_gate(m, (NPB + m) % 2)
            if x == 3:
                for b in range(DB):
                    sp.dma_start(sd[:, b], io["state_rec"][b].rearrange("h k v -> k h v")).then_inc(s_in, 16)
        for v, (src, dst, pdst) in enumerate((("state_win_k", "win_k_sample", "win_k_prompt"), ("state_win_v", "win_v_sample", "win_v_prompt"))):
            sp.dma_start(io[dst][:, 0:WIN - DS].rearrange("b s v d -> b (s v d)"),
                         io[src][:, DS:WIN].rearrange("b s v d -> b (s v d)")).then_inc(f_st, 16)
            sp.wait_ge(f_ac, ACn("new_out"))
            sp.dma_start(io[pdst][0].rearrange("s v d -> s (v d)"), kvo[:, 0, v, :]).then_inc(f_st, 16)
            for b in range(DB):
                sp.dma_start(io[dst][b, WIN - DS:WIN].rearrange("s v d -> s (v d)"), kvo[DS * b:DS * b + DS, 1, v, :]).then_inc(f_st, 16)
        sp.wait_ge(f_ac, ACn("tail_out"))
        sp.dma_start(io["conv_prompt"][0], tlo[0:3, :]).then_inc(f_st, 16)
        for b in range(DB):
            sp.dma_start(io["conv_sample"][b], tlo[4 + DS * b:7 + DS * b, :]).then_inc(f_st, 16)
        def store_dec(f, name):
            sp.wait_ge(f_dv, DVn(name))
            sp.dma_start(cols(s_br[4 * f:4 * f + 4], SEQ), dob[:, f]).then_inc(f_st, 16)

        store_dec(0, "win_o1")
        sp.wait_ge(f_st, 16 * (1 + 2 * (2 + DB) + 1 + DB + 1))
        sp.sem_inc(b_lo, 1)
        load_br(0)
        store_dec(1, "o_z")
        sp.wait_ge(g_ad, 8)
        for b in range(DB):
            sp.dma_start(io["rec_sample"][b].rearrange("h k v -> k h v"), sd[:, b]).then_inc(f_st, 16)
        store_dec(2, "mem_o")
        load_wb(0)
        load_wb(1)
        F_ST = 16 * (1 + 2 * (2 + DB) + 1 + DB + 3 + DB)
        sp.wait_ge(f_st, F_ST)
        for c in range(3):
            sp.wait_ge(gs_st[c], 16 + 16 * 24)
        load_q(0)
        load_q(1)
        for j in range(12):
            if j + 2 < 12:
                load_wb(j + 2)
                load_q(j + 2)
            if j in (0, 4):
                load_br(j // 4 + 1)
        for m in range(8):
            n = NPO + m
            load_w(n, [(raw[:, n % 2, 4 * h:4 * h + 4, :], wov[:, 4 * h:4 * h + 4, P * m:P * m + P]) for h in range(2)])
        sp.wait_ge(q_mx, 12 + 72)
        sp.wait_ge(b_hi, 20)
        for j, name in enumerate(("ln_mix_post", "ln_ffn_pre", "ln_ffn_post")):
            sp.dma_start(gn[:, j, :], io[name].partition_broadcast(P)).then_inc(b_in, 16)

        def load_f(n, slot, view, col):
            sp.wait_ge(w_lo, n + 1)
            for h in range(2):
                sp.dma_start(raw[:, slot, 4 * h:4 * h + 4, :], view[:, 4 * h:4 * h + 4, bass.ds(col, P)]).then_inc(w_in[slot], 16)

        def load_fo(n, slot, f):
            sp.wait_ge(w_lo, n + 1)
            for h in range(2):
                sp.dma_start(raw[:, slot, 4 * h:4 * h + 4, :], wgv[bass.ds(f, 1)].rearrange("a p (k n) -> p (a k) n", n=P)[:, 4 * h:4 * h + 4]).then_inc(w_in[slot], 16)

        def norm_io(t, slot, rows, src, before):
            sp.wait_ge(t_xst[slot], before)
            sp.dma_start(xr[0:rows, slot, :], src).then_inc(r_in[slot], 16)

        def store_x1(t, slot, rows, dst):
            sp.wait_ge(u_xs, 2 + t + 1)
            sp.dma_start(dst, xr[0:rows, slot, :]).then_inc(t_xst[slot], 16)

        def store_y(t, slot, rows, dst):
            sp.wait_ge(t_x1, t + 1)
            sp.dma_start(dst, xr[0:rows, slot, :]).then_inc(t_xst[slot], 16)

        load_f(NPF, NPF % 2, wfv, 0)
        load_f(NPF + 1, (NPF + 1) % 2, wfv, FF)
        sp.sem_inc(t_xst[0], 16)
        sp.sem_inc(t_xst[1], 16)
        one = lambda v, t: v[bass.ds(t, 1)].rearrange("a p d -> (a p) d")
        norm_io(0, 0, P, x_view[0], 16)
        norm_io(1, 1, P, x_view[1], 16)
        with sp.Fori(0, NT // 2 - 1) as i:
            for b in range(2):
                store_x1(2 * i + b, b, P, one(s_x1, 2 * i + b))
                norm_io(2 * i + 2 + b, b, P, one(x_view, 2 * i + 2 + b), 16 * i + 32)
        store_x1(NT - 2, 0, P, s_x1[NT - 2])
        norm_io(NT, 0, NS, xs_view, 16 * 5)
        store_x1(NT - 1, 1, P, s_x1[NT - 1])
        store_x1(NT, 0, NS, s_x1[NT][0:NS])

        def load_step(i, b):
            n = NPF + 3 * i - 1
            s = (NPF + 3 * b - 1) % 2
            load_f(n, s, wfv, P * i)
            load_f(n + 1, 1 - s, wfv, P * i + FF)
            load_fo(n + 2, s, i - 1)

        with sp.Fori(0, (NF - 2) // 2) as i:
            for b in (1, 2):
                load_step(2 * i + b, b)
        load_step(NF - 1, 1)
        load_fo(NPF + 3 * NF - 1, (NPF + 3 * NF - 1) % 2, NF - 1)

        def final_in(t, slot, rows, src, before):
            sp.wait_ge(t_xst[slot], before)
            sp.dma_start(xr[0:rows, slot, :], src).then_inc(r_in[slot], 16)

        final_in(0, 0, P, s_x1[0], 16 * 6)
        final_in(1, 1, P, s_x1[1], 16 * 5)
        with sp.Fori(0, NT // 2 - 1) as i:
            for b in range(2):
                store_y(9 + 2 * i + b, b, P, one(y_view, 2 * i + b))
            for b in range(2):
                final_in(2 * i + 2 + b, b, P, one(s_x1, 2 * i + 2 + b), 16 * i + 16 * (7 - b))
        for b in range(2):
            store_y(9 + 6 + b, b, P, y_view[6 + b])
        final_in(NT, 0, NS, s_x1[NT][0:NS], 16 * 10)
        store_y(9 + NT, 0, NS, ys_view)
        sp.wait_ge(t_xst[0], 16 * 11)
        sp.wait_ge(t_xst[1], 16 * 9)
        for s in range(2):
            sp.wait_ge(y_st[s], 16 + 16 * B_BA // 2)
            sp.wait_ge(a_st[s], 16 + 16 * NT)
        sp.wait_ge(o_st, 64)
        sp.wait_ge(ob_st, 16 + 16 * NT)
        for c in range(3):
            sp.wait_ge(gs_st[c], 16 + 16 * 24)

    @block.gpsimd
    def _(pool):
        pool.sem_inc(w_lo, 2)
        pool.memset(ssq[:], 1.0).then_inc(pad0, 1)
        pool.memset(ba[:], 0.0).then_inc(pad0, 1)
        pool.memset(st[:], 0.0).then_inc(pad0, 1)

        def split_at(n, slot, landed, done):
            pool.wait_ge(w_in[slot], landed)
            pool.wait_ge(g_mm, done)
            pool.tensor_tensor(wsp[:, slot, 0], raw[:, slot], ones.unsqueeze(1).to_broadcast([P, KT, P]),
                               ALU.mult).then_inc(w_hi, 1)
            pool.wait_ge(w_hi, n + 1)
            pool.tensor_tensor(wsp[:, slot, 1], raw[:, slot], wsp[:, slot, 0].bitcast(F32),
                               ALU.subtract).then_inc(w_lo, 1)

        def split(n, slot, landed):
            split_at(n, slot, landed, 6 + units(n - 1))

        pool.wait_ge(k_in, 16 * 6)
        split(0, 0, 32)
        split(1, 1, 32)
        pool.wait_ge(x_lo, 2 + 11)
        pool.memset(cv[:, 0, 0:3], 0.0).then_inc(pad0, 1)
        pool.memset(cv[:, 1, 0:3], 0.0).then_inc(pad0, 1)
        with pool.Fori(1, 13) as i:
            for b in range(2):
                split(2 * i + b, b, 32 * i + 32)
        for n in range(26, NPB):
            split(n, n % 2, 32 * (n // 2) + 32)
        pool.sem_inc(dm_ok, 1)
        split_at(NPB, NPB % 2, 32 * (NPB // 2) + 32, 6 + UC - 3)
        pool.wait_ge(pp, 17)
        with pool.Fori(0, 4) as i:
            for b in range(2):
                t = 2 * i + b
                pool.wait_ge(dm_ok, t + 1)
                pool.tensor_tensor(ug[:], bc_h(k_le), bc_c(per(Q_G, t)), ALU.mult).then_inc(ug_ok, 1)
                pool.tensor_tensor(mrk[:], bc_h(k_le), bc_c(per(Q_RK, t)), ALU.mult).then_inc(mrk_ok, 1)
                pool.wait_ge(kq_ok, t + 1)
                pool.tensor_tensor(bi[:], bc_h(ident), bc_c(per(Q_BK, t)), ALU.mult).then_inc(bi_ok, 1)
                for j in (1, 2):
                    s = NPB + 2 * b + j
                    split_at(NPB + 2 * t + j, s % 2, 64 * i + 32 * (s // 2) + 32, 6 + UC + 6 * t + 3 * j - 3)
        for m in range(17, 24):
            split_at(NPB + m, (NPB + m) % 2, 32 * ((NPB + m) // 2) + 32, 6 + UC + 3 * m - 3)
        for j in range(12):
            n = NPD + j
            split_at(n, n % 2, 32 * (n // 2) + 32, 6 + UD + (6 * (j - 1) if j > 0 else -3))
        for m in range(8):
            n = NPO + m
            split_at(n, n % 2, 32 * (n // 2) + 32, 6 + UO + (3 * (m - 1) if m > 0 else -6))
        split_at(NPF, NPF % 2, 32 * (NPF // 2) + 32, 6 + UF - 3)
        split_at(NPF + 1, (NPF + 1) % 2, 32 * ((NPF + 1) // 2) + 32, 6 + UF)

        with pool.Fori(0, NT // 2) as i:
            for b in range(2):
                add_row(pool, 2 * i + b, b, P, 16 * i + 16)
        add_row(pool, NT, 0, NS, 16 * 5)

        def split_step(i, b, landed):
            for j in range(3):
                if isinstance(i, int):
                    done = (3, 6, 9)[j]
                else:
                    done = 6 * i + (0, 0, 3)[j]
                    if j == 1:
                        pool.wait_ge(o_mm, 24 * i + 24)
                split_at(NPF + 3 * i - 1 + j, (NPF + 3 * b - 1 + j) % 2, landed(j), 6 + UF + done)

        base = lambda b, j: 32 * ((NPF + 3 * b - 1 + j) // 2) + 32
        split_step(1, 1, lambda j: base(1, j))
        with pool.Fori(0, (NF - 2) // 2) as i:
            for b in (2, 3):
                split_step(2 * i + b, b, lambda j, b=b: 96 * i + base(b, j))
        n = NPF + 3 * NF - 1
        split_at(n, n % 2, 32 * (n // 2) + 32, 6 + UF + 6 * NF)

    @block.tensor
    def _(pe):
        pe.sem_inc(g_mm, 6)
        pe.sem_inc(ss_mm, 1)
        pe.wait_ge(k_in, 16 * 6)
        for j in range(12):
            mm = pe.transpose(psum[:, 5, 28 * j:28 * j + 28], sc_in[:, P * j:P * j + P], ident[0:28, 0:28])
        mm.then_inc(sc_t, 1)

        def turn_x(n, slot, rows):
            pe.wait_ge(x_nm, 2 + n + 1)
            pe.wait_ge(x_lo, n + 1)
            for k in range(KT):
                mm = pe.transpose(psum[:, 2 * slot + k // 4, P * (k % 4):P * (k % 4) + rows],
                                  xs[0:rows, slot, P * k:P * k + P], ident[0:rows, 0:rows])
            mm.then_inc(x_tr, 1)

        with pe.Fori(0, NT // 2) as i:
            for b in range(2):
                turn_x(2 * i + b, b, P)
        for n, rows, *_ in rest_tiles:
            turn_x(n, n % 2, rows)

        def gemm(n, slot, m=P):
            pe.wait_ge(w_lo, n + 3)
            for c in range(3):
                pe.wait_ge(g_ev, units(n) + c + 1)
                for k in range(KT):
                    for q, (a, h) in enumerate(((0, 0), (0, 1), (1, 0))):
                        mm = pe.matmul(psum[0:m, c, 0:CH], wsp[:, slot, a, k, 0:m],
                                       actT[:, h, k, CH * c:CH * c + CH],
                                       start=(k == 0 and q == 0), stop=(k == KT - 1 and q == 2))
                mm.then_inc(g_mm, 1)

        def head_squares(n):
            pe.wait_ge(sq_ok, n + 1)
            for t in range(NT + 1):
                r = P if t < NT else NS
                mm = pe.matmul(psum[0:r, 4, bass.ds(n * (NT + 1) + t, 1)], sqb[:, P * t:P * t + r], ones[:, 0:1],
                               start=True, stop=True)
            mm.then_inc(ss_mm, 1)

        pe.wait_ge(x_lo, 2 + 11)
        gemm(0, 0)
        gemm(1, 1)
        gemm(2, 0)
        with pe.Fori(0, 4) as i:
            for b in range(2):
                gemm(2 * i + 3 + b, 1 - b)
                head_squares(2 * i + b)
        gemm(11, 1)
        with pe.Fori(6, 13) as i:
            for b in range(2):
                gemm(2 * i + b, b)
        gemm(B_BA, 0, m=8)
        for j in range(8):
            n = B_MEM + j
            pe.wait_ge(w_lo, n + 3)
            pe.wait_ge(g_ev, units(n) + 1)
            for k in range(KT):
                for q, (a, h) in enumerate(((0, 0), (0, 1), (1, 0))):
                    mm = pe.matmul(psum[:, j % 3, 0:MEM], wsp[:, n % 2, a, k], memT[:, h, k, :],
                                   start=(k == 0 and q == 0), stop=(k == KT - 1 and q == 2))
            mm.then_inc(g_mm, 1)
            if j == 0:
                pe.wait_ge(g_ev, 3 + units(B_MEM))
                for t in range(NT + 1):
                    r = P if t < NT else NS
                    mm = pe.transpose(psum[0:r, 5, 8 * t:8 * t + 8], y2[0:8, 0, P * t:P * t + r], ident[0:8, 0:8])
                mm.then_inc(mt, 1)
            if j == 5:
                pe.wait_ge(pp, 10)
                for x, (full, dcd) in enumerate(((K_LE, K_D_LE), (K_GT, K_D_GT), (K_ONE, K_D_BLK))):
                    pe.matmul(psum[:, 5, 36 * x:36 * x + 32], kc[:, full:full + P], par[:, Q_G, 0:NT, :],
                              start=True, stop=True)
                    mm = pe.matmul(psum[0:NS, 5, 36 * x + 32:36 * x + 36], kc[0:NS, dcd:dcd + NS], par[0:NS, Q_G, NT, :],
                                   start=True, stop=True)
                mm.then_inc(pg, 1)
        pe.wait_ge(g_ev, 3 + units(NPB))
        pe.wait_ge(pa, 10)
        for s in range(2):
            for v in range(2):
                j = 2 * s + v
                pe.wait_ge(mc, 1 + max(j - 1, 0))
                for h in range(4):
                    src = mkT[:, h, P * s:P * s + P] if v == 0 else y[:, h // 2, MEM * (h % 2) + P * s:MEM * (h % 2) + P * s + P]
                    mm = pe.transpose(psum[:, 5 + j % 2, P * h:P * h + P], src, ident)
                mm.then_inc(mt, 1)
        pe.wait_ge(mc, 1 + 4)
        pe.wait_ge(st0, 3)

        def mm4(bank, lhs, rhs, done, w=P):
            for h in range(BH):
                mm = pe.matmul(psum[:, bank, w * h:w * h + w], lhs(h), rhs(h), start=True, stop=True)
            mm.then_inc(done, 1)

        def pe_tile(i, b):
            t = 2 * i + b
            k, v, q = (lambda h: gin[:, b, 4 + h, :]), (lambda h: gin[:, b, 8 + h, :]), (lambda h: gin[:, b, h, :])

            def turn4(bank, src, done):
                for h in range(BH):
                    mm = pe.transpose(psum[:, bank, P * h:P * h + P], src(h), ident)
                mm.then_inc(done, 1)

            for step in TILE:
                if step == "KV":
                    pe.wait_ge(l_in["kv"][b], 16 * i + 16)
                    pe.wait_ge(c_ob, t + 1)
                    turn4(5, k, e_tk)
                    pe.wait_ge(c_o, t + 1)
                    turn4(6, v, e_tv)
                elif step == "DEC":
                    pe.wait_ge(ug_ok, t + 1)
                    pe.wait_ge(c_s, t + 1)
                    pe.matmul(psum[:, 7, :], k_gt, ug[:], start=True, stop=True).then_inc(e_gt, 1)
                    pe.wait_ge(bi_ok, t + 1)
                    pe.wait_ge(kd_ok, t + 1)
                    pe.matmul(psum[:, 5, :], ones, bi[:], start=True, stop=True).then_inc(e_br, 1)
                elif step == "KK":
                    pe.wait_ge(vb_ok, t + 1)
                    mm4(6, k, k, e_kk)
                    pe.wait_ge(dec_ok, t + 1)
                    pe.wait_ge(l_in["q"][b], 16 * i + 16)
                    mm4(7, k, q, e_kq)
                elif step == "INV":
                    pe.wait_ge(at_st, 4 * t + 4)
                    turn4(5, lambda h: xt[:, h, :], e_x0)
                elif step == "UW":
                    pe.wait_ge(c_xt, 6 * t + 6)
                    mm4(6, lambda h: xt[:, h, :], lambda h: vb[:, h, :], e_u)
                    mm4(5, lambda h: kbe[:, h, :], lambda h: xt[:, h, :], e_w)
                elif step == "PO":
                    pe.wait_ge(c_w, t + 1)
                    mm4(7, lambda h: wt[:, h, :], lambda h: st[:, h, :], e_p1)
                    mm4(5, q, lambda h: st[:, h, :], e_o1)
                elif step == "SO":
                    pe.wait_ge(vn_ok, t + 1)
                    mm4(7, lambda h: kd[:, h, :], lambda h: vn[:, h, :], e_sp)
                    pe.wait_ge(c_u, t + 1)
                    mm4(6, lambda h: kqd[:, h, :], lambda h: vn[:, h, :], e_o2)
                elif step == "OT":
                    pe.wait_ge(on_ok, t + 1)
                    pe.wait_ge(c_o1, t + 1)
                    turn4(5, lambda h: oo[:, h, :], e_ot)
                elif step[0] == "Y":
                    l = step[1]
                    pe.wait_ge(al_ok, 6 * t + l + 1)
                    pe.wait_ge(c_x, 6 * t + l)
                    mm4(6, lambda h: atl[:, l, h, :], lambda h: xx[:, h, :], e_y)
                elif step[0] == "X":
                    l = step[1]
                    pe.wait_ge(c_y, 6 * t + l)
                    if l == 1:
                        pe.wait_ge(kq_ok, t + 2)
                    else:
                        pe.wait_ge(c_xt, 6 * t + l - 1)
                    if l < 6:
                        mm4(5, lambda h: xt[:, h, :], lambda h: yy[:, h, :], e_xx)
                    mm4(7, lambda h: yy[:, h, :], lambda h: xt[:, h, :], e_xt)
                elif step[0] == "G":
                    j, c = divmod(step[1], 3)
                    if c == 0:
                        pe.wait_ge(w_lo, NPB + 2 * t + j + 3)
                    gate_chunk((NPB + j) % 2, c, UC + 6 * t + step[1])
                elif step[0] == "S":
                    j = step[1]
                    if j == 0:
                        pe.wait_ge(l_in["win"][b], 32 * i + 32)
                        pe.wait_ge(l_in["qa"][b], 16 * i + 16)
                        pe.wait_ge(a_pt, 8 * t + 1)
                        for w in range(2):
                            mm = pe.transpose(psum[:, 4, P * w:P * w + P], awin[:, b, 1, P * w:P * w + P], ident)
                        mm.then_inc(a_vt, 1)
                    if j == 4:
                        pe.wait_ge(l_in["qc"][b], 16 * i + 16)
                    pe.wait_ge(av_ok, 6 * t + j + 1)
                    if j < 4:
                        kv, g = j // 2, 2 * (j % 2)
                        for a in range(2):
                            pe.matmul(psum[:, 3, 256 * a:256 * a + 256], idb[:], mbf[:, b, :], start=True, stop=False)
                            mm = pe.matmul(psum[:, 3, 256 * a:256 * a + 256], ain[64 * kv:64 * kv + 64, b, g + a, :],
                                           awin[64 * kv:64 * kv + 64, b, 0, :], start=False, stop=True)
                    else:
                        for a in range(2):
                            h = 2 * (j - 4) + a
                            mm = pe.matmul(psum[:, 3, 256 * a:256 * a + 256], ain[:, b, 4 + h, :], mkT[:, h, :],
                                           start=True, stop=True)
                    mm.then_inc(a_s, 1)
                elif step[0] == "T":
                    j = step[1]
                    pe.wait_ge(a_e, 6 * t + j + 1)
                    pe.wait_ge(a_pt, 8 * t + QI[j] + 1)
                    if j == 0:
                        pe.wait_ge(a_vc, t + 1)
                    for a in range(2):
                        for w in range(2):
                            mm = pe.transpose(psum[:, 4, P * (2 * a + w):P * (2 * a + w) + P],
                                              pr[:, a, P * w:P * w + P], ident)
                    mm.then_inc(a_t, 1)
                elif step[0] == "V":
                    j = step[1]
                    pe.wait_ge(a_pt, 8 * t + QI[j] + 2)
                    for a in range(2):
                        w = AHD if j < 4 else P
                        for s in range(2):
                            rhs = vtok[:, s, 64 * (j // 2):64 * (j // 2) + 64] if j < 4 else \
                                mv[:, s, P * (2 * (j - 4) + a):P * (2 * (j - 4) + a) + P]
                            mm = pe.matmul(psum[:, 3, w * a:w * a + w], pt[:, 2 * a + s, :], rhs,
                                           start=(s == 0), stop=(s == 1))
                    mm.then_inc(a_v, 1)
                elif step[0] == "F":
                    f = step[1]
                    pe.wait_ge(a_on, 2 * t + f + 1)
                    pe.wait_ge(a_pt, 8 * t + (5, 8)[f])
                    for g in range(4):
                        mm = pe.transpose(psum[:, 4, P * g:P * g + P], oat[:, f, P * g:P * g + P], ident)
                    mm.then_inc(a_t, 1)

        def gate_chunk(slot, c, u):
            pe.wait_ge(g_ev, u + 1)
            for k in range(KT):
                for q, (a, h) in enumerate(((0, 0), (0, 1), (1, 0))):
                    mm = pe.matmul(psum[:, c, 0:CH], wsp[:, slot, a, k, :], actT[:, h, k, CH * c:CH * c + CH],
                                   start=(k == 0 and q == 0), stop=(k == KT - 1 and q == 2))
            mm.then_inc(g_mm, 1)

        with pe.Fori(0, 4) as i:
            for b in range(2):
                pe_tile(i, b)
        Dn = NS

        def gate_e(*chunks):
            for x in chunks:
                m = 16 + x // 3
                if x % 3 == 0:
                    pe.wait_ge(w_lo, NPB + m + 3)
                gate_chunk((NPB + m) % 2, x % 3, UC + 48 + x)

        pe.sem_inc(m_kt, 4)
        pe.sem_inc(m_sc, 1)
        gate_e(0, 1)
        pe.wait_ge(f_in, F_IN)

        def done(mm, name):
            mm.then_inc(f_pe, 1)

        for v in range(2):
            pe.transpose(psum[:, 5, P * v:P * v + P], lkv[:, v, :], ident)
            pe.transpose(psum[0:Dn, 5, 256 + P * v:256 + P * v + P], ext[:, v, :], ident)
        for n in range(12):
            mm = pe.transpose(psum[0:3 + NS, (3, 4, 6)[n // 4], P * (n % 4):P * (n % 4) + P], tail[:, n, :], ident)
        done(mm, "out")
        for b in range(4):
            mm = pe.transpose(psum[:, 7, P * b:P * b + P], wkv[:, 0, b, :], ident)
        done(mm, "win_kt0")
        gate_e(2)
        pe.wait_ge(f_ac, ACn("tail_out"))
        pe.wait_ge(f_dv, DVn("d3"))
        for h in range(BH):
            pe.transpose(psum[0:Dn, 3, P * h:P * h + P], dq[:, 4 + h, :], ident)
            pe.transpose(psum[0:Dn, 4, P * h:P * h + P], dq[:, 8 + h, :], ident)
        pe.matmul(psum[0:Dn, 5, 0:P], kc[0:Dn, K_D_GT:K_D_GT + NS], dug[:], start=True, stop=True)
        pe.matmul(psum[0:Dn, 5, P:2 * P], ones[0:Dn, 0:Dn], dia[:, 0], start=True, stop=True)
        pe.matmul(psum[:, 5, 2 * P:3 * P], ones[0:Dn, :], dia[:, 1], start=True, stop=True)
        pe.matmul(psum[:, 5, 3 * P:4 * P], ones[0:Dn, :], dia[:, 2], start=True, stop=True)
        pe.matmul(psum[:, 6, 0:P], ones[0:Dn, :], dia[:, 3], start=True, stop=True)
        for h in range(BH):
            pe.matmul(psum[0:Dn, 6, P + NS * h:P + NS * h + NS], dq[:, 4 + h, :], dq[:, 4 + h, :], start=True, stop=True)
            mm = pe.matmul(psum[0:Dn, 6, 2 * P + NS * h:2 * P + NS * h + NS], dq[:, 4 + h, :], dq[:, h, :], start=True, stop=True)
        done(mm, "bcast")
        pe.wait_ge(f_ac, ACn("wkT0"))
        for b in range(4):
            mm = pe.transpose(psum[:, 7, P * b:P * b + P], wkv[:, 0, 4 + b, :], ident)
        done(mm, "win_kt1")
        gate_e(3)
        pe.wait_ge(f_dv, DVn("el"))
        pe.wait_ge(f_ac, ACn("rq"))

        def mem_keys(b):
            pe.wait_ge(m_in[b % 2], 16 * (b // 2) + 16)
            for half, read in ((0, m_ka), (1, m_kd)):
                pe.wait_ge(read, b + 1)
                for x in range(4):
                    h, t = 2 * half + x // 2, x % 2
                    mm = pe.transpose(psum[:, 3 + half, P * x:P * x + P], ck[:, b % 2, t, P * h:P * h + P], ident)
                mm.then_inc(m_kt, 1)

        def mem_scores(b):
            pe.wait_ge(m_ka, b + 2)
            pe.wait_ge(m_kd, b + 2)
            for h in range(4):
                for t in range(2):
                    mm = pe.matmul(psum[:, 5, P * t + DS * h + 16 * b:P * t + DS * h + 16 * b + DS], ckT[:, h, P * t:P * t + P],
                                   da[:, 4 + h, DS * b:DS * b + DS], start=True, stop=True)
            mm.then_inc(m_sc, 1)

        def mem_values(b):
            pe.wait_ge(m_in[b % 2], 16 * (4 + b // 2) + 16)
            for h in range(4):
                for t in range(2):
                    mm = pe.matmul(psum[:, 6, 2 * P + NS * h + DS * b:2 * P + NS * h + DS * b + DS], ck[:, b % 2, t, P * h:P * h + P],
                                   mS[:, t, 16 * b + DS * h:16 * b + DS * h + DS], start=(t == 0), stop=(t == 1))
            if b < DB - 1:
                mm.then_inc(m_kt, 2)
            return mm

        def update(j):
            half, h = divmod(j, 4)
            pe.wait_ge(f_dv, DVn(f"vm{half}"))
            if j >= 3:
                pe.wait_ge(g_ad, j - 2)
            pe.matmul(psum[:, (3, 5, 4)[j % 3], :], dkd[:, h, :], vnm[:, h], start=True, stop=True).then_inc(g_up, 1)

        mem_keys(0)
        for b in range(DB):
            gate_e(4 + b)
            mem_scores(b)
            if b + 1 < DB:
                mem_keys(b + 1)
        pe.wait_ge(f_dv, DVn("xt0"))
        for h in range(BH):
            mm = pe.transpose(psum[0:Dn, 3, NS * h:NS * h + NS], dxt[:, h, :], ident[0:Dn, 0:Dn])
        done(mm, "x0")
        pe.wait_ge(f_ac, ACn("wkT1"))
        for v in range(2):
            rows = slice(64 * v, 64 * v + 64)
            bank = (4, 7)[v]
            for b in range(DB):
                pe.matmul(psum[:, bank, 0:P].rearrange("p (g b s) -> p g b s", g=4, b=DB)[:, :, b, :], wkT[rows, b, :],
                          da[rows, 0:4, DS * b:DS * b + DS], start=True, stop=True)
            mm = pe.matmul(psum[0:Dn, bank, 256:256 + P], ext[rows, 0, :], da[rows, 0:4, :], start=True, stop=True)
        done(mm, "new_sc")
        pe.wait_ge(f_ac, ACn("mem_s"))
        for t in range(2):
            mm = pe.transpose(psum[:, 6, P * t:P * t + P], mS[:, t, :], ident)
        done(mm, "mem_rows")
        gate_e(12)
        pe.wait_ge(f_dv, DVn("at1"))
        pe.wait_ge(f_ac, ACn("x0"))
        for h in range(BH):
            mm = pe.matmul(psum[0:Dn, 3, P + NS * h:P + NS * h + NS], dat1[:, h, :], dxx[:, h, :], start=True, stop=True)
        done(mm, "y")
        pe.wait_ge(f_ac, ACn("win_s"))
        for v in range(2):
            pe.transpose(psum[:, 5, 160 * v:160 * v + P], sS[:, v, :], ident)
            mm = pe.transpose(psum[:, 5, 160 * v + P:160 * v + 160], sS[0:Dn, 2 + v, :], ident[0:Dn, 0:Dn])
        done(mm, "win_rows")
        gate_e(13)
        pe.wait_ge(f_ac, ACn("y"))
        for h in range(BH):
            mm = pe.matmul(psum[0:Dn, 3, 2 * P + NS * h:2 * P + NS * h + NS], dyy[:, h, :], dxt[:, h, :], start=True, stop=True)
        done(mm, "xt")
        gate_e(14)
        pe.wait_ge(f_dv, DVn("mem_n"))
        for t in range(2):
            mm = pe.transpose(psum[:, 6, P * t:P * t + P], mR[:, P * t:P * t + P], ident)
        done(mm, "mem_pt")
        pe.wait_ge(f_dv, DVn("xt"))
        for h in range(BH):
            pe.matmul(psum[:, 4, NS * h:NS * h + NS], dvb[:, h, :], dxt[:, h, :], start=True, stop=True)
            mm = pe.matmul(psum[:, 4, P + NS * h:P + NS * h + NS], dkb[:, h, :], dxt[:, h, :], start=True, stop=True)
        done(mm, "u_w")
        gate_e(15)
        pe.wait_ge(f_dv, DVn("win_n"))
        for v in range(2):
            pe.transpose(psum[:, 5, P * v:P * v + P], sR[:, v, 0:P], ident)
            mm = pe.transpose(psum[0:Dn, 5, 256 + P * v:256 + P * v + P], sR[:, v, P:P + NS], ident)
        done(mm, "win_pt")
        pe.wait_ge(f_ac, ACn("mem_p"))
        mem_values(0)
        pe.wait_ge(f_dv, DVn("wT"))
        pe.wait_ge(s_in, 5 + 16 * DB)
        for b in range(DB):
            for h in range(BH):
                mm = pe.matmul(psum[:, 7, 64 * h + 8 * b:64 * h + 8 * b + 8], sd[:, b, h, :],
                               wq[:, h, b].rearrange("p a s -> p (a s)"), start=True, stop=True)
        done(mm, "w_q_s")
        mem_values(1)
        gate_e(16)
        pe.wait_ge(f_dv, DVn("vT"))
        for h in range(BH):
            mm = pe.transpose(psum[0:Dn, 4, P * h:P * h + P], dvT[:, h, :], ident)
        done(mm, "vn")
        mem_values(2)
        gate_e(17)
        pe.wait_ge(f_ac, ACn("win_p"))
        for b in range(DB):
            pe.matmul(psum[:, 3, 0:256].rearrange("p (a b s) -> p a b s", a=8, b=DB)[:, :, b, :], wkv[:, 1, b, :],
                      sS[:, 0:2, :].rearrange("p v (g b s) -> p (v g) b s", g=4, b=DB)[:, :, b, :], start=True, stop=True)
        mm = pe.matmul(psum[:, 3, 256:512], kvo[0:Dn, 1, 1, :], sS[0:Dn, 2:4, :], start=True, stop=True)
        done(mm, "win_o")
        pe.wait_ge(f_ac, ACn("vn"))
        pe.wait_ge(f_dv, DVn("qe"))
        for h in range(BH):
            mm = pe.matmul(psum[:, 7, 2 * P + NS * h:2 * P + NS * h + NS], dvn[:, h, :], dkq[:, h, :], start=True, stop=True)
        done(mm, "o")
        mem_values(3)
        gate_e(18)
        pe.wait_ge(f_ac, ACn("sq"))
        mm = pe.matmul(psum[:, 7, 3 * P:4 * P], ones, dsq[:], start=True, stop=True)
        done(mm, "sumsq")
        pe.wait_ge(f_dv, DVn("win_o1"))
        update(0)
        update(1)
        update(2)
        mem_values(4)
        gate_e(19)
        update(3)
        mem_values(5)
        for j in range(4, 7):
            update(j)
        mem_values(6)
        gate_e(20)
        update(7)
        done(mem_values(7), "mem_o")
        gate_e(21, 22, 23)
        pe.sem_inc(o_mm, 48)
        passes = ((0, 0), (0, 1), (1, 0))
        for j in range(12):
            n, a4 = NPD + j, 4 * ((j // 4) % 2)
            pe.wait_ge(w_lo, n + 3)
            for half in range(2):
                for c in range(3):
                    pe.wait_ge(g_ev, UD + 6 * j + 3 * half + c + 1)
                    for k in range(4):
                        if j % 4 == 0 and half == 0 and c == 0:
                            pe.wait_ge(b_lo, 1 + 4 * (j // 4) + k + 1)
                        for q, (a, h) in enumerate(passes):
                            mm = pe.matmul(psum[:, c, 0:CH], slab(wsp[:, :, a], n % 2)[:, k, P * half:P * half + P],
                                           actD[:, h, a4 + k, CH * c:CH * c + CH], start=(k == 0 and q == 0), stop=(k == 3 and q == 2))
                    mm.then_inc(g_mm, 1)

        def full_chunk(slot, c):
            for k in range(KT):
                for q, (a, h) in enumerate(passes):
                    mm = pe.matmul(psum[:, c, 0:CH], wsp[:, slot, a, k, :], actD[:, h, k, CH * c:CH * c + CH],
                                   start=(k == 0 and q == 0), stop=(k == KT - 1 and q == 2))
            mm.then_inc(g_mm, 1)

        def mix_chunk(slot, c, first):
            for m in range(KT):
                if first:
                    pe.wait_ge(b_lo, 13 + m + 1)
                for q, (a, h) in enumerate(passes):
                    mm = pe.matmul(psum[:, c, 0:CH], wsp[:, slot, a, m, :], actD[:, h, (m + 4) % 8, CH * c:CH * c + CH],
                                   start=(m == 0 and q == 0), stop=(m == KT - 1 and q == 2))
            mm.then_inc(g_mm, 1)

        for m in range(8):
            n = NPO + m
            pe.wait_ge(w_lo, n + 3)
            for c in range(3):
                pe.wait_ge(g_ev, UO + 3 * m + c + 1)
                mix_chunk(n % 2, c, m == 0 and c == 0)

        def turn_rows(t, slot, rows, col, ahead):
            pe.wait_ge(t_y, ahead)
            for k in range(KT):
                mm = pe.transpose(psum[0:rows, 2 * slot + k // 4, P * (k % 4):P * (k % 4) + P], accT[:, k, col:col + rows], ident)
            mm.then_inc(t_tr, 1)

        def turn_back(t, slot, rows):
            pe.wait_ge(u_xs, 2 + t + 1)
            pe.wait_ge(u_lo, t + 1)
            for k in range(KT):
                mm = pe.transpose(psum[:, 4 + 2 * slot + k // 4, P * (k % 4):P * (k % 4) + rows],
                                  xs2[0:rows, slot, P * k:P * k + P], ident[0:rows, 0:rows])
            mm.then_inc(u_tr, 1)

        pe.wait_ge(g_ev, 3 + UF)
        for t in range(NT + 3):
            if t <= NT:
                turn_rows(t, t % 2, P if t < NT else NS, P * t, t + 1)
            if t >= 2:
                turn_back(t - 2, t % 2, P if t - 2 < NT else NS)

        def in_panel(n, slot, read, before):
            pe.wait_ge(w_lo, n + 3)
            for c in range(3):
                pe.wait_ge(read, before + c + 1)
                full_chunk(slot, c)

        def out_panel(n, slot, i, fs):
            pe.wait_ge(w_lo, n + 3)
            pe.wait_ge(f_lo, 3 + 3 * i + 3)
            for m in range(KT):
                for c in range(3):
                    x = 3 * m + c
                    pe.wait_ge(o_ad, 24 * i + x + 1)
                    for q, (a, h) in enumerate(passes):
                        mm = pe.matmul(psum[:, 3 + x % 4, 0:CH], wsp[:, slot, a, m, :], fT[:, fs, h, CH * c:CH * c + CH],
                                       start=(q == 0), stop=(q == 2))
                    mm.then_inc(o_mm, 1)

        pe.wait_ge(u_lo, 2 + 9)
        pe.wait_ge(t_y, 2 + 9)
        in_panel(NPF, NPF % 2, f_fr, 0)
        in_panel(NPF + 1, (NPF + 1) % 2, g_ev, 3 + UF)

        def ffn_step(i, b):
            n, s = NPF + 3 * i - 1, (NPF + 3 * b - 1) % 2
            in_panel(n, s, f_fr, 3 * i)
            in_panel(n + 1, 1 - s, g_ev, 3 + UF + 3 * i)
            out_panel(n + 2, s, i - 1, (b - 1) % 2)

        with pe.Fori(0, (NF - 2) // 2) as i:
            for b in (1, 2):
                ffn_step(2 * i + b, b)
        ffn_step(NF - 1, 1)
        n = NPF + 3 * NF - 1
        out_panel(n, n % 2, NF - 1, 1)

        pe.wait_ge(o_ad, 4 + 24 * NF)
        for i in range(NT // 2):
            for b in range(2):
                turn_rows(9 + 2 * i + b, b, P, 2 * P * i + P * b, 2 * i + 10 + b)
        turn_rows(9 + NT, 0, NS, SEQ, 9 + NT + 1)

    @block.scalar
    def _(act):
        act.sem_inc(g_ev, 3)
        act.sem_inc(y_a, 2)

        def squares(n, slot, rows, landed):
            act.wait_ge(x_in[slot], landed)
            act.activation(xjunk[0:rows, :], xin[0:rows, slot, :], ACT.Square,
                           accum_out=rs[0:rows, slot, 0:1]).then_inc(x_sq, 1)

        def root(n, slot, rows):
            act.wait_ge(x_rs, 2 * n + 1)
            act.activation(rs[0:rows, slot, 2:3], rs[0:rows, slot, 1:2], ACT.Sqrt).then_inc(x_rt, 1)

        def hi_x(n, slot, rows, dst, col):
            act.wait_ge(x_tr, n + 1)
            act.activation(dst[:, 0, :, bass.ds(col, rows)],
                           psum[:, 2 * slot:2 * slot + 2, :].rearrange("p b (k t) -> p (b k) t", t=P)[:, :, 0:rows],
                           ACT.Copy).then_inc(x_hi, 1)

        act.wait_ge(sc_t, 1)
        act.activation(scT[:].rearrange("p n c -> p (n c)"), psum[:, 5, 0:336], ACT.Copy).then_inc(sc_c, 1)
        with act.Fori(0, NT // 2) as i:
            for b in range(2):
                squares(2 * i + b, b, P, 16 * i + 16)
                root(2 * i + b, b, P)
            for b in range(2):
                hi_x(2 * i + b, b, P, actT, 2 * P * i + P * b)
        for n, rows, _, _, dst, col in rest_tiles:
            squares(n, n % 2, rows, 16 * (n // 2) + 16)
            root(n, n % 2, rows)
            hi_x(n, n % 2, rows, dst, col)

        def evac_conv(n, slot):
            act.wait_ge(cv_st, 8 * n + 8)
            act.activation(by_step(cv[:, slot, 3 + SEQ:])[:, :, 0:3],
                           scT[:, bass.ds(n, 1), 0:24].rearrange("p a (b s) -> p (a b) s", b=DB), ACT.Copy)
            for c in range(3):
                act.wait_ge(g_mm, 6 + 3 * n + c + 1)
                w = CH if c < 2 else SEQ - 2 * CH
                if c == 2:
                    act.activation(by_step(cv[:, slot, 3 + SEQ:])[:, :, 3:7], by_step(psum[:, 2, w:CH]), ACT.Copy)
                    act.activation(cv[:, slot, 3 + CH * c:3 + CH * c + w], psum[:, c, 0:w], ACT.Copy).then_inc(cv_in, 1)
                    act.activation(tail[:, bass.ds(n, 1), :].rearrange("p a t -> p (a t)"),
                                   psum[:, 2, w - 3:CH], ACT.Copy).then_inc(g_ev, 1)
                else:
                    act.activation(cv[:, slot, 3 + CH * c:3 + CH * c + w], psum[:, c, 0:w], ACT.Copy).then_inc(g_ev, 1)

        def silu(n, slot, stored):
            act.wait_ge(cv_st, 16 + 8 * n + 8)
            act.wait_ge(y_st[slot], stored)
            act.activation(y2[:, slot, :], y[:, slot, :], ACT.Silu).then_inc(y_a, 1)

        def squares_of(n, slot):
            act.wait_ge(y_a, 2 + n + 1)
            act.wait_ge(ss_mm, n + 1)
            act.activation(sqb[:], y2[:, slot, :], ACT.Square).then_inc(sq_ok, 1)

        act.wait_ge(pad0, 5)
        act.wait_ge(sc_c, 1)
        evac_conv(0, 0)
        evac_conv(1, 1)
        with act.Fori(0, 4) as i:
            for b in range(2):
                evac_conv(2 * i + 2 + b, b)
                silu(2 * i + b, b, 16 * i + 16)
                squares_of(2 * i + b, b)
        for n in (10, 11):
            evac_conv(n, n % 2)
            silu(n - 2, n % 2, 16 * ((n - 2) // 2) + 16)

        def copy_row(n, dst_of, func, before=None):
            for c in range(3):
                act.wait_ge(g_mm, 6 + 3 * n + c + 1)
                if before is not None and c == 0:
                    act.wait_ge(*before)
                act.activation(dst_of(c), psum[:, c, 0:CH], func).then_inc(g_ev, 1)

        for n in range(B_Z, B_C):
            if n < B_Z + 2:
                silu(n - 2, n % 2, 16 * ((n - 2) // 2) + 16)
            copy_row(n, lambda c, n=n: y[:, n % 2, CH * c:CH * c + CH], ACT.Silu, (y_d, n - B_Z - 1) if n >= B_Z + 2 else (y_a, n + 1))
        for n in range(B_C, B_A):
            copy_row(n, lambda c, n=n: y2[:, n % 2, CH * c:CH * c + CH], ACT.Copy, (y_st[n % 2], 16 * (n // 2) + 16))
        act.wait_ge(ss_mm, 9)
        ssps = psum[:, 4, 0:8 * (NT + 1)].rearrange("p (n t) -> p n t", n=8)
        act.activation(ssq[:, :, 0:NT], ssps[:, :, 0:NT], ACT.Copy)
        act.activation(ssq[0:NS, :, NT:NT + 1], ssps[0:NS, :, NT:NT + 1], ACT.Copy).then_inc(ssq_ok, 1)
        for n in range(B_A, B_VA):
            act.wait_ge(y_d, (3, 4)[n - B_A] if n < B_A + 2 else YD(n - 2))
            for c in range(3):
                act.wait_ge(g_mm, 6 + 3 * n + c + 1)
                act.activation(y[:, n % 2, CH * c:CH * c + CH], psum[:, c, 0:CH], ACT.Copy)
                for quad in range(4):
                    mm = act.activation(cv[32 * quad:32 * quad + 32, n % 2, CH * c:CH * c + CH],
                                        psum[32 * (quad ^ 1):32 * (quad ^ 1) + 32, c, 0:CH], ACT.Copy)
                mm.then_inc(g_ev, 1)
        n = B_VA
        copy_row(n, lambda c: y2[:, 1, CH * c:CH * c + CH], ACT.Copy, (y_st[1], 16 * (n // 2) + 16))
        n = B_BA
        act.wait_ge(y_st[0], 16 * (n // 2) + 16)
        for c in range(3):
            act.wait_ge(g_mm, 6 + 3 * n + c + 1)
            act.activation(y2[0:8, 0, CH * c:CH * c + CH], psum[0:8, c, 0:CH], ACT.Copy).then_inc(g_ev, 1)
        act.wait_ge(y_d, YD(B_K))
        for j in range(8):
            act.wait_ge(g_mm, 6 + units(B_MEM + j) + 1)
            dst = mkT[:, j, :] if j < 4 else y[:, (j - 4) // 2, MEM * (j % 2):MEM * (j % 2) + MEM]
            act.activation(dst, psum[:, j % 3, 0:MEM], ACT.Copy).then_inc(g_ev, 1)
            if j == 0:
                act.wait_ge(mt, 1)
                act.activation(ba[:, 0:NT, :], psum[:, 5, 0:8 * NT].rearrange("p (t c) -> p t c", c=8), ACT.Copy)
                act.activation(ba[0:NS, NT, :], psum[0:NS, 5, 8 * NT:8 * NT + 8], ACT.Copy).then_inc(mc, 1)
            if j == 2:
                act.wait_ge(mc, 1)
                act.wait_ge(p_in, 64)
                act.activation(par[:, Q_BETA], ba[:, :, 0:4], ACT.Sigmoid).then_inc(pa, 1)
                act.wait_ge(pp, 2)
                act.activation(tmp[:, 2], tmp[:, 1], ACT.Exp, scale=-1.0).then_inc(pa, 1)
            if j == 3:
                act.wait_ge(pp, 3)
                act.activation(tmp[:, 4], tmp[:, 3], ACT.Ln).then_inc(pa, 1)
                act.activation(hp[:, 0, :], hp[:, 0, :], ACT.Exp).then_inc(pa, 1)
            if j == 6:
                act.wait_ge(pg, 1)
                act.wait_ge(st0, 1)
                for x, dst in enumerate((par[:, Q_EG], tmp[:, 2], egl[:])):
                    if x == 1:
                        act.wait_ge(pp, 6)
                    act.activation(dst[:, 0:NT, :], psum[:, 5, 36 * x:36 * x + 32].rearrange("p (t h) -> p t h", h=BH), ACT.Exp).then_inc(pa, 1)
                    act.activation(dst[0:NS, NT, :], psum[0:NS, 5, 36 * x + 32:36 * x + 36], ACT.Exp).then_inc(pa, 1)
                act.wait_ge(pp, 11)
                act.activation(rr[:, 1], rr[:, 0], ACT.Sqrt).then_inc(pa, 1)
        for s in range(2):
            for v in range(2):
                j = 2 * s + v
                act.wait_ge(mt, 1 + j + 1)
                act.activation(mout[:, s, :] if v == 0 else mv[:, s, :], psum[:, 5 + j % 2, :], ACT.Copy).then_inc(mc, 1)
        for c in range(3):
            act.sem_inc(gs_st[c], 16)
        act.sem_inc(a_st[0], 16)
        act.sem_inc(a_st[1], 16)
        act.sem_inc(a_pt, 1)
        act.wait_ge(mc, 1 + 4)
        act.wait_ge(o_st, 64)
        act.wait_ge(k_in, 16)
        act.activation(idb[:], ident, ACT.Copy).then_inc(st0, 1)
        act.activation(snk[:, 1, :], snk[:, 0, :], ACT.Copy, scale=-1.0).then_inc(st0, 1)

        def act_tile(i, b):
            t = 2 * i + b

            def copy(waits, dst, src, done):
                act.wait_ge(*waits)
                act.activation(dst, src, ACT.Copy).then_inc(done, 1)

            for step in TILE:
                if step == "DEC":
                    act.wait_ge(e_gt, t + 1)
                    act.wait_ge(dm_ok, t + 1)
                    act.activation(dec[:].rearrange("p h i -> p (h i)"), psum[:, 7, :], ACT.Exp).then_inc(dec_ok, 1)
                elif step == "INV":
                    copy((e_x0, t + 1), xx[:].rearrange("p h i -> p (h i)"), psum[:, 5, :], c_x)
                elif step == "UW":
                    copy((e_u, t + 1), uu[:].rearrange("p h i -> p (h i)"), psum[:, 6, :], c_u)
                    copy((e_w, t + 1), wt[:].rearrange("p h i -> p (h i)"), psum[:, 5, :], c_w)
                elif step == "SO":
                    act.wait_ge(c_o, t + 2)
                    for h in range(BH):
                        mm = act.activation(dec[:, h, :], oo[:, h, :], ACT.Square, accum_out=osm[:, 0, h:h + 1])
                    mm.then_inc(o_sq, 1)
                elif step == "N1":
                    act.wait_ge(o_st1, 5 * t + 3)
                    act.activation(osm[:, 2, :], osm[:, 1, :], ACT.Sqrt).then_inc(o_rt, 1)
                elif step[0] == "Y":
                    copy((e_y, 6 * t + step[1]), yy[:].rearrange("p h i -> p (h i)"), psum[:, 6, :], c_y)
                elif step[0] == "G":
                    j, c = divmod(step[1], 3)
                    act.wait_ge(gs_st[c], 16 * (2 * t + j) + 16)
                    copy((g_mm, 6 + UC + 6 * t + step[1] + 1), gst[:, c], psum[:, c, 0:CH], g_ev)
                elif step[0] == "S":
                    j = step[1]
                    if j == 0:
                        copy((a_vt, t + 1), vtok[:].rearrange("p a d -> p (a d)"), psum[:, 4, 0:2 * P], a_vc)
                    act.wait_ge(a_nm, 6 * t + j + 1)
                    for a in range(2):
                        mm = act.activation(pr[:, a, :], psum[:, 3, 256 * a:256 * a + 256], ACT.Exp, scale=A_SC[j],
                                            bias=asm[:, S_NM, 2 * j + a:2 * j + a + 1],
                                            accum_out=asm[:, S_SM, 2 * j + a:2 * j + a + 1])
                    mm.then_inc(a_e, 1)
                elif step[0] == "T":
                    copy((a_t, 8 * t + QI[step[1]] + 1), pt[:].rearrange("p a d -> p (a d)"), psum[:, 4, :], a_pt)
                elif step == ("D", 0):
                    act.wait_ge(a_sk, 4 * t + 4)
                    act.activation(asm[:, S_ES, 0:8], asm[:, S_SK, 0:8], ACT.Exp).then_inc(a_es, 1)
                elif step[0] == "F":
                    f = step[1]
                    act.wait_ge(a_st[f], 16 * t + 16)
                    copy((a_t, 8 * t + (5, 8)[f]), oba[:, f].rearrange("p a d -> p (a d)"), psum[:, 4, :], a_pt)
                    act.wait_ge(a_pt, 8 * t + (5, 8)[f] + 1)
                    act.dma_start(s_br[8 * f:8 * f + 4].rearrange("n p t -> p n t")[:, :, bass.ds(P * t, P)],
                                  oba[:, f]).then_inc(a_st[f], 16)

        with act.Fori(0, 4) as i:
            for b in range(2):
                act_tile(i, b)
        Dn = NS
        act.sem_inc(m_ka, 1)

        def fdone(op, name):
            op.then_inc(f_ac, 1)

        def copy_e(name, dst, src, after):
            act.wait_ge(f_pe, PEn(after))
            fdone(act.activation(dst, src, ACT.Copy), name)

        def gates(*chunks):
            for x in chunks:
                c, u = x % 3, UC + 48 + x
                act.wait_ge(gs_st[c], 16 * (16 + x // 3) + 16)
                act.wait_ge(g_mm, 6 + u + 1)
                act.activation(gst[:, c], psum[:, c, 0:CH], ACT.Copy).then_inc(g_ev, 1)
                act.wait_ge(g_ev, 3 + u + 1)
                act.dma_start(s_gate[16 + x // 3][:, CH * c:CH * c + CH], gst[:, c]).then_inc(gs_st[c], 16)

        flat = lambda ap: ap.rearrange("p h i -> p (h i)")
        gates(0, 1)
        copy_e("kv_out", kvo[:, 0].rearrange("p v d -> p (v d)"), psum[:, 5, 0:256], "out")
        copy_e("new_out", kvo[0:Dn, 1].rearrange("p v d -> p (v d)"), psum[0:Dn, 5, 256:512], "out")
        act.activation(tlo[:, 0:8 * P], psum[0:3 + NS, 3:5, :].rearrange("p b n -> p (b n)"), ACT.Copy)
        copy_e("tail_out", tlo[:, 8 * P:12 * P], psum[0:3 + NS, 6, :], "out")
        copy_e("wkT0", wkT[:, 0:4].rearrange("p b s -> p (b s)"), psum[:, 7, :], "win_kt0")
        gates(2)
        act.wait_ge(f_pe, PEn("bcast"))
        fdone(act.activation(flat(ddc[:]), psum[0:Dn, 5, 0:P], ACT.Exp), "dec")
        fdone(act.activation(flat(dnm[:]), psum[:, 5, 3 * P:4 * P], ACT.Copy), "rq")
        copy_e("wkT1", wkT[:, 4:8].rearrange("p b s -> p (b s)"), psum[:, 7, :], "win_kt1")
        gates(3)
        for b in range(DB):
            act.wait_ge(m_kt, 4 + 2 * b + 1)
            act.wait_ge(m_sc, b + 1)
            act.activation(ckT[:, 0:2, :].rearrange("p h k -> p (h k)"), psum[:, 3, :], ACT.Copy).then_inc(m_ka, 1)
            gates(4 + b)
        act.wait_ge(m_sc, 1 + DB)
        fdone(act.activation(flat(mS[:]), psum[:, 5, 0:256], ACT.Copy), "mem_s")
        copy_e("x0", flat(dxx[:]), psum[0:Dn, 3, 0:P], "x0")
        act.wait_ge(f_pe, PEn("new_sc"))
        for v in range(2):
            act.activation(sS[:, v, :], psum[:, (4, 7)[v], 0:P], ACT.Copy)
            mm = act.activation(sS[0:Dn, 2 + v, :], psum[0:Dn, (4, 7)[v], 256:256 + P], ACT.Copy)
        fdone(mm, "win_s")
        gates(12)
        copy_e("y", flat(dyy[:]), psum[0:Dn, 3, P:2 * P], "y")
        act.wait_ge(f_dv, DVn("mem_nm"))
        fdone(act.activation(mR[:], psum[:, 6, 0:256], ACT.Exp, scale=P ** -0.5, bias=dsm[:, 1:2], accum_out=dsm[:, 2:3]), "mem_exp")
        gates(13)
        act.wait_ge(f_dv, DVn("win_nm"))
        for v in range(2):
            mm = act.activation(sR[:, v, :], sR[:, v, :], ACT.Exp, scale=AHD ** -0.5, bias=dsm[:, 6 + v:7 + v], accum_out=dsm[:, 8 + v:9 + v])
        fdone(mm, "win_exp")
        act.wait_ge(f_dv, DVn("win_sk"))
        fdone(act.activation(dsm[:, 12:14], dsm[:, 10:12], ACT.Exp), "win_sk")
        gates(14)
        copy_e("mem_p", flat(mS[:]), psum[:, 6, 0:256], "mem_pt")
        gates(15)
        act.wait_ge(f_pe, PEn("win_pt"))
        act.activation(flat(sS[:, 0:2, :]), psum[:, 5, 0:256], ACT.Copy)
        fdone(act.activation(flat(sS[0:Dn, 2:4, :]), psum[0:Dn, 5, 256:512], ACT.Copy), "win_p")
        gates(16)
        copy_e("vn", flat(dvn[:]), psum[0:Dn, 4, :], "vn")
        gates(17)
        act.wait_ge(f_dv, DVn("o_"))
        fdone(act.activation(dsq[:], dqe[:], ACT.Square), "sq")
        gates(18)
        act.wait_ge(f_dv, DVn("n2"))
        fdone(act.activation(dsq[:], duT[:], ACT.Sqrt), "root")
        gates(*range(19, 24))
        def hi_br(r, k):
            act.wait_ge(b_in, 16 * r + 16)
            if k == 0:
                act.wait_ge(g_mm, 6 + UD + (24 if r == 2 else 0))
            act.activation(actD[:, 0, 4 * (r % 2) + k, :], brw[:, k], ACT.Copy).then_inc(b_hi, 1)

        for k in range(4):
            hi_br(0, k)
        for j in range(12):
            for half in range(2):
                if (j, half) in BR_AT:
                    hi_br(*BR_AT[j, half])
            act.wait_ge(q_in[j % 2], 16 * (j // 2) + 16)
            act.activation(gat[:, j % 2], gat[:, j % 2], ACT.Sigmoid).then_inc(q_sg, 1)
        for m in range(8):
            act.wait_ge(q_mx, 12 + 48 + 3 * m + 3)
            if m == 4:
                act.wait_ge(g_mm, 6 + UO)
            act.activation(actD[:, 0, (m + 4) % 8, :], accT[:, m, :], ACT.Copy).then_inc(b_hi, 1)
        for m in range(8):
            if m == 0:
                act.wait_ge(b_lo, 21)
            for c in range(3):
                act.wait_ge(g_mm, 6 + UO + 3 * m + c + 1)
                act.activation(accT[:, m, CH * c:CH * c + CH], psum[:, c, 0:CH], ACT.Copy).then_inc(g_ev, 1)

        def rows_psum(slot, rows):
            return psum[0:rows, 2 * slot:2 * slot + 2, :].rearrange("p b n -> p (b n)")

        def norm1(t, slot, rows):
            act.wait_ge(t_tr, t + 1)
            act.activation(jk[0:rows, slot, :], rows_psum(slot, rows), ACT.Square, accum_out=ns[0:rows, slot, 0, 0:1]).then_inc(t_sq, 1)

        def root1(t, slot, rows):
            act.wait_ge(t_ms, t + 1)
            act.activation(ns[0:rows, slot, 0, 2:3], ns[0:rows, slot, 0, 1:2], ACT.Sqrt).then_inc(t_rt, 1)

        def norm2(t, slot, rows):
            act.wait_ge(t_x1, t + 1)
            act.activation(jk[0:rows, slot, :], xr[0:rows, slot, :], ACT.Square, accum_out=ns[0:rows, slot, 1, 0:1]).then_inc(u_sq, 1)

        def root2(t, slot, rows):
            act.wait_ge(u_ms, t + 1)
            act.activation(ns[0:rows, slot, 1, 2:3], ns[0:rows, slot, 1, 1:2], ACT.Sqrt).then_inc(u_rt, 1)

        def hi_back(t, slot, rows, col):
            act.wait_ge(u_tr, t + 1)
            act.activation(actD[:, 0, :, bass.ds(col, rows)],
                           psum[:, 4 + 2 * slot:6 + 2 * slot, :].rearrange("p b (k t) -> p (b k) t", t=P)[:, :, 0:rows], ACT.Copy).then_inc(u_hi, 1)

        def norms(t, b, first=P, second=P, third=P):
            if first:
                norm1(t + 1, 1 - b, first)
                root1(t + 1, 1 - b, first)
            if third:
                hi_back(t - 1, 1 - b, third, P * t - P)
            if second:
                norm2(t, b, second)
                root2(t, b, second)

        act.wait_ge(b_in, 96)
        norms(-1, 1, second=0, third=0)
        norms(0, 0, third=0)
        with act.Fori(0, (NT - 2) // 2) as i:
            for b in (1, 2):
                norms(2 * i + b, b % 2)
        norms(NT - 1, 1, first=NS)
        norms(NT, 0, first=0, second=NS)
        norms(NT + 1, 1, first=0, second=0, third=NS)

        def gt_panel(u, i):
            for c in range(3):
                act.wait_ge(g_mm, 6 + UF + u + c + 1)
                if c == 0:
                    act.wait_ge(f_fr, 3 * i + 3)
                act.activation(sg[:, CH * c:CH * c + CH], psum[:, c, 0:CH], ACT.Silu).then_inc(g_ev, 1)

        act.sem_inc(f_hi, 3)

        def hi_f(i, fs):
            act.wait_ge(o_mm, 24 * i + 24)
            for c in range(3):
                act.wait_ge(f_fr, 3 + 3 * i + c + 1)
                act.activation(fT[:, fs, 0, CH * c:CH * c + CH], fr[:, CH * c:CH * c + CH], ACT.Copy).then_inc(f_hi, 1)

        with act.Fori(0, NF // 2) as i:
            for b in range(2):
                gt_panel(12 * i + 6 * b, 2 * i + b)
                hi_f(2 * i + b, b)
        with act.Fori(0, NT // 2) as i:
            for f in (norm1, root1):
                for b in range(2):
                    f(9 + 2 * i + b, b, P)
        norm1(9 + NT, 0, NS)
        root1(9 + NT, 0, NS)

    @block.vector
    def _(dve):
        dve.sem_inc(x_lo, 2)
        dve.sem_inc(cv_st, 16)
        dve.wait_ge(k_in, 16 * 6)

        def norm(n, slot, rows, gain):
            dve.wait_ge(x_sq, n + 1)
            dve.tensor_scalar(rs[0:rows, slot, 1:2], rs[0:rows, slot, 0:1], 1.0 / D, EPS, ALU.mult, ALU.add).then_inc(x_rs, 1)
            dve.wait_ge(x_rt, n + 1)
            dve.reciprocal(rs[0:rows, slot, 3:4], rs[0:rows, slot, 2:3]).then_inc(x_rs, 1)
            dve.wait_ge(x_rs, 2 * n + 2)
            dve.scalar_tensor_tensor(out=xs[0:rows, slot, :], in0=xin[0:rows, slot, :], scalar=rs[0:rows, slot, 3:4],
                                     in1=gbc[0:rows, gain, :], op0=ALU.mult, op1=ALU.mult).then_inc(x_nm, 1)

        def lo_x(n, slot, rows, dst, col):
            dve.wait_ge(x_hi, n + 1)
            src = psum[:, 2 * slot:2 * slot + 2, :].rearrange("p b (k t) -> p (b k) t", t=P)[:, :, 0:rows]
            dve.tensor_tensor(dst[:, 1, :, bass.ds(col, rows)], src, dst[:, 0, :, bass.ds(col, rows)].bitcast(F32),
                              ALU.subtract).then_inc(x_lo, 1)

        with dve.Fori(0, NT // 2) as i:
            for b in range(2):
                norm(2 * i + b, b, P, 0)
            for b in range(2):
                lo_x(2 * i + b, b, P, actT, 2 * P * i + P * b)
        for n, rows, _, gain, dst, col in rest_tiles:
            norm(n, n % 2, rows, gain)
            lo_x(n, n % 2, rows, dst, col)

        def conv(n, slot):
            dve.wait_ge(cv_in, n + 1)
            dve.wait_ge(y_a, n + 1)
            dst = (y[:, slot, 0:SEQ], by_step(y[:, slot, SEQ:N]))
            for tap in range(CW):
                src = (cv[:, slot, tap:tap + SEQ], by_step(cv[:, slot, 3 + SEQ:])[:, :, tap:tap + DS])
                w = scT[:, bass.ds(n, 1), 24 + tap]
                for part in range(2):
                    if tap == 0:
                        op = dve.tensor_scalar(dst[part], src[part], w, None, ALU.mult)
                    else:
                        dve.wait_ge(cv_st, 16 + 8 * n + 2 * tap + part - 1)
                        op = dve.scalar_tensor_tensor(out=dst[part], in0=src[part], scalar=w, in1=dst[part],
                                                      op0=ALU.mult, op1=ALU.add)
                    op.then_inc(cv_st, 1)

        with dve.Fori(0, 6) as i:
            for b in range(2):
                conv(2 * i + b, b)
        for n in range(B_Z, B_C):
            dve.wait_ge(g_ev, 3 + 3 * n + 3)
            dve.wait_ge(y_st[n % 2], 16 * (n // 2) + 16)
            dve.tensor_scalar(y2[:, n % 2, :], y[:, n % 2, :], nw[:, 0:1], None, ALU.mult).then_inc(y_d, 1)
        dve.wait_ge(k_in, 16 * 7)
        for n in range(B_A, B_VA):
            dve.wait_ge(g_ev, 3 + 3 * n + 3)
            dve.wait_ge(y_st[n % 2], 16 * (n // 2) + 16)
            dve.tensor_tensor(y2[:, n % 2, :], y[:, n % 2, :], rope[:, 0, :], ALU.mult).then_inc(y_d, 1)
            dve.tensor_tensor(cv[:, n % 2, 0:N], cv[:, n % 2, 0:N], rope[:, 1, :], ALU.mult).then_inc(y_d, 1)
            dve.wait_ge(y_d, YD(n) - 1)
            dve.tensor_tensor(y2[:, n % 2, :], y2[:, n % 2, :], cv[:, n % 2, 0:N], ALU.add).then_inc(y_d, 1)
        dve.sem_inc(kq_ok, 1)
        dve.sem_inc(al_ok, 1)
        dve.sem_inc(c_o, 1)
        dve.sem_inc(c_s, 1)
        dve.sem_inc(av_ok, 1)
        dve.sem_inc(ob_st, 16)

        class Chain:
            n = 0

        def pstep(op):
            Chain.n += 1
            op.then_inc(pp, 1)
            dve.wait_ge(pp, Chain.n)

        allp = [P, NT + 1, BH]
        dve.wait_ge(mc, 1)
        dve.wait_ge(p_in, 64)
        dve.memset(par[:, Q_EG], 0.0).then_inc(st0, 1)
        pstep(dve.tensor_tensor(tmp[:, 0], ba[:, :, 4:8], hp[:, 1, :].unsqueeze(1).to_broadcast(allp), ALU.add))
        pstep(dve.scalar_tensor_tensor(out=tmp[:, 1], in0=tmp[:, 0], scalar=-1.0, in1=tmp[:, 0], op0=ALU.mult, op1=ALU.max))
        dve.wait_ge(pa, 2)
        pstep(dve.tensor_scalar(tmp[:, 3], tmp[:, 2], 1.0, None, ALU.add))
        pstep(dve.reciprocal(tmp[:, 5], tmp[:, 3]))
        pstep(dve.tensor_scalar(tmp[:, 1], tmp[:, 3], 1.0, None, ALU.subtract))
        pstep(dve.tensor_tensor(tmp[:, 1], tmp[:, 2], tmp[:, 1], ALU.subtract))
        pstep(dve.tensor_tensor(tmp[:, 1], tmp[:, 1], tmp[:, 5], ALU.mult))
        dve.wait_ge(pa, 4)
        pstep(dve.tensor_tensor(tmp[:, 1], tmp[:, 1], tmp[:, 4], ALU.add))
        pstep(dve.scalar_tensor_tensor(out=tmp[:, 0], in0=tmp[:, 0], scalar=0.0, in1=tmp[:, 1], op0=ALU.max, op1=ALU.add))
        pstep(dve.scalar_tensor_tensor(out=par[:, Q_G], in0=tmp[:, 0], scalar=-1.0,
                                       in1=hp[:, 0, :].unsqueeze(1).to_broadcast(allp), op0=ALU.mult, op1=ALU.mult))
        dve.wait_ge(ssq_ok, 1)
        pstep(dve.tensor_scalar(rr[:, 0], ssq[:], EPS, None, ALU.add))
        dve.wait_ge(pa, 11)
        pstep(dve.reciprocal(rr[:, 0], rr[:, 1]))
        pstep(dve.tensor_copy(par[:, Q_RK], rr[:, 0, 4:8, :].rearrange("p h t -> p t h")))
        pstep(dve.tensor_scalar(par[:, Q_RQ], rr[:, 0, 0:4, :].rearrange("p h t -> p t h"), P ** -0.5, None, ALU.mult))
        pstep(dve.tensor_tensor(par[:, Q_BK], par[:, Q_BETA], par[:, Q_RK], ALU.mult))
        pstep(dve.tensor_tensor(par[:, Q_BKE], par[:, Q_BK], par[:, Q_EG], ALU.mult))
        pstep(dve.tensor_tensor(par[:, Q_KD], tmp[:, 2], par[:, Q_RK], ALU.mult))
        dve.wait_ge(mc, 1 + 4)
        dve.wait_ge(o_st, 64)
        dve.wait_ge(st0, 3)

        def head4(bank):
            return psum[:, bank, :].rearrange("p (h i) -> p h i", h=BH)

        def dve_tile(i, b):
            t = 2 * i + b
            for step in TILE:
                if step == "KV":
                    dve.wait_ge(e_tk, t + 1)
                    dve.tensor_tensor(kbe[:], head4(5), bc_c(per(Q_BKE, t)), ALU.mult)
                    dve.tensor_tensor(kd[:], head4(5), bc_c(per(Q_KD, t)), ALU.mult).then_inc(kd_ok, 1)
                    dve.wait_ge(e_tv, t + 1)
                    dve.tensor_tensor(vb[:], head4(6), bc_c(per(Q_BETA, t)), ALU.mult).then_inc(vb_ok, 1)
                elif step == "DEC":
                    dve.wait_ge(dec_ok, t + 1)
                    dve.wait_ge(mrk_ok, t + 1)
                    dve.wait_ge(kq_ok, t + 1)
                    dve.tensor_tensor(decm[:], dec[:], mrk[:], ALU.mult).then_inc(dm_ok, 1)
                elif step == "KK":
                    dve.wait_ge(dm_ok, t + 2)
                    dve.wait_ge(al_ok, 6 * t + 1)
                    dve.wait_ge(e_kk, t + 1)
                    dve.tensor_tensor(at[:], head4(6), decm[:], ALU.mult).then_inc(at_st, 1)
                    dve.wait_ge(e_br, t + 1)
                    dve.wait_ge(at_st, 4 * t + 1)
                    dve.tensor_tensor(at[:], at[:], head4(5), ALU.mult).then_inc(at_st, 1)
                    dve.wait_ge(e_kq, t + 1)
                    dve.tensor_tensor(kqd[:], head4(7), decm[:], ALU.mult).then_inc(kq_ok, 1)
                    dve.wait_ge(at_st, 4 * t + 2)
                    for l in range(NLV):
                        m = bc_h(kc[:, K_LV + P * l:K_LV + P * l + P])
                        if l == 0:
                            dve.tensor_tensor(xt[:], at[:], m, ALU.mult).then_inc(at_st, 1)
                            dve.wait_ge(at_st, 4 * t + 3)
                            dve.tensor_tensor(xt[:], bc_h(ident), xt[:], ALU.subtract).then_inc(at_st, 1)
                        else:
                            dve.tensor_tensor(atl[:, l], at[:], m, ALU.mult).then_inc(al_ok, 1)
                elif step == "PO":
                    dve.wait_ge(c_u, t + 1)
                    dve.wait_ge(e_p1, t + 1)
                    dve.tensor_tensor(vn[:], uu[:], head4(7), ALU.subtract).then_inc(vn_ok, 1)
                    dve.wait_ge(e_o1, t + 1)
                    dve.wait_ge(c_o, t + 1)
                    dve.tensor_tensor(o1s[:], head4(5), bc_c(per(Q_EG, t)), ALU.mult).then_inc(c_o1, 1)
                    dve.wait_ge(c_s, t + 1)
                    dve.tensor_tensor(st[:], st[:], bc_c(egl[:, bass.ds(t, 1), :]), ALU.mult).then_inc(c_sm, 1)
                elif step == "SO":
                    dve.wait_ge(e_sp, t + 1)
                    dve.wait_ge(c_sm, t + 1)
                    dve.tensor_tensor(st[:], st[:], head4(7), ALU.add).then_inc(c_s, 1)
                    dve.wait_ge(e_o2, t + 1)
                    dve.wait_ge(c_o1, t + 1)
                    dve.tensor_tensor(oo[:], o1s[:], head4(6), ALU.add).then_inc(c_o, 1)
                elif step == "N1":
                    dve.wait_ge(o_sq, t + 1)
                    rq = per(Q_RQ, t).rearrange("p a h -> p (a h)")
                    dve.tensor_tensor(osm[:, 1, :], osm[:, 0, :], rq, ALU.mult).then_inc(o_st1, 1)
                    dve.wait_ge(o_st1, 5 * t + 1)
                    dve.tensor_tensor(osm[:, 1, :], osm[:, 1, :], rq, ALU.mult).then_inc(o_st1, 1)
                    dve.wait_ge(o_st1, 5 * t + 2)
                    dve.tensor_scalar(osm[:, 1, :], osm[:, 1, :], 1.0 / P, EPS, ALU.mult, ALU.add).then_inc(o_st1, 1)
                elif step == "N2":
                    dve.wait_ge(o_rt, t + 1)
                    rq = per(Q_RQ, t).rearrange("p a h -> p (a h)")
                    dve.reciprocal(osm[:, 3, :], osm[:, 2, :]).then_inc(o_st1, 1)
                    dve.wait_ge(o_st1, 5 * t + 4)
                    dve.tensor_tensor(osm[:, 4, :], osm[:, 3, :], rq, ALU.mult).then_inc(o_st1, 1)
                    dve.wait_ge(o_st1, 5 * t + 5)
                    dve.tensor_tensor(oo[:], oo[:], osm[:, 4, :].unsqueeze(2).to_broadcast([P, BH, P]), ALU.mult).then_inc(on_ok, 1)
                elif step == "OT":
                    dve.wait_ge(e_ot, t + 1)
                    dve.wait_ge(l_in["z"][b], 16 * i + 16)
                    dve.wait_ge(ob_st, 16 * t + 16)
                    dve.tensor_tensor(obb[:], head4(5), gin[:, b, 12:16, :], ALU.mult).then_inc(c_ob, 1)
                elif step[0] == "X":
                    l = step[1]
                    if l < 6:
                        dve.wait_ge(e_xx, 5 * t + l)
                        dve.tensor_tensor(xx[:], xx[:], head4(5), ALU.subtract).then_inc(c_x, 1)
                    dve.wait_ge(e_xt, 6 * t + l)
                    dve.tensor_tensor(xt[:], xt[:], head4(7), ALU.subtract).then_inc(c_xt, 1)
                elif step[0] == "S":
                    j = step[1]
                    cols = slice(2 * j, 2 * j + 2)
                    dve.wait_ge(a_s, 6 * t + j + 1)
                    dve.tensor_reduce(asm[:, S_MX, cols], psum[:, 3, :].rearrange("p (a k) -> p a k", a=2), AX.X, ALU.max).then_inc(a_mx, 1)
                    dve.wait_ge(a_mx, 6 * t + j + 1)
                    if j < 4:
                        dve.scalar_tensor_tensor(out=asm[:, S_NM, cols], in0=asm[:, S_MX, cols], scalar=-A_SC[j],
                                                 in1=snk[:, 1, cols], op0=ALU.mult, op1=ALU.min).then_inc(a_nm, 1)
                        dve.wait_ge(a_nm, 6 * t + j + 1)
                        dve.tensor_tensor(asm[:, S_SK, cols], asm[:, S_NM, cols], snk[:, 0, cols], ALU.add).then_inc(a_sk, 1)
                    else:
                        dve.tensor_scalar(asm[:, S_NM, cols], asm[:, S_MX, cols], -A_SC[j], None, ALU.mult).then_inc(a_nm, 1)
                elif step[0] == "V":
                    j = step[1]
                    dve.wait_ge(a_v, 6 * t + j + 1)
                    if j < 4:
                        dst = oat[:, 0, :].rearrange("p (g v d) -> p g v d", g=4, v=2)[:, 2 * (j % 2):2 * (j % 2) + 2, j // 2]
                        src = psum[:, 3, 0:P].rearrange("p (g d) -> p g d", g=2)
                    else:
                        dst, src = oat[:, 1, 256 * (j - 4):256 * (j - 4) + 256], psum[:, 3, 0:2 * P]
                    dve.tensor_copy(dst, src).then_inc(av_ok, 1)
                elif step[0] == "D":
                    f = step[1]
                    cols, heads, w = ((slice(0, 8), 8, AHD), (slice(8, 12), 4, P))[f]
                    if f == 0:
                        dve.wait_ge(a_es, t + 1)
                        dve.tensor_tensor(asm[:, S_DEN, cols], asm[:, S_SM, cols], asm[:, S_ES, cols], ALU.add).then_inc(a_dn, 1)
                    else:
                        dve.tensor_copy(asm[:, S_DEN, cols], asm[:, S_SM, cols]).then_inc(a_dn, 1)
                    dve.wait_ge(a_dn, 4 * t + 2 * f + 1)
                    dve.reciprocal(asm[:, S_RD, cols], asm[:, S_DEN, cols]).then_inc(a_dn, 1)
                    dve.wait_ge(a_dn, 4 * t + 2 * f + 2)
                    dve.wait_ge(av_ok, 6 * t + (5, 7)[f])
                    if f == 0:
                        o = oat[:, 0, :].rearrange("p (g v d) -> p g v d", g=4, v=2)
                        rd = asm[:, S_RD, cols].rearrange("p (v g) -> p g v", v=2).unsqueeze(3).to_broadcast([P, 4, 2, w])
                    else:
                        o = oat[:, 1, :].rearrange("p (h d) -> p h d", d=w)
                        rd = asm[:, S_RD, cols].unsqueeze(2).to_broadcast([P, heads, w])
                    dve.tensor_tensor(o, o, rd, ALU.mult).then_inc(a_on, 1)

        with dve.Fori(0, 4) as i:
            for b in range(2):
                dve_tile(i, b)
        Dn = NS
        dve.sem_inc(m_kd, 1)
        dve.wait_ge(f_in, F_IN)

        def f(name, op):
            op.then_inc(f_dv, 1)

        own = lambda name: dve.wait_ge(f_dv, DVn(name))
        dP = lambda q: par[0:Dn, q, NT, :].unsqueeze(2).to_broadcast([Dn, BH, NS])
        dW = lambda q: par[0:Dn, q, NT, :].unsqueeze(2).to_broadcast([Dn, BH, P])
        bD = lambda ap: ap.unsqueeze(1).to_broadcast([Dn, BH, NS])
        q4 = lambda bank, j, rows=Dn: psum[0:rows, bank, P * j:P * j + P].rearrange("p (h i) -> p h i", h=BH)
        le, idd = bD(kc[0:Dn, K_D_LE:K_D_LE + NS]), bD(ident[0:Dn, 0:Dn])
        f("ug", dve.tensor_tensor(dug[:], le, dP(Q_G), ALU.mult))
        f("d0", dve.tensor_tensor(dia[:, 0], idd, dP(Q_BK), ALU.mult))
        f("d1", dve.tensor_tensor(dia[:, 1], idd, dP(Q_EG), ALU.mult))
        f("d2", dve.tensor_tensor(dia[:, 2], idd, dP(Q_RQ), ALU.mult))
        f("d3", dve.tensor_tensor(dia[:, 3], idd, egl[0:Dn, NT, :].unsqueeze(2).to_broadcast([Dn, BH, NS]), ALU.mult))
        f("mr", dve.tensor_tensor(dmr[:], le, dP(Q_RK), ALU.mult))
        dve.wait_ge(f_pe, PEn("bcast"))
        f("kb", dve.tensor_tensor(dkb[:], psum[0:Dn, 3, :].rearrange("p (h i) -> p h i", h=BH), dW(Q_BKE), ALU.mult))
        f("kd", dve.tensor_tensor(dkd[:], psum[0:Dn, 3, :].rearrange("p (h i) -> p h i", h=BH), dW(Q_KD), ALU.mult))
        f("vb", dve.tensor_tensor(dvb[:], psum[0:Dn, 4, :].rearrange("p (h i) -> p h i", h=BH), dW(Q_BETA), ALU.mult))
        dve.wait_ge(f_ac, ACn("rq"))
        own("mr")
        f("dcm", dve.tensor_tensor(ddc[:], ddc[:], dmr[:], ALU.mult))
        own("dcm")
        f("at0", dve.tensor_tensor(dat[:], q4(6, 1), ddc[:], ALU.mult))
        own("at0")
        f("at", dve.tensor_tensor(dat[:], dat[:], q4(5, 1), ALU.mult))
        f("kq", dve.tensor_tensor(dkq[:], q4(6, 2), ddc[:], ALU.mult))
        own("at")
        f("x_", dve.tensor_tensor(dxt[:], dat[:], bD(kc[0:Dn, K_LV:K_LV + NS]), ALU.mult))
        own("x_")
        f("xt0", dve.tensor_tensor(dxt[:], idd, dxt[:], ALU.subtract))
        f("at1", dve.tensor_tensor(dat1[:], dat[:], bD(kc[0:Dn, K_LV + P:K_LV + P + NS]), ALU.mult))
        f("eg", dve.tensor_copy(deg[:], q4(5, 2, P)))
        f("el", dve.tensor_copy(del_[:], q4(6, 0, P)))
        for b in range(DB):
            dve.wait_ge(m_kt, 4 + 2 * b + 2)
            dve.wait_ge(m_sc, b + 1)
            dve.tensor_copy(ckT[:, 2:4, :].rearrange("p h k -> p (h k)"), psum[:, 4, :]).then_inc(m_kd, 1)
        dve.wait_ge(f_pe, PEn("mem_rows"))
        f("mem_mx", dve.tensor_reduce(dsm[:, 0:1], psum[:, 6, 0:256], AX.X, ALU.max))
        own("mem_mx")
        f("mem_nm", dve.tensor_scalar(dsm[:, 1:2], dsm[:, 0:1], -P ** -0.5, None, ALU.mult))
        dve.wait_ge(f_pe, PEn("win_rows"))
        for v in range(2):
            f(f"win_m{v}", dve.tensor_tensor(sR[:, v, :], psum[:, 5, 160 * v:160 * v + 160], dmk[:], ALU.add))
        own("win_m1")
        f("win_mx", dve.tensor_reduce(dsm[:, 4:6], sR[:], AX.X, ALU.max))
        own("win_mx")
        f("win_nx", dve.scalar_tensor_tensor(out=dsm[:, 4:6], in0=dsm[:, 4:6], scalar=AHD ** -0.5, in1=sks[:], op0=ALU.mult, op1=ALU.max))
        own("win_nx")
        f("win_nm", dve.tensor_scalar(dsm[:, 6:8], dsm[:, 4:6], -1.0, None, ALU.mult))
        own("win_nm")
        f("win_sk", dve.tensor_tensor(dsm[:, 10:12], sks[:], dsm[:, 6:8], ALU.add))
        dve.wait_ge(f_ac, ACn("mem_exp"))
        f("mem_rd", dve.reciprocal(dsm[:, 3:4], dsm[:, 2:3]))
        own("mem_rd")
        f("mem_n", dve.tensor_scalar(mR[:], mR[:], dsm[:, 3:4], None, ALU.mult))
        dve.wait_ge(f_pe, PEn("xt"))
        f("xt", dve.tensor_tensor(dxt[:], dxt[:], q4(3, 2), ALU.subtract))
        dve.wait_ge(f_ac, ACn("win_sk"))
        f("win_dn", dve.tensor_tensor(dsm[:, 14:16], dsm[:, 8:10], dsm[:, 12:14], ALU.add))
        own("win_dn")
        f("win_rd", dve.reciprocal(dsm[:, 16:18], dsm[:, 14:16]))
        own("win_rd")
        f("win_n", dve.tensor_tensor(sR[:], sR[:], dsm[:, 16:18].unsqueeze(2).to_broadcast([P, 2, WIN + NS]), ALU.mult))
        dve.wait_ge(f_pe, PEn("u_w"))
        f("uT", dve.tensor_copy(duT[:], q4(4, 0, P)))
        for h in range(BH):
            dve.tensor_copy(wq[:, h, :, 1, :], by_step(dq[:, h, :]))
        for h in range(BH):
            op = dve.tensor_copy(wq[:, h, :, 0, :], by_step(psum[:, 4, P + NS * h:P + NS * h + NS]))
        f("wT", op)
        dve.wait_ge(f_pe, PEn("w_q_s"))
        for h in range(BH):
            src = psum[:, 7, 64 * h:64 * h + 64].rearrange("p (b a s) -> p b a s", b=DB, a=2)
            op = dve.tensor_tensor(by_step(dvT[:, h, :]), by_step(duT[:, h, :]), src[:, :, 0, :], ALU.subtract)
        f("vT", op)
        for h in range(BH):
            src = psum[:, 7, 64 * h:64 * h + 64].rearrange("p (b a s) -> p b a s", b=DB, a=2)
            op = dve.tensor_tensor(by_step(dqe[:, h, :]), by_step(deg[:, h, :]), src[:, :, 1, :], ALU.mult)
        f("qe", op)
        dve.wait_ge(f_ac, ACn("vn"))
        blk = kc[0:Dn, K_D_BLK:K_D_BLK + NS].rearrange("p (b s) -> p b s", s=DS)[:, :, 0]

        def keep(half):
            return dve.tensor_tensor(vnm[:], dvn[:].unsqueeze(2).to_broadcast([Dn, 4, 4, P]),
                                     blk[:, 4 * half:4 * half + 4].unsqueeze(1).unsqueeze(3).to_broadcast([Dn, 4, 4, P]), ALU.mult)

        f("vm0", keep(0))
        dve.wait_ge(f_pe, PEn("win_o"))
        for v in range(2):
            rows = slice(64 * v, 64 * v + 64)
            f(f"win_c{v}", dve.tensor_copy(dob[rows, 0], psum[rows, 3, P * v:P * v + P].rearrange("p (g t) -> p g t", g=4)))
        own("win_c1")
        for v in range(2):
            rows = slice(64 * v, 64 * v + 64)
            f(f"win_o{v}", dve.tensor_tensor(dob[rows, 0], dob[rows, 0], psum[rows, 3, 256 + P * v:256 + P * v + P].rearrange("p (g t) -> p g t", g=4), ALU.add))
        dve.wait_ge(f_pe, PEn("o"))
        f("o_", dve.tensor_tensor(dqe[:], dqe[:], q4(7, 2, P), ALU.add))
        el4 = del_[:].rearrange("p h (b s) -> p b h s", s=DS)[:, :, :, 0].unsqueeze(3)
        f("s_e", dve.tensor_tensor(sd[:], sd[:], el4.to_broadcast([P, DB, BH, P]), ALU.mult))
        dve.wait_ge(f_pe, PEn("sumsq"))
        f("n0", dve.tensor_tensor(duT[:], q4(7, 3, P), dnm[:], ALU.mult))
        own("n0")
        f("n1", dve.tensor_tensor(duT[:], duT[:], dnm[:], ALU.mult))
        own("n1")
        f("n2", dve.tensor_scalar(duT[:], duT[:], 1.0 / P, EPS, ALU.mult, ALU.add))
        f("oq", dve.tensor_tensor(dqe[:], dqe[:], dnm[:], ALU.mult))
        own("oq")
        f("oz", dve.tensor_tensor(dqe[:], dqe[:], dq[:, 12:16, :], ALU.mult))
        dve.wait_ge(f_ac, ACn("root"))
        f("n3", dve.reciprocal(dvT[:], dsq[:]))
        own("n3")
        f("o_z", dve.tensor_tensor(dob[:, 1], dqe[:], dvT[:], ALU.mult))
        for j in range(8):
            half, h = divmod(j, 4)
            dve.wait_ge(g_up, j + 1)
            own("s_e")
            dve.tensor_tensor(sd[:, 4 * half:4 * half + 4, h, :], sd[:, 4 * half:4 * half + 4, h, :],
                              psum[:, (3, 5, 4)[j % 3], :].rearrange("p (b d) -> p b d", b=4), ALU.add).then_inc(g_ad, 1)
            if j == 3:
                f("vm1", keep(1))
        dve.wait_ge(f_pe, PEn("mem_o"))
        f("mem_o", dve.tensor_copy(dob[:, 2], q4(6, 2, P)))
        dve.sem_inc(q_mx, 12)
        dve.sem_inc(t_y, 2)
        dve.sem_inc(u_xs, 2)
        dve.sem_inc(u_lo, 2)
        dve.sem_inc(f_fr, 3)
        dve.sem_inc(f_lo, 3)
        dve.sem_inc(o_ad, 3)

        def lo_br(r, k):
            a = 4 * (r % 2) + k
            dve.wait_ge(b_hi, 4 * r + k + 1)
            dve.tensor_tensor(actD[:, 1, a, :], brw[:, k], actD[:, 0, a, :].bitcast(F32), ALU.subtract).then_inc(b_lo, 1)

        for k in range(4):
            lo_br(0, k)
        for j in range(12):
            r = j // 4
            dve.wait_ge(q_sg, j + 1)
            for half in range(2):
                if (j, half) in BR_AT:
                    lo_br(*BR_AT[j, half])
                for c in range(3):
                    x = 6 * j + 3 * half + c
                    m = 2 * (j % 4) + half
                    cols = slice(CH * c, CH * c + CH)
                    dve.wait_ge(g_mm, 6 + UD + x + 1)
                    if r == 0:
                        dve.tensor_tensor(accT[:, m, cols], psum[:, c, 0:CH], gat[:, j % 2, half, cols], ALU.mult).then_inc(q_mx, 1)
                        dve.wait_ge(q_mx, 12 + x + 1)
                        dve.sem_inc(g_ev, 1)
                    else:
                        dve.wait_ge(q_mx, 12 + x - 1)
                        dve.tensor_tensor(prd[:, x % 2], psum[:, c, 0:CH], gat[:, j % 2, half, cols], ALU.mult).then_inc(g_ev, 1)
                        dve.wait_ge(g_ev, 3 + UD + x + 1)
                        dve.tensor_tensor(accT[:, m, cols], accT[:, m, cols], prd[:, x % 2], ALU.add).then_inc(q_mx, 1)
        for m in range(8):
            dve.wait_ge(b_hi, 12 + m + 1)
            dve.tensor_tensor(actD[:, 1, (m + 4) % 8, :], accT[:, m, :], actD[:, 0, (m + 4) % 8, :].bitcast(F32), ALU.subtract).then_inc(b_lo, 1)

        def mean1(t, slot, rows):
            dve.wait_ge(t_sq, t + 1)
            dve.tensor_scalar(ns[0:rows, slot, 0, 1:2], ns[0:rows, slot, 0, 0:1], 1.0 / D, EPS, ALU.mult, ALU.add).then_inc(t_ms, 1)

        def apply1(t, slot, rows, gain):
            dve.wait_ge(t_rt, t + 1)
            dve.reciprocal(ns[0:rows, slot, 0, 3:4], ns[0:rows, slot, 0, 2:3]).then_inc(t_rd, 1)
            dve.wait_ge(t_rd, t + 1)
            dve.scalar_tensor_tensor(out=yr[0:rows, slot, :], in0=rows_v(slot, rows), scalar=ns[0:rows, slot, 0, 3:4],
                                     in1=gn[0:rows, gain, :], op0=ALU.mult, op1=ALU.mult).then_inc(t_y, 1)
        def rows_v(slot, rows):
            return psum[0:rows, 2 * slot:2 * slot + 2, :].rearrange("p b n -> p (b n)")

        def mean2(t, slot, rows):
            dve.wait_ge(u_sq, t + 1)
            dve.tensor_scalar(ns[0:rows, slot, 1, 1:2], ns[0:rows, slot, 1, 0:1], 1.0 / D, EPS, ALU.mult, ALU.add).then_inc(u_ms, 1)

        def apply2(t, slot, rows):
            dve.wait_ge(u_rt, t + 1)
            dve.reciprocal(ns[0:rows, slot, 1, 3:4], ns[0:rows, slot, 1, 2:3]).then_inc(u_rd, 1)
            dve.wait_ge(u_rd, t + 1)
            dve.scalar_tensor_tensor(out=xs2[0:rows, slot, :], in0=xr[0:rows, slot, :], scalar=ns[0:rows, slot, 1, 3:4],
                                     in1=gn[0:rows, 1, :], op0=ALU.mult, op1=ALU.mult).then_inc(u_xs, 1)

        def lo_back(t, slot, rows, col):
            dve.wait_ge(u_hi, t + 1)
            src = psum[:, 4 + 2 * slot:6 + 2 * slot, :].rearrange("p b (k t) -> p (b k) t", t=P)[:, :, 0:rows]
            dve.tensor_tensor(actD[:, 1, :, bass.ds(col, rows)], src, actD[:, 0, :, bass.ds(col, rows)].bitcast(F32), ALU.subtract).then_inc(u_lo, 1)

        def norms(t, b, first=P, second=P, third=P):
            if first:
                mean1(t + 1, 1 - b, first)
                if second and not (isinstance(t, int) and t == 0):
                    dve.wait_ge(t_x1, t)
                apply1(t + 1, 1 - b, first, 0)
            if third:
                lo_back(t - 1, 1 - b, third, P * t - P)
            if second:
                mean2(t, b, second)
                apply2(t, b, second)

        dve.wait_ge(b_in, 96)
        norms(-1, 1, second=0, third=0)
        norms(0, 0, third=0)
        with dve.Fori(0, (NT - 2) // 2) as i:
            for b in (1, 2):
                norms(2 * i + b, b % 2)
        norms(NT - 1, 1, first=NS)
        norms(NT, 0, first=0, second=NS)
        norms(NT + 1, 1, first=0, second=0, third=NS)
        dve.memset(accT[:], 0.0).then_inc(o_ad, 1)

        def uf_panel(i, fs):
            for c in range(3):
                cols = slice(CH * c, CH * c + CH)
                dve.wait_ge(g_ev, 3 + UF + 3 * i + c + 1)
                dve.wait_ge(g_mm, 6 + UF + 6 * i + 3 + c + 1)
                dve.wait_ge(f_hi, 3 * i + c + 1)
                dve.wait_ge(f_lo, 3 * i + c + 1)
                dve.tensor_tensor(fr[:, cols], psum[:, c, 0:CH], sg[:, cols], ALU.mult).then_inc(f_fr, 1)
            for c in range(3):
                cols = slice(CH * c, CH * c + CH)
                dve.wait_ge(f_hi, 3 + 3 * i + c + 1)
                dve.tensor_tensor(fT[:, fs, 1, cols], fr[:, cols], fT[:, fs, 0, cols].bitcast(F32), ALU.subtract).then_inc(f_lo, 1)

        def add_out(i):
            dve.wait_ge(o_ad, 24 * i + 4)
            for m in range(KT):
                for c in range(3):
                    x = 3 * m + c
                    cols = slice(CH * c, CH * c + CH)
                    dve.wait_ge(o_mm, 48 + 24 * i + x + 1)
                    dve.tensor_tensor(accT[:, m, cols], accT[:, m, cols], psum[:, 3 + x % 4, 0:CH], ALU.add).then_inc(o_ad, 1)

        uf_panel(0, 0)
        with dve.Fori(0, (NF - 2) // 2) as i:
            for b in (1, 2):
                uf_panel(2 * i + b, b % 2)
                add_out(2 * i + b - 1)
        uf_panel(NF - 1, 1)
        add_out(NF - 2)
        add_out(NF - 1)

        def last_rows(t, tiles, landed):
            for o, slot, rows in tiles:
                mean1(t + o, slot, rows)
            for o, slot, rows in tiles:
                dve.wait_ge(t_x1, t + o - 1)
                apply1(t + o, slot, rows, 2)
            for o, slot, rows in tiles:
                add_row(dve, t + o, slot, rows, landed - 16 * slot)

        with dve.Fori(0, NT // 2) as i:
            last_rows(9 + 2 * i, [(b, b, P) for b in range(2)], 16 * i + 16 * 6)
        last_rows(9 + NT, [(0, 0, NS)], 16 * 10)

    ctx.close()


INS = ["x_prompt", "x_sample", "mem_prompt", "state_win_k", "state_win_v", "state_conv", "state_rec", "cache_mem_k",
       "cache_mem_v", "ln_mix_pre", "w_in", "attn_sink", "gdn_conv_w", "gdn_a_log", "gdn_dt_bias", "gdn_norm_w",
       "ln_mem", "w_mem_kv", "w_branch", "w_out", "ln_mix_post", "ln_ffn_pre", "w_ffn_in", "w_ffn_out", "ln_ffn_post"]
OUTS = [("y_prompt", (1, SEQ, D)), ("y_sample", (DB, DS, D)),
        ("win_k_prompt", (1, WIN, AKV, AHD)), ("win_v_prompt", (1, WIN, AKV, AHD)),
        ("conv_prompt", (1, CW - 1, 12 * P)), ("rec_prompt", (1, BH, P, P)),
        ("mem_k_prompt", (1, MEM, 4, P)), ("mem_v_prompt", (1, MEM, 4, P)),
        ("win_k_sample", (DB, WIN, AKV, AHD)), ("win_v_sample", (DB, WIN, AKV, AHD)),
        ("conv_sample", (DB, CW - 1, 12 * P)), ("rec_sample", (DB, BH, P, P))]


def kernel(**inputs):
    import concourse.bacc as bacc
    from concourse.bass_utils import run_bass_kernel_spmd

    nc = bacc.Bacc("TRN2", target_bir_lowering=False, num_devices=1)
    arrays, io = {}, {}
    tables = dict(zip(("k_const", "k_rope", "k_swa", "k_dmask"), constants()))
    for name in INS + list(tables):
        a = np.ascontiguousarray(inputs[name] if name in inputs else tables[name])
        arrays["in_" + name] = a
        io[name] = nc.dram_tensor("in_" + name, a.shape, mybir.dt.from_np(a.dtype), kind="ExternalInput").ap()
    for name, shape in OUTS:
        io[name] = nc.dram_tensor("out_" + name, shape, F32, kind="ExternalOutput").ap()
    build(nc, io)
    r = run_bass_kernel_spmd(nc, [arrays], core_ids=[0])
    return tuple(r.results[0]["out_" + name] for name, _ in OUTS)
```
